# Optimizing a Trainium2 kernel written in Bass

```python
import math
import jax, jax.numpy as jnp
from jax import lax
import numpy as np
import jax
import jax.numpy as jnp

D_MODEL = 2048
BATCH = 1
SEQ = 256
DEPTH = 1

N_MEM = 256
NORM_EPS = 1e-6

SSD_WIDTH = D_MODEL // 2
SSD_HEAD_DIM = 64
SSD_HEADS = SSD_WIDTH // SSD_HEAD_DIM
SSD_GROUPS = 2
SSD_HEADS_PER_GROUP = SSD_HEADS // SSD_GROUPS
SSD_STATE = 128
SSD_CONV = 4
SSD_CHUNK = 128
SSD_CONV_DIM = SSD_WIDTH + 2 * SSD_GROUPS * SSD_STATE
SSD_IN = SSD_WIDTH + SSD_CONV_DIM + SSD_HEADS

RWKV_WIDTH = D_MODEL - SSD_WIDTH
RWKV_HEAD_DIM = 64
RWKV_HEADS = RWKV_WIDTH // RWKV_HEAD_DIM
RWKV_DECAY_RANK = 96
RWKV_AAA_RANK = 96
RWKV_GATE_RANK = 256
RWKV_IN = 3 * RWKV_WIDTH + RWKV_DECAY_RANK + RWKV_AAA_RANK + RWKV_GATE_RANK
RWKV_LN_EPS = 64e-5

MIX_WIDTH = SSD_WIDTH + RWKV_WIDTH
D_IN = SSD_IN + RWKV_IN

XATTN_HEADS = 4
XATTN_HEAD_DIM = D_MODEL // XATTN_HEADS

D_FF = 4 * D_MODEL


def rms_norm(x, g, eps=NORM_EPS):
    xf = x.astype(jnp.float32)
    y = xf * lax.rsqrt(jnp.mean(xf * xf, axis=-1, keepdims=True) + eps)
    return (y * g).astype(x.dtype)

def causal_depthwise_conv(u, w, b):
    y = lax.conv_general_dilated(
        u, w, window_strides=(1,), padding=[(w.shape[0] - 1, 0)],
        dimension_numbers=("NWC", "WIO", "NWC"), feature_group_count=u.shape[-1])
    return y + b

def ssd_mixer(u, conv_w, conv_b, dt_bias, a_log, d_skip, norm_g):
    f32 = jnp.float32
    bsz, seq, _ = u.shape
    G, E, P, N, Q = SSD_GROUPS, SSD_HEADS_PER_GROUP, SSD_HEAD_DIM, SSD_STATE, SSD_CHUNK
    nc = seq // Q
    z, xbc, dt = jnp.split(u, [SSD_WIDTH, SSD_WIDTH + SSD_CONV_DIM], axis=-1)
    xbc = jax.nn.silu(causal_depthwise_conv(xbc, conv_w, conv_b))
    xs, bm, cm = jnp.split(xbc, [SSD_WIDTH, SSD_WIDTH + G * N], axis=-1)
    xs = xs.astype(f32).reshape(bsz, nc, Q, G, E, P)
    bm = bm.astype(f32).reshape(bsz, nc, Q, G, N)
    cm = cm.astype(f32).reshape(bsz, nc, Q, G, N)
    dt = jax.nn.softplus(dt.astype(f32) + dt_bias.astype(f32))
    a = -jnp.exp(a_log.astype(f32))
    dt_c = dt.reshape(bsz, nc, Q, G, E)
    xdt = xs * dt_c[..., None]
    da = jnp.transpose(dt_c * a.reshape(G, E), (0, 1, 3, 4, 2))
    cs = jnp.cumsum(da, axis=-1)
    causal = jnp.tril(jnp.ones((Q, Q), dtype=bool))
    seg = cs[..., :, None] - cs[..., None, :]
    lmat = jnp.where(causal, jnp.exp(jnp.where(causal, seg, 0.0)), 0.0)
    cb = jnp.einsum('bclgn,bcsgn->bcgls', cm, bm)
    y_diag = jnp.einsum('bcgls,bcgels,bcsgep->bclgep', cb, lmat, xdt)
    decay_to_end = jnp.exp(cs[..., -1:] - cs)
    chunk_states = jnp.einsum('bcsgn,bcges,bcsgep->bcgepn', bm, decay_to_end, xdt)
    chunk_decay = jnp.exp(cs[..., -1])

    def carry_state(h, inp):
        st, dec = inp
        return h * dec[..., None, None] + st, h

    h0 = jnp.zeros((bsz, G, E, P, N), f32)
    _, start_states = lax.scan(carry_state, h0,
                               (jnp.moveaxis(chunk_states, 1, 0), jnp.moveaxis(chunk_decay, 1, 0)))
    start_states = jnp.moveaxis(start_states, 0, 1)
    y_off = jnp.einsum('bclgn,bcgepn,bcgel->bclgep', cm, start_states, jnp.exp(cs))
    y = y_diag + y_off + xs * d_skip.astype(f32).reshape(G, E, 1)
    y = y.reshape(bsz, seq, SSD_WIDTH) * jax.nn.silu(z.astype(f32))
    yg = y.reshape(bsz, seq, G, SSD_WIDTH // G)
    yg = yg * lax.rsqrt(jnp.mean(yg * yg, axis=-1, keepdims=True) + NORM_EPS)
    y = yg.reshape(bsz, seq, SSD_WIDTH) * norm_g
    return y.astype(u.dtype)

def rwkv7_mixer(u, mu, w0, w2, a0, a2, g2, k_k, k_a, r_k, ln_w, ln_b):
    f32 = jnp.float32
    bsz, seq, _ = u.shape
    H, N, W = RWKV_HEADS, RWKV_HEAD_DIM, RWKV_WIDTH
    uf = u.astype(f32)
    u_prev = jnp.pad(uf, ((0, 0), (1, 0), (0, 0)))[:, :-1]
    uf = uf + (u_prev - uf) * mu
    r, k, v, pw, pa, pg = jnp.split(
        uf, [W, 2 * W, 3 * W, 3 * W + RWKV_DECAY_RANK,
             3 * W + RWKV_DECAY_RANK + RWKV_AAA_RANK], axis=-1)
    w_log = -jax.nn.softplus(-(w0 + jnp.tanh(pw) @ w2)) - 0.5
    decay = jnp.exp(-jnp.exp(w_log))
    iclr = jax.nn.sigmoid(a0 + pa @ a2)
    gate = jax.nn.sigmoid(pg) @ g2
    heads = lambda t: t.reshape(bsz, seq, H, N)
    kk = heads(k * k_k)
    kk = kk / jnp.maximum(jnp.sqrt(jnp.sum(kk * kk, axis=-1, keepdims=True)), 1e-12)
    k = k * (1.0 + (iclr - 1.0) * k_a)
    r, k, v, decay, iclr = heads(r), heads(k), heads(v), heads(decay), heads(iclr)

    def step(state, inp):
        r_t, w_t, k_t, v_t, kk_t, a_t = inp
        sa = jnp.einsum('bhij,bhj->bhi', state, -kk_t)
        state = (state * w_t[:, :, None, :]
                 + sa[..., None] * (kk_t * a_t)[:, :, None, :]
                 + v_t[..., None] * k_t[:, :, None, :])
        return state, jnp.einsum('bhij,bhj->bhi', state, r_t)

    seq_first = lambda t: jnp.moveaxis(t, 1, 0)
    s0 = jnp.zeros((bsz, H, N, N), f32)
    _, y = lax.scan(step, s0, (seq_first(r), seq_first(decay), seq_first(k),
                               seq_first(v), seq_first(kk), seq_first(iclr)))
    y = jnp.moveaxis(y, 0, 1)
    mean = jnp.mean(y, axis=-1, keepdims=True)
    var = jnp.mean(jnp.square(y - mean), axis=-1, keepdims=True)
    y = ((y - mean) * lax.rsqrt(var + RWKV_LN_EPS)).reshape(bsz, seq, W) * ln_w + ln_b
    bonus = jnp.sum(r * k * r_k, axis=-1, keepdims=True) * v
    y = (y + bonus.reshape(bsz, seq, W)) * gate
    return y.astype(u.dtype)

def memory_cross_attention(h, m, wq, wk, wv, wo):
    bsz, seq, _ = h.shape
    q = (h @ wq).reshape(bsz, seq, XATTN_HEADS, XATTN_HEAD_DIM)
    k = (m @ wk).reshape(bsz, m.shape[1], XATTN_HEADS, XATTN_HEAD_DIM)
    v = (m @ wv).reshape(bsz, m.shape[1], XATTN_HEADS, XATTN_HEAD_DIM)
    scores = jnp.einsum('bshd,bmhd->bhsm', q, k).astype(jnp.float32) * (XATTN_HEAD_DIM ** -0.5)
    p = jax.nn.softmax(scores, axis=-1).astype(v.dtype)
    o = jnp.einsum('bhsm,bmhd->bshd', p, v).reshape(bsz, seq, D_MODEL)
    return o @ wo

def first_inputs(seed: int = 0) -> dict:
    key = jax.random.key(seed)
    ks = iter(jax.random.split(key, 40))
    nrm = lambda shape, scale: jax.random.normal(next(ks), shape, jnp.float32) * scale
    uni = lambda shape, lo, hi: jax.random.uniform(next(ks), shape, jnp.float32, lo, hi)
    L = DEPTH
    dt0 = jnp.exp(uni((L, SSD_HEADS), math.log(1e-3), math.log(1e-1)))
    return {
        "x": nrm((BATCH, SEQ, D_MODEL), 1.0),
        "mem": nrm((BATCH, N_MEM, D_MODEL), 1.0),
        "norm_mix_g": 1.0 + nrm((L, D_MODEL), 0.02),
        "w_in": nrm((L, D_MODEL, D_IN), D_MODEL ** -0.5),
        "ssd_conv_w": nrm((L, SSD_CONV, 1, SSD_CONV_DIM), SSD_CONV ** -0.5),
        "ssd_conv_b": nrm((L, SSD_CONV_DIM), 0.01),
        "ssd_dt_bias": dt0 + jnp.log(-jnp.expm1(-dt0)),
        "ssd_a_log": jnp.log(uni((L, SSD_HEADS), 1.0, 16.0)),
        "ssd_d": 1.0 + nrm((L, SSD_HEADS), 0.1),
        "ssd_norm_g": 1.0 + nrm((L, SSD_WIDTH), 0.02),
        "rwkv_mu": uni((L, RWKV_IN), 0.0, 1.0),
        "rwkv_w0": uni((L, RWKV_WIDTH), -6.0, -1.0),
        "rwkv_w2": nrm((L, RWKV_DECAY_RANK, RWKV_WIDTH), 0.5 * RWKV_DECAY_RANK ** -0.5),
        "rwkv_a0": nrm((L, RWKV_WIDTH), 0.1),
        "rwkv_a2": nrm((L, RWKV_AAA_RANK, RWKV_WIDTH), RWKV_AAA_RANK ** -0.5),
        "rwkv_g2": nrm((L, RWKV_GATE_RANK, RWKV_WIDTH), RWKV_GATE_RANK ** -0.5),
        "rwkv_k_k": 0.85 + nrm((L, RWKV_WIDTH), 0.05),
        "rwkv_k_a": 1.0 + nrm((L, RWKV_WIDTH), 0.05),
        "rwkv_r_k": nrm((L, RWKV_HEADS, RWKV_HEAD_DIM), 0.1),
        "rwkv_ln_w": 1.0 + nrm((L, RWKV_WIDTH), 0.02),
        "rwkv_ln_b": nrm((L, RWKV_WIDTH), 0.01),
        "w_out": nrm((L, MIX_WIDTH, D_MODEL), MIX_WIDTH ** -0.5),
        "norm_x_g": 1.0 + nrm((L, D_MODEL), 0.02),
        "norm_mem_g": 1.0 + nrm((L, D_MODEL), 0.02),
        "xattn_wq": nrm((L, D_MODEL, D_MODEL), D_MODEL ** -0.5),
        "xattn_wk": nrm((L, D_MODEL, D_MODEL), D_MODEL ** -0.5),
        "xattn_wv": nrm((L, D_MODEL, D_MODEL), D_MODEL ** -0.5),
        "xattn_wo": nrm((L, D_MODEL, D_MODEL), D_MODEL ** -0.5),
        "norm_ffn_g": 1.0 + nrm((L, D_MODEL), 0.02),
        "ffn_w1": nrm((L, D_MODEL, D_FF), D_MODEL ** -0.5),
        "ffn_w2": nrm((L, D_FF, D_MODEL), D_FF ** -0.5),
        "final_norm_g": 1.0 + nrm((D_MODEL,), 0.02),
    }

def first_block(x, mem, norm_mix_g, w_in, ssd_conv_w, ssd_conv_b, ssd_dt_bias, ssd_a_log,
              ssd_d, ssd_norm_g, rwkv_mu, rwkv_w0, rwkv_w2, rwkv_a0, rwkv_a2, rwkv_g2,
              rwkv_k_k, rwkv_k_a, rwkv_r_k, rwkv_ln_w, rwkv_ln_b, w_out, norm_x_g,
              norm_mem_g, xattn_wq, xattn_wk, xattn_wv, xattn_wo, norm_ffn_g, ffn_w1,
              ffn_w2, final_norm_g):
    for l in range(DEPTH):
        h = rms_norm(x, norm_mix_g[l])
        u = h @ w_in[l]
        y_ssd = ssd_mixer(u[..., :SSD_IN], ssd_conv_w[l], ssd_conv_b[l], ssd_dt_bias[l],
                          ssd_a_log[l], ssd_d[l], ssd_norm_g[l])
        y_rwkv = rwkv7_mixer(u[..., SSD_IN:], rwkv_mu[l], rwkv_w0[l], rwkv_w2[l], rwkv_a0[l],
                             rwkv_a2[l], rwkv_g2[l], rwkv_k_k[l], rwkv_k_a[l], rwkv_r_k[l],
                             rwkv_ln_w[l], rwkv_ln_b[l])
        x = x + jnp.concatenate([y_ssd, y_rwkv], axis=-1) @ w_out[l]
        h = rms_norm(x, norm_x_g[l])
        m = rms_norm(mem, norm_mem_g[l])
        x = x + memory_cross_attention(h, m, xattn_wq[l], xattn_wk[l], xattn_wv[l], xattn_wo[l])
        h = rms_norm(x, norm_ffn_g[l])
        x = x + jnp.square(jax.nn.relu(h @ ffn_w1[l])) @ ffn_w2[l]
    return rms_norm(x, final_norm_g)


GRID_W = 64
CTX_LEN = 256
D_MIX = D_MODEL
HEAD_DIM = 128
NA_WIDTH = D_MIX // 2
NA_HEADS = NA_WIDTH // HEAD_DIM
NA_KH = 8
NA_KW = 16
FN_WIDTH = D_MIX // 4
FN_GROUPS = 4
FN_GROUP_DIM = FN_WIDTH // FN_GROUPS
HY_WIDTH = D_MIX - NA_WIDTH - FN_WIDTH
HY_ORDER = 2
HY_BANDS = 16
HY_EMB = 1 + 2 * HY_BANDS
HY_FILTER_HIDDEN = 64
HY_FAST_DECAY = 0.3
HY_SLOW_DECAY = 1.5
HY_TARGET = 1e-2
HY_MIN_DECAY = math.log(HY_TARGET) / HY_SLOW_DECAY
HY_MAX_DECAY = math.log(HY_TARGET) / HY_FAST_DECAY
CONV_W = 3
D_FF_2 = 11 * D_MODEL // 4
D_IN_2 = 3 * NA_WIDTH + FN_WIDTH + (HY_ORDER + 1) * HY_WIDTH
N_MOD = 6
EPS = 1e-6


def rmsnorm(x, g):
    xf = x.astype(jnp.float32)
    y = xf * lax.rsqrt(jnp.mean(xf * xf, axis=-1, keepdims=True) + EPS)
    return (y * g.astype(jnp.float32)).astype(x.dtype)

def modulate(h, shift, scale):
    return h * (1 + scale) + shift

def dwconv_centred(x, w, b):
    L = x.shape[1]
    pad = CONV_W // 2
    xp = jnp.pad(x, ((0, 0), (pad, pad), (0, 0)))
    return sum(xp[:, j:j + L] * w[j] for j in range(CONV_W)) + b

def heads(t):
    return t.reshape(*t.shape[:-1], NA_HEADS, HEAD_DIM)

def split_projection(p):
    o1, o2, o3 = NA_WIDTH, 2 * NA_WIDTH, 3 * NA_WIDTH
    o4 = o3 + FN_WIDTH
    return p[..., :o1], p[..., o1:o2], p[..., o2:o3], p[..., o3:o4], p[..., o4:]

def neighbourhood_attention(q, k, v, kc, vc, rpb):
    B, L, H, Dh = q.shape
    rows = L // GRID_W
    kh = min(NA_KH, rows)
    n_loc = kh * NA_KW
    scale = Dh ** -0.5
    col = np.arange(GRID_W)
    col_start = np.clip(col - NA_KW // 2, 0, GRID_W - NA_KW)
    col_idx = col_start[:, None] + np.arange(NA_KW)[None, :]
    dcol = col_idx - col[:, None] + (NA_KW - 1)
    rpb_cols = rpb[:, :, dcol]
    kg = k.reshape(B, rows, GRID_W, H, Dh)
    vg = v.reshape(B, rows, GRID_W, H, Dh)
    q_rows = q.reshape(B, rows, GRID_W, H, Dh).transpose(1, 0, 2, 3, 4)

    def row_block(args):
        r, q_r = args
        r0 = jnp.clip(r - kh // 2, 0, rows - kh)
        k_rows = lax.dynamic_slice_in_dim(kg, r0, kh, axis=1)
        v_rows = lax.dynamic_slice_in_dim(vg, r0, kh, axis=1)
        k_win = jnp.take(k_rows, col_idx, axis=2)
        v_win = jnp.take(v_rows, col_idx, axis=2)
        drow = r0 + jnp.arange(kh) - r + (NA_KH - 1)
        bias = jnp.take(rpb_cols, drow, axis=1).transpose(0, 2, 1, 3)
        s_loc = jnp.einsum("bqhd,biqjhd->bhqij", q_r, k_win).astype(jnp.float32) * scale
        s_loc = s_loc + bias.astype(jnp.float32)
        s_ctx = jnp.einsum("bqhd,bchd->bhqc", q_r, kc).astype(jnp.float32) * scale
        s = jnp.concatenate([s_loc.reshape(B, H, GRID_W, n_loc), s_ctx], axis=-1)
        p = jax.nn.softmax(s, axis=-1).astype(v.dtype)
        p_loc = p[..., :n_loc].reshape(B, H, GRID_W, kh, NA_KW)
        return (jnp.einsum("bhqij,biqjhd->bqhd", p_loc, v_win)
                + jnp.einsum("bhqc,bchd->bqhd", p[..., n_loc:], vc))

    out = lax.map(row_block, (jnp.arange(rows), q_rows))
    return out.transpose(1, 0, 2, 3, 4).reshape(B, L, H * Dh)

def context_attention(qc, kc, vc):
    B, Lc, H, Dh = qc.shape
    s = jnp.einsum("bqhd,bkhd->bhqk", qc, kc).astype(jnp.float32) * (Dh ** -0.5)
    p = jax.nn.softmax(s, axis=-1).astype(vc.dtype)
    return jnp.einsum("bhqk,bkhd->bqhd", p, vc).reshape(B, Lc, H * Dh)

def fourier_mix(f):
    B, L, _ = f.shape
    fg = f.astype(jnp.float32).reshape(B, L, FN_GROUPS, FN_GROUP_DIM)
    y = jnp.fft.fft2(fg, axes=(1, 3), norm="ortho").real
    return y.reshape(B, L, FN_WIDTH).astype(f.dtype)

def hyena_kernel_spectrum(L, w1, b1, w2, b2, w3, freq):
    pos = jnp.arange(L, dtype=jnp.float32)[:, None]
    t = pos / max(L - 1, 1)
    bands = jnp.linspace(1e-4, HY_BANDS - 1, HY_BANDS, dtype=jnp.float32)
    ang = bands * (2.0 * math.pi / L) * pos
    z = jnp.concatenate([t, jnp.cos(ang), -jnp.sin(ang)], axis=-1)
    hdn = jnp.sin(freq * (z @ w1 + b1))
    hdn = jnp.sin(freq * (hdn @ w2 + b2))
    h = (hdn @ w3).astype(jnp.float32).reshape(L, HY_ORDER, 2, HY_WIDTH)
    deltas = jnp.linspace(HY_MIN_DECAY, HY_MAX_DECAY, HY_WIDTH, dtype=jnp.float32)
    h = h * jnp.exp(-t * jnp.abs(deltas))[:, None, None, :]
    hf, hb = h[:, :, 0], h[:, :, 1]
    kernel = jnp.concatenate([hf, jnp.zeros_like(hf[:1]), hb[:0:-1]], axis=0)
    return jnp.fft.rfft(kernel, axis=0)

def long_conv(z, k_spec, bias):
    L = z.shape[1]
    zf = z.astype(jnp.float32)
    y = jnp.fft.irfft(jnp.fft.rfft(zf, n=2 * L, axis=1) * k_spec, n=2 * L, axis=1)[:, :L]
    return (y + zf * bias).astype(z.dtype)

def hyena_mix(u, conv_w, conv_b, k_spec, bias):
    u = dwconv_centred(u, conv_w, conv_b)
    v, x1, x2 = jnp.split(u, HY_ORDER + 1, axis=-1)
    z = x1 * long_conv(v, k_spec[:, 0], bias[0])
    return x2 * long_conv(z, k_spec[:, 1], bias[1])

def merge_groups(a, f, hy, g):
    o1, o2 = NA_WIDTH, NA_WIDTH + FN_WIDTH
    return jnp.concatenate([rmsnorm(a, g[:o1]), rmsnorm(f, g[o1:o2]), rmsnorm(hy, g[o2:])], axis=-1)

def conv_gated_mlp(h, w_up, conv_w, conv_b, w_down):
    gate, up = jnp.split(h @ w_up, 2, axis=-1)
    return (jax.nn.gelu(dwconv_centred(gate, conv_w, conv_b), approximate=True) * up) @ w_down

def second_inputs(seed: int = 0) -> dict:
    key = jax.random.key(seed)
    ks = jax.random.split(key, 26)

    def nrm(k, shape, s):
        return s * jax.random.normal(k, shape, dtype=jnp.float32)

    def gain(k, shape):
        return 1.0 + 0.02 * jax.random.normal(k, shape, dtype=jnp.float32)

    return {
        "x": nrm(ks[0], (BATCH, SEQ, D_MODEL), 1.0),
        "c": nrm(ks[1], (BATCH, D_MODEL), 1.0),
        "ctx": nrm(ks[2], (BATCH, CTX_LEN, D_MODEL), 1.0),
        "c_ctx": nrm(ks[3], (D_MODEL,), 1.0),
        "ada_w": nrm(ks[4], (DEPTH, D_MODEL, N_MOD * D_MODEL), 0.3 * D_MODEL ** -0.5),
        "ada_b": nrm(ks[5], (DEPTH, N_MOD * D_MODEL), 0.02),
        "norm1_g": gain(ks[6], (DEPTH, D_MODEL)),
        "norm2_g": gain(ks[7], (DEPTH, D_MODEL)),
        "w_in": nrm(ks[8], (DEPTH, D_MODEL, D_IN_2), D_MODEL ** -0.5),
        "na_rpb": nrm(ks[9], (DEPTH, NA_HEADS, 2 * NA_KH - 1, 2 * NA_KW - 1), 0.02),
        "hy_conv_w": nrm(ks[10], (DEPTH, CONV_W, (HY_ORDER + 1) * HY_WIDTH), CONV_W ** -0.5),
        "hy_conv_b": nrm(ks[11], (DEPTH, (HY_ORDER + 1) * HY_WIDTH), 0.02),
        "hy_w1": nrm(ks[12], (DEPTH, HY_EMB, HY_FILTER_HIDDEN), HY_EMB ** -0.5),
        "hy_b1": nrm(ks[13], (DEPTH, HY_FILTER_HIDDEN), 0.02),
        "hy_w2": nrm(ks[14], (DEPTH, HY_FILTER_HIDDEN, HY_FILTER_HIDDEN), HY_FILTER_HIDDEN ** -0.5),
        "hy_b2": nrm(ks[15], (DEPTH, HY_FILTER_HIDDEN), 0.02),
        "hy_w3": nrm(ks[16], (DEPTH, HY_FILTER_HIDDEN, HY_ORDER * 2 * HY_WIDTH), HY_FILTER_HIDDEN ** -0.5),
        "hy_freq": gain(ks[17], (DEPTH, HY_FILTER_HIDDEN)),
        "hy_bias": nrm(ks[18], (DEPTH, HY_ORDER, HY_WIDTH), 0.1),
        "mix_norm_g": gain(ks[19], (DEPTH, D_MIX)),
        "w_out": nrm(ks[20], (DEPTH, D_MIX, D_MODEL), D_MIX ** -0.5),
        "ffn_w_up": nrm(ks[21], (DEPTH, D_MODEL, 2 * D_FF_2), D_MODEL ** -0.5),
        "ffn_conv_w": nrm(ks[22], (DEPTH, CONV_W, D_FF_2), CONV_W ** -0.5),
        "ffn_conv_b": nrm(ks[23], (DEPTH, D_FF_2), 0.02),
        "ffn_w_down": nrm(ks[24], (DEPTH, D_FF_2, D_MODEL), D_FF_2 ** -0.5),
        "final_norm_g": gain(ks[25], (D_MODEL,)),
    }

def second_block(x, c, ctx, c_ctx, ada_w, ada_b, norm1_g, norm2_g, w_in, na_rpb,
              hy_conv_w, hy_conv_b, hy_w1, hy_b1, hy_w2, hy_b2, hy_w3, hy_freq, hy_bias,
              mix_norm_g, w_out, ffn_w_up, ffn_conv_w, ffn_conv_b, ffn_w_down, final_norm_g):
    L = x.shape[1]
    Lc = ctx.shape[1]
    xc = ctx
    s_lat = jax.nn.silu(c)
    s_ctx = jax.nn.silu(c_ctx)
    for l in range(DEPTH):
        update_ctx = l < DEPTH - 1
        mod = (s_lat @ ada_w[l] + ada_b[l])[:, None, :]
        sh1, sc1, g1, sh2, sc2, g2 = jnp.split(mod, N_MOD, axis=-1)
        mod_c = s_ctx @ ada_w[l] + ada_b[l]
        csh1, csc1, cg1, csh2, csc2, cg2 = jnp.split(mod_c, N_MOD, axis=-1)
        filt = (hy_w1[l], hy_b1[l], hy_w2[l], hy_b2[l], hy_w3[l], hy_freq[l])

        h = modulate(rmsnorm(x, norm1_g[l]), sh1, sc1)
        hc = modulate(rmsnorm(xc, norm1_g[l]), csh1, csc1)
        q, k, v, f, hy = split_projection(h @ w_in[l])
        if update_ctx:
            qc, kc, vc, fc, hyc = split_projection(hc @ w_in[l])
        else:
            kc, vc = jnp.split(hc @ w_in[l][:, NA_WIDTH:3 * NA_WIDTH], 2, axis=-1)
        kc_h, vc_h = heads(kc), heads(vc)
        a = neighbourhood_attention(heads(q), heads(k), heads(v), kc_h, vc_h, na_rpb[l])
        y = merge_groups(a, fourier_mix(f),
                         hyena_mix(hy, hy_conv_w[l], hy_conv_b[l], hyena_kernel_spectrum(L, *filt), hy_bias[l]),
                         mix_norm_g[l])
        x = x + g1 * (y @ w_out[l])
        if update_ctx:
            ac = context_attention(heads(qc), kc_h, vc_h)
            yc = merge_groups(ac, fourier_mix(fc),
                              hyena_mix(hyc, hy_conv_w[l], hy_conv_b[l], hyena_kernel_spectrum(Lc, *filt), hy_bias[l]),
                              mix_norm_g[l])
            xc = xc + cg1 * (yc @ w_out[l])

        ffn = (ffn_w_up[l], ffn_conv_w[l], ffn_conv_b[l], ffn_w_down[l])
        x = x + g2 * conv_gated_mlp(modulate(rmsnorm(x, norm2_g[l]), sh2, sc2), *ffn)
        if update_ctx:
            xc = xc + cg2 * conv_gated_mlp(modulate(rmsnorm(xc, norm2_g[l]), csh2, csc2), *ffn)
    return rmsnorm(x, final_norm_g)


def setup_inputs(seed=0):
    out = dict(first_inputs(seed))
    for name, value in second_inputs(seed + 1).items():
        if name != "x":
            out[name + "_2"] = value
    return out


def reference(
    x, mem, norm_mix_g, w_in, ssd_conv_w, ssd_conv_b, ssd_dt_bias, ssd_a_log, ssd_d, ssd_norm_g,
    rwkv_mu, rwkv_w0, rwkv_w2, rwkv_a0, rwkv_a2, rwkv_g2, rwkv_k_k, rwkv_k_a, rwkv_r_k,
    rwkv_ln_w, rwkv_ln_b, w_out, norm_x_g, norm_mem_g, xattn_wq, xattn_wk, xattn_wv, xattn_wo,
    norm_ffn_g, ffn_w1, ffn_w2, final_norm_g, c_2, ctx_2, c_ctx_2, ada_w_2, ada_b_2, norm1_g_2,
    norm2_g_2, w_in_2, na_rpb_2, hy_conv_w_2, hy_conv_b_2, hy_w1_2, hy_b1_2, hy_w2_2, hy_b2_2,
    hy_w3_2, hy_freq_2, hy_bias_2, mix_norm_g_2, w_out_2, ffn_w_up_2, ffn_conv_w_2,
    ffn_conv_b_2, ffn_w_down_2, final_norm_g_2,
):
    x = first_block(
        x, mem, norm_mix_g, w_in, ssd_conv_w, ssd_conv_b, ssd_dt_bias, ssd_a_log, ssd_d,
        ssd_norm_g, rwkv_mu, rwkv_w0, rwkv_w2, rwkv_a0, rwkv_a2, rwkv_g2, rwkv_k_k, rwkv_k_a,
        rwkv_r_k, rwkv_ln_w, rwkv_ln_b, w_out, norm_x_g, norm_mem_g, xattn_wq, xattn_wk,
        xattn_wv, xattn_wo, norm_ffn_g, ffn_w1, ffn_w2, final_norm_g,
    )
    return second_block(
        x, c_2, ctx_2, c_ctx_2, ada_w_2, ada_b_2, norm1_g_2, norm2_g_2, w_in_2, na_rpb_2,
        hy_conv_w_2, hy_conv_b_2, hy_w1_2, hy_b1_2, hy_w2_2, hy_b2_2, hy_w3_2, hy_freq_2,
        hy_bias_2, mix_norm_g_2, w_out_2, ffn_w_up_2, ffn_conv_w_2, ffn_conv_b_2, ffn_w_down_2,
        final_norm_g_2,
    )


_drawn_inputs = setup_inputs


def setup_inputs(seed=0):
    import zlib

    import numpy as np

    out = dict(_drawn_inputs(seed))
    spreads = {}
    factors = {'norm_mix_g': 2.709,
     'ssd_conv_b': 6.753,
     'ssd_norm_g': 4.999,
     'rwkv_w2': 7.308,
     'rwkv_a0': 4.184,
     'rwkv_k_k': 4.581,
     'rwkv_k_a': 3.123,
     'rwkv_ln_w': 8.0,
     'rwkv_ln_b': 8.0,
     'norm_x_g': 8.0,
     'norm_mem_g': 8.0,
     'norm_ffn_g': 3.398,
     'final_norm_g': 2.852,
     'norm1_g_2': 8.0,
     'norm2_g_2': 21.844,
     'na_rpb_2': 64.0,
     'hy_conv_b_2': 40.078,
     'hy_b1_2': 7.274,
     'hy_b2_2': 8.0,
     'hy_freq_2': 8.0,
     'hy_bias_2': 8.0,
     'mix_norm_g_2': 35.392,
     'ffn_conv_b_2': 24.304,
     'final_norm_g_2': 20.679}
    for name, (base, spread) in spreads.items():
        noise = np.random.default_rng([zlib.crc32(name.encode()), seed]).standard_normal(out[name].shape)
        drawn = base * np.exp(spread * noise) if base else spread * noise
        out[name] = jnp.asarray(drawn.astype(out[name].dtype))
    for name, factor in factors.items():
        out[name] = (out[name] * factor).astype(out[name].dtype)
    return out
```

```python
from contextlib import ExitStack

import concourse.bass as bass
from concourse import mybir

F32 = mybir.dt.float32
F32R = mybir.dt.float32r
ACT = mybir.ActivationFunctionType
ALU = mybir.AluOpType
AX_X = mybir.AxisListType.X
ADD, SUB, MUL, MAX, MIN = ALU.add, ALU.subtract, ALU.mult, ALU.max, ALU.min
P = 128
T = 256
NR = 6
NH = 4
CS = 1024
CN = 512

COLS = [("norm_mix_g", 16), ("conv_w", 48), ("conv_b", 12), ("ssd_g", 8), ("ssd_d", 8), ("dt_bias", 1),
        ("a_log", 1), ("mu", 28), ("w0", 8), ("a0", 8), ("k_k", 8), ("k_a", 8), ("r_k", 8), ("ln_w", 8),
        ("ln_b", 8), ("norm_x_g", 16), ("norm_mem_g", 16), ("norm_ffn_g", 16), ("final_g", 16), ("c", 16),
        ("c_ctx", 16), ("ada_b", 96), ("norm1_g", 16), ("norm2_g", 16), ("hy_cw", 36), ("hy_cb", 12),
        ("mix_g", 16), ("ff_cw", 132), ("ff_cb", 44), ("hy_bias", 8), ("final_g2", 16), ("hy_b1", 1),
        ("hy_b2", 1), ("hy_freq", 1), ("one", 1), ("eps6", 1), ("eps64", 1), ("zero", 1)]
MATS = ["ident", "ones", "bones"]
MATS1 = ["cm", "l1", "t1", "t2", "t4", "t8", "t16", "t32", "strict", "incl"]
RMS = ["rm128", "rm64"]


def offsets(items):
    out, at = {}, 0
    for name, n in items:
        out[name] = at
        at += n
    return out, at


class Queue:

    def __init__(self, sem, chain):
        self.sem, self.chain, self.ops, self.n, self.seen, self.held = sem, chain, [], 0, {}, []

    def add(self, fn, w=(), inc=True):
        need = {}
        toks = list(w) + self.held + ([(self.sem, self.n)] if self.chain and self.n else [])
        self.held = []
        while toks:
            t = toks.pop()
            if isinstance(t, list):
                toks += t
            elif isinstance(t, dict):
                toks += t["g"]
            elif t is not None and t[1] > max(need.get(t[0], 0), self.seen.get(t[0], 0)):
                need[t[0]] = t[1]
        self.seen.update(need)
        self.ops.append((list(need.items()), fn, inc))
        self.n += 1 if inc else 0
        return (self.sem, self.n) if inc else None

    def now(self):
        assert self.chain or not self.ops or self.ops[-1][2]
        return (self.sem, self.n)

    def play(self, eng, sems):
        for need, fn, inc in self.ops:
            for s, v in need:
                eng.wait_ge(sems[s], v)
            ins = fn(eng)
            if inc:
                ins.then_inc(sems[self.sem], 1)


def build(nc, A_, out, stop=99):
    sems = {}
    top = ExitStack()
    with top:
        def sem(name):
            sems[name] = top.enter_context(nc.semaphore(name))
            return name

        class Scope:
            def __init__(self, side="left"):
                self.st, self.side = ExitStack(), side

            def __call__(self, name, shape, dt=F32):
                return self.st.enter_context(nc.sbuf_tensor(name, shape, dt, side=self.side))

            def close(self):
                self.st.close()
                fence()

        V, A, G, TE, SP = (Queue(sem("s_dve"), True), Queue(sem("s_act"), True), Queue(sem("s_pool"), True),
                           Queue(sem("s_pe"), False), Queue(sem("s_sp"), False))
        counts = {}

        def fence():
            toks = [q.now() for q in (V, A, G, TE)]
            for q in (V, A, G, TE):
                q.held += toks
            return toks

        def tt(q, o, a, b, op, w=()):
            return q.add(lambda e: e.tensor_tensor(o, a, b, op), w)

        def stt(o, a, s, b, op0, op1, w=()):
            return V.add(lambda e: e.scalar_tensor_tensor(o, a, s, b, op0, op1), w)

        def ts(q, o, a, s1, s2, op0, op1=None, w=()):
            if op1 is None:
                return q.add(lambda e: e.tensor_scalar(o, a, s1, None, op0), w)
            return q.add(lambda e: e.tensor_scalar(o, a, s1, s2, op0, op1), w)

        def cp(q, o, a, w=()):
            return q.add(lambda e: e.tensor_copy(o, a), w)

        def act(o, a, f, w=(), bias=None, scale=1.0, acc=None):
            if bias is None:
                if acc is None:
                    return A.add(lambda e: e.activation(o, a, f, scale=scale), w)
                return A.add(lambda e: e.activation(o, a, f, scale=scale, accum_out=acc), w)
            if acc is None:
                return A.add(lambda e: e.activation(o, a, f, bias=bias, scale=scale), w)
            return A.add(lambda e: e.activation(o, a, f, bias=bias, scale=scale, accum_out=acc), w)

        def recip(o, a, w=()):
            return V.add(lambda e: e.reciprocal(o, a), w)

        def scan(o, d0, d1, w=()):
            return V.add(lambda e: e.tensor_tensor_scan(o, d0, d1, 0.0, MUL, ADD), w)

        def fill(q, o, v, w=()):
            return q.add(lambda e: e.memset(o, v), w)

        def mm(o, l, r, start=True, stop=True, w=(), inc=False):
            return TE.add(lambda e: e.matmul(o, l, r, start=start, stop=stop), w, inc)

        def tr(o, i, ident, w=(), inc=False):
            return TE.add(lambda e: e.transpose(o, i, ident), w, inc)

        def dma(q, name, o, i, w=()):
            if name not in sems:
                sem(name)
            counts[name] = counts.get(name, 0) + 16
            v = counts[name]
            q.add(lambda e: e.dma_start(o, i).then_inc(sems[name], 16), w, inc=False)
            return (name, v)

        def dma_g(name, o, i, w=()):
            if name not in sems:
                sem(name)
            counts[name] = counts.get(name, 0) + 16
            v = counts[name]
            G.add(lambda e: e.dma_start(o, i).then_inc(sems[name], 16), w, inc=False)
            return (name, v)

        def dump(name, ap):
            o = nc.dram_tensor("dbg_" + name, tuple(ap.shape), F32, kind="ExternalOutput").ap()
            dma(SP, "d_dbg", o, ap, fence())

        def end():
            SP.add(lambda e: e.nop(), [(n, v) for n, v in counts.items() if n in ("d_out", "d_dbg")], inc=False)
            with nc.Block() as block:
                @block.sync
                def _(e):
                    SP.play(e, sems)

                @block.tensor
                def _(e):
                    TE.play(e, sems)

                @block.vector
                def _(e):
                    V.play(e, sems)

                @block.scalar
                def _(e):
                    A.play(e, sems)

                @block.gpsimd
                def _(e):
                    G.play(e, sems)

        base = Scope()
        PSUM = top.enter_context(nc.psum_tensor("psum", [P, 8, 512], F32))
        WRAW = [base(f"wraw{i}", [P, CS]) for i in range(NR)]
        WHI = [base(f"whi{i}", [P, CS], F32R) for i in range(NH)]
        WLO = [base(f"wlo{i}", [P, CS], F32R) for i in range(NH)]
        off, npk = offsets(COLS)
        PK = base("pk", [P, npk])
        MT = base("mats", [P, len(MATS) * P])
        MOD = base("mod", [P, 96, 2])
        GS = base("gs", [P, 3, 16])
        ident, ones, bones = (MT[:, i * P:(i + 1) * P] for i in range(3))

        def col(name, j=0, rows=P):
            return PK[0:rows, off[name] + j:off[name] + j + 1]

        bank_free = [[] for _ in range(8)]
        turn = [0]

        def bank(i):
            return PSUM[:, i, :]

        def take(n):
            if n > 4:
                b = list(range(8))
            else:
                b = [turn[0] * 4 + i for i in range(n)]
                turn[0] ^= 1
            return b

        tk_pk = [dma(SP, "d_pk", PK[:, :], A_["pack"]), dma(SP, "d_mt", MT[:, :], A_["mats"])]

        chunks = []

        def plan(w, k0, kt, blocks):
            out = []
            for c0, n in blocks:
                ids = []
                ck = min(CS // n, 4)
                for k in range(0, kt, ck):
                    m = min(ck, kt - k)
                    ids.append((len(chunks), k, m))
                    chunks.append((A_[w][(k0 + k) * P:(k0 + k + m) * P, c0:c0 + n].rearrange("(k p) n -> p k n", p=P),
                                   m, n))
                out.append((c0, n, ids))
            return out

        def cols(a, b, step=CN):
            return [(c, min(step, b - c)) for c in range(a, b, step)]

        PL = {}
        PL["in_ssd"] = plan("w_in", 0, 16, cols(0, 2560) + [(2560, 128)])
        PL["in_rwkv"] = plan("w_in", 0, 16, cols(2576, 5648) + [(5648, 448)])
        PL["ada"] = plan("ada_w_2", 0, 16, cols(0, 12288))
        PL["out"] = plan("w_out", 0, 16, cols(0, 2048))
        PL["xk"] = plan("xattn_wk", 0, 16, cols(0, 2048))
        PL["xv"] = plan("xattn_wv", 0, 16, cols(0, 2048))
        PL["xq"] = plan("xattn_wq", 0, 16, cols(0, 2048))
        PL["xo"] = plan("xattn_wo", 0, 16, cols(0, 2048))
        for i in range(4):
            PL[f"up{i}"] = plan("ffn_w1", 0, 16, cols(2048 * i, 2048 * i + 2048))
            PL[f"dn{i}"] = plan("ffn_w2", 16 * i, 16, cols(0, 2048))
        PL["k2"] = plan("w_in_2", 0, 16, cols(1024, 2048, 256))
        PL["v2"] = plan("w_in_2", 0, 16, cols(2048, 3072))
        PL["q2"] = plan("w_in_2", 0, 16, cols(0, 1024))
        PL["fh"] = plan("w_in_2", 0, 16, cols(3072, 5120))
        PL["out2"] = plan("w_out_2", 0, 16, cols(0, 2048))
        for i in range(4):
            PL[f"ga{i}"] = plan("ffn_w_up_2", 0, 16, cols(1408 * i, 1408 * i + 1408))
            PL[f"uu{i}"] = plan("ffn_w_up_2", 0, 16, cols(5632 + 1408 * i, 5632 + 1408 * i + 1408))
            PL[f"dd{i}"] = plan("ffn_w_down_2", 11 * i, 11, cols(0, 2048))

        loaded, hi_tok, lo_tok, used = {}, {}, {}, {}

        def view(t, i):
            _, m, n = chunks[i]
            return t[:, 0:m * n].rearrange("p (m n) -> p m n", n=n)

        def load(i):
            if i < len(chunks):
                loaded[i] = dma(SP, f"d_w{i % NR}", view(WRAW[i % NR], i), chunks[i][0], [hi_tok.get(i - NR), lo_tok.get(i - NR)])

        def split(i):
            for k in range(len(hi_tok), min(i + 4, len(chunks))):
                hi_tok[k] = act(view(WHI[k % NH], k), view(WRAW[k % NR], k), ACT.Copy, [loaded[k], used.get(k - NH)])
            for k in range(len(lo_tok), min(i + 3, len(chunks))):
                lo_tok[k] = tt(V, view(WLO[k % NH], k), view(WRAW[k % NR], k), view(WHI[k % NH], k).bitcast(F32), SUB,
                               [hi_tok[k], used.get(k - NH)])
                load(k + NR)

        for i in range(NR):
            load(i)

        side = []

        def step():
            while side:
                if next(side[0], "end") != "end":
                    return
                side.pop(0)

        def both(*gens):
            live = list(gens)
            while live:
                for g in list(live):
                    if next(g, "end") == "end":
                        live.remove(g)
                yield

        def at(ready, k):
            return ready["g"][k // 4] if isinstance(ready, dict) else ready

        def drain():
            while side:
                step()

        def run(gen):
            for _ in gen:
                pass

        def gemm(blocks, rhs, evac, ready, tiles=None, kmap=None):
            t = 0
            for c0, n, ids in blocks:
                starts = tiles(c0, n) if tiles else [(128 * j) for j in range(n // 128)]
                bs = take(len(starts) * len(rhs))
                ends = {}
                for i, k0, m in ids:
                    split(i)
                    hi, lo = view(WHI[i % NH], i), view(WLO[i % NH], i)
                    w = [hi_tok[i], lo_tok[i], at(ready, k0 + m - 1)]
                    for j, s in enumerate(starts):
                        for r, (HH, HL) in enumerate(rhs):
                            b = bs[j * len(rhs) + r]
                            for kk in range(m):
                                k = k0 + kk
                                last = k == blocks_k(ids) - 1
                                o = PSUM[:, b, 0:T]
                                if k == 0:
                                    w = w + [bank_free[b]]
                                mm(o, hi[:, kk, s:s + 128], HH[:, k, :], k == 0, False, w)
                                mm(o, hi[:, kk, s:s + 128], HL[:, k, :], False, False)
                                fin = last or (kk == m - 1 and j == len(starts) - 1 and r == len(rhs) - 1)
                                tok = mm(o, lo[:, kk, s:s + 128], HH[:, k, :], False, last, inc=fin)
                                w = []
                                if last:
                                    ends[(j, r)] = tok
                    used[i] = tok
                    step()
                for j in range(len(starts)):
                    for r in range(len(rhs)):
                        b = bs[j * len(rhs) + r]
                        bank_free[b] = [evac(t, r, PSUM[:, b, 0:T], ends[(j, r)])]
                    t += 1

        def blocks_k(ids):
            return ids[-1][1] + ids[-1][2]

        def gemm_tok(blocks, lhs, evac, ready):
            for bi, (c0, n, ids) in enumerate(blocks):
                bs = take(len(lhs))
                ends = {}
                for i, k0, m in ids:
                    split(i)
                    hi, lo = view(WHI[i % NH], i), view(WLO[i % NH], i)
                    w = [hi_tok[i], lo_tok[i], at(ready, k0 + m - 1)]
                    for r, (HH, HL, sl) in enumerate(lhs):
                        for kk in range(m):
                            k = k0 + kk
                            last = k == blocks_k(ids) - 1
                            o = PSUM[0:sl.stop - sl.start, bs[r], 0:n]
                            if k == 0:
                                w = w + [bank_free[bs[r]]]
                            mm(o, HH[:, k, sl], hi[:, kk, 0:n], k == 0, False, w)
                            if HL is not None:
                                mm(o, HL[:, k, sl], hi[:, kk, 0:n], False, False)
                            fin = last or (kk == m - 1 and r == len(lhs) - 1)
                            tok = mm(o, HH[:, k, sl], lo[:, kk, 0:n], False, last, inc=fin)
                            w = []
                            if last:
                                ends[r] = tok
                    used[i] = tok
                    step()
                for r in range(len(lhs)):
                    sl = lhs[r][2]
                    bank_free[bs[r]] = [evac(bi, r, PSUM[0:sl.stop - sl.start, bs[r], 0:n], ends[r])]

        def bc(ap, axis, shape):
            return ap.unsqueeze(axis).to_broadcast(shape)

        def mean_square(src, acc, w, n=16):
            a = act(acc[:, 0:4, :], src[:, 0:4, :], ACT.Square, w)
            for g in range(1, n // 4):
                s = act(acc[:, 4:8, :], src[:, 4 * g:4 * g + 4, :], ACT.Square, [a])
                a = tt(G, acc[:, 0:4, :], acc[:, 0:4, :], acc[:, 4:8, :], ADD, [s])
            return a

        def rstd_of(parts, n, eps, dst, w, b=None, mat=None):
            b = 4 * turn[0] if b is None else b
            for i, p in enumerate(parts):
                t = mm(PSUM[:, b, 0:T], ones if mat is None else mat, p, i == 0, i == len(parts) - 1,
                       [w, bank_free[b]], inc=i == len(parts) - 1)
            s = act(dst, PSUM[:, b, 0:T], ACT.Sqrt, [t], bias=col(eps), scale=1.0 / n)
            bank_free[b] = [s]
            return recip(dst, dst, [s])

        def normed(src, rstd, gain, shift, tmp, HH, HL, w, res):
            res["g"] = []
            for g in range(4):
                t = tmp[:, (g % 2) * 4:(g % 2) * 4 + 4, :]
                m = tt(V, t, src[:, 4 * g:4 * g + 4, :], bc(rstd, 1, [P, 4, T]), MUL, [w])
                for j in range(4):
                    a = act(t[:, j, :], t[:, j, :], ACT.Identity, [m], bias=shift(4 * g + j), scale=gain(4 * g + j))
                h = act(HH[:, 4 * g:4 * g + 4, :], t, ACT.Copy, [a, w])
                done = tt(V, HL[:, 4 * g:4 * g + 4, :], t, HH[:, 4 * g:4 * g + 4, :].bitcast(F32), SUB, [h])
                res["g"].append([h, done])
                yield

        def zcol(j):
            return col("zero")

        def residual(XT, acc, sq, scale=None):
            last = {}

            def ev(t, r, ps, tok):
                if scale is None:
                    v = tt(V, XT[:, t, :], ps, XT[:, t, :], ADD, [tok])
                else:
                    v = stt(XT[:, t, :], ps, scale(t), XT[:, t, :], MUL, ADD, [tok])
                if acc is not None:
                    if t == 0:
                        last["g"] = act(acc, XT[:, 0, :], ACT.Square, [v, last.get("g")])
                    else:
                        s = act(sq[:, t % 2, :], XT[:, t, :], ACT.Square, [v, last.get(t - 2)])
                        last["g"] = last[t] = tt(G, acc, acc, sq[:, t % 2, :], ADD, [s, last["g"]])
                last["v"] = v
                return v
            return ev, last

        s1 = Scope()
        M1 = s1("m1", [P, len(MATS1) * P + 2 * T])
        m1 = {n: M1[:, i * P:(i + 1) * P] for i, n in enumerate(MATS1)}
        rm128 = M1[:, len(MATS1) * P:len(MATS1) * P + T]
        rm64 = M1[:, len(MATS1) * P + T:len(MATS1) * P + 2 * T]
        YS = s1("ys", [P, 8, T])
        LD = s1("ld", [P, 8, T])
        s1a = Scope()
        RK = s1a("rk", [P, 28, T + 1])
        DT = s1a("dt", [P, 4, T])
        s1b = Scope()
        ZZ = s1b("zz", [P, 8, T])
        XB = s1b("xb", [P, 12, T + 3])
        s1c = Scope()
        HH = s1c("h1hi", [P, 16, T], F32R)
        HL = s1c("h1lo", [P, 16, T], F32R)
        X0 = s1c("x0", [P, 16, T])
        TM = s1c("tm1", [P, 8, T])
        RS = s1c("rs1", [P, T])
        tk_x0 = dma_g("d_x0", X0[:, :, :], A_["x"])
        tk_m1 = dma_g("d_m1", M1[:, :], A_["mats1"])
        fill(G, XB[:, :, 0:3], 0.0)
        zpad = fill(G, RK[:, :, 0:1], 0.0)
        sq = mean_square(X0, TM, [tk_x0, tk_pk])
        r = rstd_of([TM[:, i, :] for i in range(4)], 2048, "eps6", RS[:, :], [sq, tk_pk])
        ready = {}
        run(normed(X0, RS[:, :], lambda j: col("norm_mix_g", j), zcol, TM, HH, HL, [r], ready))

        def ev_ssd(t, r_, ps, tok):
            if t < 8:
                return act(ZZ[:, t, :], ps, ACT.Silu, [tok])
            if t < 20:
                return act(XB[:, t - 8, 3:T + 3], ps, ACT.Copy, [tok])
            return act(DT[:, 0, :], ps, ACT.Copy, [tok])

        gemm(PL["in_ssd"], [(HH, HL)], ev_ssd, ready)
        tk_ssd = A.now()

        def ev_rwkv(t, r_, ps, tok):
            return act(RK[:, t, 1:T + 1], ps, ACT.Copy, [tok])

        gemm(PL["in_rwkv"], [(HH, HL)], ev_rwkv, ready,
             tiles=lambda c0, n: [0, 96, 192, 320] if n == 448 else [0, 128, 256, 384])
        s1c.close()

        s1c = Scope()
        S4 = s1c("s4", [P, 16, 4], F32R)
        SI = s1c("si", [P, 2, 16])
        MO = s1c("mo", [4, 2, CN])
        CB = s1c("comb", [4, 2])
        tk_cb = dma_g("d_cb", CB[:, :], A_["comb"], fence())
        a = act(SI[:, 0, :], PK[:, off["c"]:off["c"] + 16], ACT.Silu, [tk_pk])
        a = act(SI[:, 1, :], PK[:, off["c_ctx"]:off["c_ctx"] + 16], ACT.Silu)
        s4 = S4[:, :, :].rearrange("p k m -> p m k")
        a = act(s4[:, 0:2, :], SI[:, :, :], ACT.Copy)
        a = tt(V, s4[:, 2:4, :], SI[:, :, :], s4[:, 0:2, :].bitcast(F32), SUB, [a])
        ada_mm = {}

        def ev_ada(bi, r_, ps, tok):
            v = act(MO[:, bi % 2, :], ps, ACT.Copy, [tok, ada_mm.get(bi - 2)])
            b = 7
            for j in range(4):
                n = bi * 4 + j
                t = mm(PSUM[:, b, 2 * n:2 * n + 2], MO[0:4, bi % 2, 128 * j:128 * j + 128], CB[:, :],
                       w=[v, tk_cb, bank_free[b]], inc=j == 3)
            ada_mm[bi] = t
            return v

        gemm_tok(PL["ada"], [(S4, None, slice(0, 4))], ev_ada, a)
        v = tt(V, MOD[:, :, :], PSUM[:, 7, 0:192].rearrange("p (n c) -> p n c", c=2),
               bc(PK[:, off["ada_b"]:off["ada_b"] + 96], 2, [P, 96, 2]), ADD, [ada_mm[23]])
        bank_free[7] = [v]
        s1c.close()
        s1c = Scope()
        AC = s1c("cacc", [P, 2, T])
        SEL = s1c("sel", [16, 16 * P])
        DTT = s1c("dtt", [P, 2, 16])
        CST = s1c("cst", [P, 2, 16])
        DE = s1c("de", [P, 2, 16])
        CBM = s1c("cbm", [P, 4, P])
        E = s1c("e", [P, 16, P])
        XD = s1c("xd", [P, 2, 1024])
        XE = s1c("xe", [P, 1024])
        BM = s1c("bm", [P, 2, P])
        ST = s1c("st", [P, 2, 512])
        YK = s1c("yk", [P, 2, 1024])
        RG = s1c("rg", [P, 2, T])
        tk_sel = dma_g("d_sel", SEL[:, :], A_["sel"])
        x_, w_, conv = XB, off["conv_w"], {}
        for j in [8, 9, 10, 11] + list(range(8)):
            b = AC[:, j % 2, :]
            ts(V, b, x_[:, j, 3:T + 3], col("conv_w", 36 + j), None, MUL, w=[conv.get(j % 2)])
            for i in (2, 1, 0):
                v = stt(b, x_[:, j, i:i + T], col("conv_w", 12 * i + j), b, MUL, ADD)
            conv[j % 2] = xs_ok = act(x_[:, j, 3:T + 3], b, ACT.Silu, [v], bias=col("conv_b", j))
            if j == 11:
                bc_ok = xs_ok
        d = [DT[0:16, i, :] for i in range(4)]
        ts(V, d[0], d[0], col("dt_bias", rows=16), None, ADD)
        v = stt(d[1], d[0], -1.0, d[0], MUL, MAX)
        act(d[1], d[1], ACT.Exp, [v], scale=-1.0)
        act(d[2][:, 0:1], col("a_log", rows=16), ACT.Exp)
        a = act(d[1], d[1], ACT.Ln, bias=col("one", rows=16))
        v = stt(d[0], d[0], 0.0, d[1], MAX, ADD, [a])
        v = ts(V, d[3], d[0], d[2][:, 0:1], -1.0, MUL, MUL)
        CSR = d[1]
        v = scan(CSR, rm128[0:16, :], d[3], [tk_m1])
        for c in range(2):
            tr(PSUM[:, 0, 32 * c:32 * c + 16], d[0][:, 128 * c:128 * c + 128], ident[0:16, 0:16], [v, bank_free[0]])
            t = tr(PSUM[:, 0, 32 * c + 16:32 * c + 32], CSR[:, 128 * c:128 * c + 128], ident[0:16, 0:16], inc=True)
        v2 = PSUM[:, 0, 0:64].rearrange("p (c a h) -> p c a h", c=2, a=2)
        cp(V, DTT[:, :, :], v2[:, :, 0, :], [t])
        cst_ok = cp(V, CST[:, :, :], v2[:, :, 1, :])
        bank_free[0] = [cst_ok]
        for c in range(2):
            for g in range(2):
                sl = slice(3 + 128 * c, 131 + 128 * c)
                t = mm(PSUM[:, 1, (2 * c + g) * 128:(2 * c + g) * 128 + 128], XB[:, 8 + g, sl], XB[:, 10 + g, sl],
                       w=[bc_ok, bank_free[1]], inc=True)
        cb_ok = tt(V, CBM[:, :, :], PSUM[:, 1, :].rearrange("p (a l) -> p a l", l=P), bc(m1["cm"], 1, [P, 4, P]), MUL, [t, tk_m1])
        bank_free[1] = [cb_ok]
        for g in range(2):
            t = tr(PSUM[:, 2, g * 128:g * 128 + 128], XB[:, 8 + g, 3:131], ident, [bc_ok, bank_free[2]], inc=True)
        bm_ok = act(BM[:, :, :], PSUM[:, 2, 0:256].rearrange("p (g n) -> p g n", g=2), ACT.Copy, [t])
        bank_free[2] = [bm_ok]
        xd_ok = []
        for c in range(2):
            bs = [4 + 2 * c, 5 + 2 * c]
            for j in range(8):
                t = tr(PSUM[:, bs[j // 4], (j % 4) * 128:(j % 4) * 128 + 128], XB[:, j, 3 + 128 * c:131 + 128 * c], ident,
                       [xs_ok, bank_free[bs[j // 4]]], inc=True)
            v = tt(V, XD[:, c, :].rearrange("p (h d) -> p h d", d=64),
                   PSUM[:, bs[0]:bs[0] + 2, :].rearrange("p b (h d) -> p (b h) d", d=64),
                   bc(DTT[:, c, :], 2, [P, 16, 64]), MUL, [t])
            bank_free[bs[0]] = bank_free[bs[1]] = [v]
            xd_ok.append(v)
        y_ok = []
        e_free = None
        for c in range(2):
            for h in range(16):
                b = h // 4
                t = mm(PSUM[:, b, (h % 4) * 128:(h % 4) * 128 + 128], SEL[:, h * P:(h + 1) * P], CSR[:, 128 * c:128 * c + 128],
                       w=[tk_sel, bank_free[b]], inc=h == 15)
            csb = PSUM[:, 0:4, :].rearrange("p b (h l) -> p (b h) l", l=P)
            if c == 0:
                tt(V, DE[:, 0, :], csb[:, :, 127], CST[:, 0, :], SUB, [t])
                de_ok = act(DE[:, 0, :], DE[:, 0, :], ACT.Exp, [V.now()])
                de_ok = act(DE[:, 1, :], CST[:, 1, :], ACT.Exp, [cst_ok])
            v = tt(V, E[:, :, :], csb, bc(CST[:, c, :], 2, [P, 16, P]), SUB, [t, e_free])
            for b in range(4):
                bank_free[b] = [v]
            v = ts(V, E[:, :, :], E[:, :, :], 0.0, None, MIN)
            a = act(E[:, :, :], E[:, :, :], ACT.Exp, [v])
            for g in range(2):
                v = tt(V, E[:, 8 * g:8 * g + 8, :], E[:, 8 * g:8 * g + 8, :],
                       bc(CBM[:, 2 * c + g, :], 1, [P, 8, P]), MUL, [a, cb_ok])
            if c == 0:
                x_ = tt(V, XE[:, :].rearrange("p (h d) -> p h d", d=64), XD[:, 0, :].rearrange("p (h d) -> p h d", d=64),
                        bc(DE[:, 0, :], 2, [P, 16, 64]), MUL, [de_ok])
                for g in range(2):
                    t = mm(PSUM[:, 4 + g, :], BM[:, g, :], XE[:, g * 512:g * 512 + 512], w=[x_, bm_ok, bank_free[4 + g]], inc=True)
                    st_ok = act(ST[:, g, :], PSUM[:, 4 + g, :], ACT.Copy, [t])
                    bank_free[4 + g] = [st_ok]
            for h in range(16):
                b = 6 + h // 8
                t = mm(PSUM[:, b, (h % 8) * 64:(h % 8) * 64 + 64], E[:, h, :], XD[:, c, h * 64:h * 64 + 64],
                       w=[v, xd_ok[c], bank_free[b]], inc=h == 15)
            e_free = t
            yd = PSUM[:, 6:8, :].rearrange("p b n -> p (b n)")
            if c == 0:
                y = act(YK[:, 0, :], yd, ACT.Copy, [t])
            else:
                for g in range(2):
                    t2 = mm(PSUM[:, 4 + g, :], XB[:, 10 + g, 131:259], ST[:, g, :], w=[st_ok, bank_free[4 + g]], inc=True)
                v = tt(V, YK[:, 1, :].rearrange("p (h d) -> p h d", d=64),
                       PSUM[:, 4:6, :].rearrange("p b (h d) -> p (b h) d", d=64), bc(DE[:, 1, :], 2, [P, 16, 64]), MUL, [t2, de_ok])
                bank_free[4] = bank_free[5] = [v]
                y = tt(V, YK[:, 1, :], YK[:, 1, :], yd, ADD, [t])
            bank_free[6] = bank_free[7] = [y]
            y_ok.append(y)
        for b in range(4):
            for j in (2 * b, 2 * b + 1):
                for c in range(2):
                    t = tr(PSUM[:, b, (j % 2) * T + 128 * c:(j % 2) * T + 128 * c + 128], YK[:, c, 128 * j:128 * j + 128],
                           ident, [y_ok, bank_free[b]], inc=True)
            for j in (2 * b, 2 * b + 1):
                v = stt(YS[:, j, :], XB[:, j, 3:T + 3], col("ssd_d", j), PSUM[:, b, (j % 2) * T:(j % 2) * T + T], MUL, ADD, [t])
            bank_free[b] = [v]
        v = tt(V, YS[:, :, :], YS[:, :, :], ZZ[:, :, :], MUL)
        for g in range(2):
            a = act(ZZ[:, 4 * g:4 * g + 4, :], YS[:, 4 * g:4 * g + 4, :], ACT.Square, [v])
            r = rstd_of([ZZ[:, 4 * g + i, :] for i in range(4)], 512, "eps6", RG[:, g, :], [a])
            for j in range(4 * g, 4 * g + 4):
                stt(YS[:, j, :], YS[:, j, :], col("ssd_g", j), RG[:, g, :], MUL, MUL)
        s1c.close()
        s1b.close()
        if stop == 1:
            dump("ys", YS[:, :, :])
            dump("rk", RK[:, :, :])
            dump("mod", MOD[:, :, :])
            return end()
        s2 = Scope()
        C = s2("rc", [P, 8, T])
        IC = s2("ric", [P, 8, T])
        KK = s2("rkk", [P, 8, T])
        RT = s2("rrt", [P, 8, T])
        VT, BT, KT = (s2(n, [P, 1024]) for n in ("rvt", "rbt", "rkt"))
        LA, MB, MK, XT_ = (s2(n, [P, 16, P]) for n in ("rla", "rmb", "rmk", "rxt"))
        US, SS = (s2(n, [P, 1024]) for n in ("rus", "rss"))
        S = s2("rs", [P, 8, P])
        TW = s2("rtw", [96, T])
        PCE = s2("rpce", [P, 8, 4])
        OK = s2("romka", [P, 8])

        def U(j):
            return RK[:, j, 1:T + 1]

        def UU(a, b):
            return RK[:, a:b, 1:T + 1]

        def pair_banks(b, n=4):
            return PSUM[:, b:b + n, :].rearrange("p b (j t) -> p (b j) t", t=T)

        tk_w2 = dma_g("d_rw2", BT[0:96, :], A_["rw2"])
        tk_a2 = dma_g("d_ra2", KT[0:96, :], A_["ra2"])
        s0 = fill(G, S[:, :, :], 0.0)
        for g in [6, 2, 3, 0, 1, 4, 5]:
            d = (US if g % 2 else SS)[:, :].rearrange("p (a t) -> p a t", t=T)
            tt(V, d, RK[:, 4 * g:4 * g + 4, 0:T], UU(4 * g, 4 * g + 4), SUB, [zpad])
            for j in range(4):
                v = stt(U(4 * g + j), d[:, j, :], col("mu", 4 * g + j), U(4 * g + j), MUL, ADD)
            if g == 6:
                pw_ok = v
            if g == 3:
                k_ok = v
        sh_ok = v
        a = act(TW[:, :], RK[0:96, 24, 1:T + 1], ACT.Tanh, [pw_ok])
        for j in range(8):
            t = mm(PSUM[:, j // 2, (j % 2) * T:(j % 2) * T + T], BT[0:96, 128 * j:128 * j + 128], TW[:, :],
                   w=[a, tk_w2, bank_free[j // 2]], inc=True)
        for j in range(8):
            t2 = mm(PSUM[:, 4 + j // 2, (j % 2) * T:(j % 2) * T + T], KT[0:96, 128 * j:128 * j + 128], RK[0:96, 25, 1:T + 1],
                    w=[tk_a2, pw_ok, bank_free[4 + j // 2]], inc=True)
        for j in range(8):
            ld_ok = act(LD[:, j, :], pair_banks(0)[:, j, :], ACT.Sigmoid, [t], bias=col("w0", j))
            bank_free[j // 2] = [ld_ok]
        for j in range(8):
            ic_ok = act(IC[:, j, :], pair_banks(4)[:, j, :], ACT.Sigmoid, [t2], bias=col("a0", j))
            bank_free[4 + j // 2] = [ic_ok]
        pg_ok = act(UU(26, 28), UU(26, 28), ACT.Sigmoid, [pw_ok])
        for j in range(8):
            a = act(KK[:, j, :], U(8 + j), ACT.Copy, [k_ok], scale=col("k_k", j))
        SQ = LA[:, :, :].rearrange("p a b -> p (a b)").rearrange("p (j t) -> p j t", t=T)
        RN = MB[:, :, :].rearrange("p a b -> p (a b)").rearrange("p (j t) -> p j t", t=T)
        KM = MK[:, :, :].rearrange("p a b -> p (a b)").rearrange("p (j t) -> p j t", t=T)
        a = act(SQ, KK[:, :, :], ACT.Square)
        for j in range(8):
            t = mm(pair_banks(0)[:, j, :], bones, SQ[:, j, :], w=[a, bank_free[j // 2]], inc=True)
        rn = act(RN, pair_banks(0), ACT.Sqrt, [t])
        for b in range(4):
            bank_free[b] = [rn]
        om = ts(V, OK[:, :], PK[:, off["k_a"]:off["k_a"] + 8], -1.0, 1.0, MUL, ADD)
        for j in range(8):
            km = act(KM[:, j, :], IC[:, j, :], ACT.Identity, [om], scale=col("k_a", j), bias=OK[:, j:j + 1])
        ts(V, LD[:, :, :], LD[:, :, :], -0.6065306597126334, None, MUL, w=[ld_ok])
        for j in range(8):
            c_ok = scan(C[:, j, :], rm64, LD[:, j, :])
        v = tt(V, LD[:, :, :], C[:, :, :], LD[:, :, :], SUB)
        a_ld = act(LD[:, :, :], LD[:, :, :], ACT.Exp, [v])
        a_rt = act(RT[:, :, :], C[:, :, :], ACT.Exp)
        a_c = act(C[:, :, :], C[:, :, :], ACT.Exp, scale=-1.0)
        ts(V, RN, RN, 1e-12, None, MAX, w=[rn])
        recip(RN, RN)
        kk_ok = tt(V, KK[:, :, :], KK[:, :, :], RN, MUL)
        km_ok = tt(V, UU(8, 16), UU(8, 16), KM, MUL, [km])
        g_ic = tt(G, IC[:, :, :], IC[:, :, :], KK[:, :, :], MUL, [kk_ok, km])
        al_ok = stt(LD[:, :, :], LD[:, :, :], -1.0, KK[:, :, :], MUL, MUL, [a_ld])
        cp(V, PCE[:, :, :], RT[:, :, 63::64], [a_rt])
        r_ok = tt(V, RT[:, :, :], RT[:, :, :], UU(0, 8), MUL)
        b_ok = tt(V, IC[:, :, :], IC[:, :, :], C[:, :, :], MUL, [g_ic, a_c])
        kt_ok = tt(V, C[:, :, :], C[:, :, :], UU(8, 16), MUL)
        g_rk = tt(G, UU(0, 8), UU(0, 8), UU(8, 16), MUL, [r_ok, kt_ok])
        for j in range(8):
            a = act(U(j), U(j), ACT.Copy, [g_rk], scale=col("r_k", j))
        for j in range(8):
            t = mm(pair_banks(4)[:, j, :], bones, U(j), w=[a, bank_free[4 + j // 2]], inc=True)
        bo_ok = tt(V, UU(0, 8), pair_banks(4), UU(16, 24), MUL, [t])
        for b in range(4, 8):
            bank_free[b] = [bo_ok]
        in_ok = [al_ok, r_ok, b_ok, kt_ok, bo_ok]
        if stop == 2:
            dump("a", LD[:, :, :])
            dump("r", RT[:, :, :])
            dump("b", IC[:, :, :])
            dump("k", C[:, :, :])
            dump("bo", UU(0, 8))
            return end()
        half = [KK[:, :, :].rearrange("p a t -> p (a t)"), RK[:, 8:16, :].rearrange("p a t -> p (a t)")[:, 0:2048]]
        tmp4 = [[h[:, 512 * i:512 * i + 512].rearrange("p (h t) -> p h t", t=P) for i in range(4)] for h in half]
        seq_ok = None

        def slot(h):
            return 8 * (h // 8) + 4 * (h % 2) + h % 8 // 2

        for tq in range(2):
            tsl = slice(128 * tq, 128 * tq + 128)
            toks = []
            for i, (src, dst) in enumerate(((UU(16, 24), VT), (IC, BT), (C, KT))):
                for j in range(8):
                    b = 2 * i + j // 4
                    t = tr(PSUM[:, b, (j % 4) * 128:(j % 4) * 128 + 128], src[:, j, tsl], ident, [in_ok, bank_free[b]], inc=True)
                a = act(dst[:, :], PSUM[:, 2 * i:2 * i + 2, :].rearrange("p b n -> p (b n)"), ACT.Copy, [t, seq_ok])
                bank_free[2 * i] = bank_free[2 * i + 1] = [a]
                toks.append(a)

            def chain(g, ch):
                LT, X, Z, ML = tmp4[ch]
                XT = XT_[:, 4 * g:4 * g + 4, :]
                hs = slice(4 * g, 4 * g + 4)
                b0 = 4 * ch

                def four(b, lsrc, rsrc):
                    for i in range(4):
                        p = slice(64 * ch, 64 * ch + 64)
                        t = mm(PSUM[:, b, 128 * i:128 * i + 128], lsrc[p, 4 * (g // 2) + i, tsl], rsrc[p, 4 * (g // 2) + i, tsl],
                               w=[in_ok, bank_free[b]], inc=i == 3)
                    return t, PSUM[:, b, :].rearrange("p (h t) -> p h t", t=P)

                def m4(n):
                    return bc(m1[n], 1, [P, 4, P])

                t, ps = four(b0, IC, LD)
                lt_ok = act(LT, ps, ACT.Copy, [t])
                bank_free[b0] = [lt_ok]
                t, ps = four(b0 + 1, LD, IC)
                v = tt(V, X, ps, m4("l1"), MUL, [t])
                bank_free[b0 + 1] = [v]
                yield
                x_ok = tt(V, X, X, bc(ident, 1, [P, 4, P]), ADD)
                tt(V, XT, LT, m4("t1"), MUL, [lt_ok, seq_ok])
                xt_ok = tt(V, XT, XT, bc(ident, 1, [P, 4, P]), ADD)
                yield
                lv = None
                rest = [(C, LD, LA, "strict"), (IC, RT, MB, "incl"), (C, RT, MK, "incl")]
                for s in (2, 4, 8, 16, 32):
                    ml = tt(G, ML, LT, m4(f"t{s}"), MUL, [lt_ok, lv])
                    if rest:
                        ls, rs_, dst, msk = rest.pop(0)
                        t, ps = four(b0 + 3, ls, rs_)
                        v = tt(V, dst[:, hs, :], ps, m4(msk), MUL, [t, seq_ok])
                        bank_free[b0 + 3] = [v]
                        done.append(v)
                    for i in range(4):
                        t = mm(PSUM[:, b0, 128 * i:128 * i + 128], ML[:, i, :], X[:, i, :], w=[ml, x_ok, bank_free[b0]], inc=i == 3)
                    lv = t
                    z = act(Z, PSUM[:, b0, :].rearrange("p (h t) -> p h t", t=P), ACT.Copy, [t, xt_ok, x_ok])
                    bank_free[b0] = [z]
                    yield
                    for i in range(4):
                        t = mm(PSUM[:, b0 + 1, 128 * i:128 * i + 128], Z[:, i, :], XT[:, i, :], w=[z, xt_ok, bank_free[b0 + 1]],
                               inc=i == 3)
                    t1 = t
                    if s < 32:
                        for i in range(4):
                            t = mm(PSUM[:, b0 + 2, 128 * i:128 * i + 128], XT[:, i, :], Z[:, i, :], w=[bank_free[b0 + 2]], inc=i == 3)
                    xt_ok = tt(V, XT, XT, PSUM[:, b0 + 1, :].rearrange("p (h t) -> p h t", t=P), ADD, [t])
                    bank_free[b0 + 1] = [xt_ok]
                    if s < 32:
                        x_ok = tt(V, X, X, PSUM[:, b0 + 2, :].rearrange("p (h t) -> p h t", t=P), ADD)
                        bank_free[b0 + 2] = [x_ok]
                    yield
                done.append(xt_ok)
                busy[ch] = [xt_ok, lv]

            done, busy = [], {}
            for gp in range(2):
                live = [chain(2 * gp, 0), chain(2 * gp + 1, 1)]
                while live:
                    for c_ in list(live):
                        if next(c_, "end") == "end":
                            live.remove(c_)
            s_ok = [s0] if tq == 0 else s_ok
            for cl in range(2):
                R = slice(64 * cl, 64 * cl + 64)
                for j in range(8):
                    b, o = j // 4, (j % 4) * 128
                    mm(PSUM[:, b, o:o + 128], LD[:, j, tsl], S[:, j, :], True, False, [done, toks, s_ok, bank_free[b]])
                    for q in range(2):
                        h = 2 * j + q
                        t = mm(PSUM[:, b, o + 64 * q:o + 64 * q + 64], LA[R, slot(h), :], VT[R, 64 * h:64 * h + 64], False, q == 1, inc=True)
                u_ok = act(US[R, :], PSUM[R, 0:2, :].rearrange("p b n -> p (b n)"), ACT.Copy, [t, seq_ok])
                bank_free[0] = bank_free[1] = [u_ok]
                for h in range(16):
                    b, o = 2 + h // 8, (h % 8) * 64
                    t = mm(PSUM[:, b, o:o + 64], XT_[R, slot(h), :], US[R, 64 * h:64 * h + 64], w=[u_ok, bank_free[b]], inc=True)
                sa_ok = act(SS[R, :], PSUM[R, 2:4, :].rearrange("p b n -> p (b n)"), ACT.Copy, [t])
                bank_free[2] = bank_free[3] = [sa_ok]
                for j in range(8):
                    b, o = 6 + j // 4, (j % 4) * 128
                    js = slice(128 * j, 128 * j + 128)
                    mm(PSUM[:, b, o:o + 128], BT[R, js], SS[R, js], True, False, [sa_ok, bank_free[b]])
                    ts_ok = mm(PSUM[:, b, o:o + 128], KT[R, js], VT[R, js], False, True, inc=True)
                for j in range(8):
                    b, o = 4 + j // 4, (j % 4) * 128
                    mm(PSUM[:, b, o:o + 128], RT[:, j, tsl], S[:, j, :], True, False, [bank_free[b]])
                    for q in range(2):
                        h = 2 * j + q
                        hc = slice(64 * h, 64 * h + 64)
                        mm(PSUM[:, b, o + 64 * q:o + 64 * q + 64], MB[R, slot(h), :], SS[R, hc], False, False)
                        t = mm(PSUM[:, b, o + 64 * q:o + 64 * q + 64], MK[R, slot(h), :], VT[R, hc], False, q == 1, inc=True)
                sp = PSUM[:, 6:8, :].rearrange("p b (j n) -> p (b j) n", n=P)
                for q in range(2):
                    p = slice(64 * q, 64 * q + 64)
                    tt(V, S[p, :, p], S[p, :, p], sp[p, :, p], ADD, [t, ts_ok])
                    v = tt(V, S[p, :, p], S[p, :, p], bc(PCE[p, :, 2 * tq + cl], 2, [64, 8, 64]), MUL)
                s_ok = [v]
                bank_free[6] = bank_free[7] = [v]
                y_ok = act(US[R, :], PSUM[R, 4:6, :].rearrange("p b n -> p (b n)"), ACT.Copy, [t])
                bank_free[4] = bank_free[5] = [y_ok]
            for j in range(8):
                b = j // 4
                t = tr(PSUM[:, b, (j % 4) * 128:(j % 4) * 128 + 128], US[:, 128 * j:128 * j + 128], ident, [y_ok, bank_free[b]], inc=True)
            a = act(LD[:, :, tsl], PSUM[:, 0:2, :].rearrange("p b (j n) -> p (b j) n", n=P), ACT.Copy, [t])
            bank_free[0] = bank_free[1] = [a]
            seq_ok = t
        G2 = C[:, :, :].rearrange("p a t -> p (a t)").rearrange("p (k n) -> p k n", k=2)
        tk_g2 = dma_g("d_rg2", G2, A_["rg2"].rearrange("(k p) n -> p k n", p=P), [seq_ok])
        for j in range(8):
            t = mm(pair_banks(0)[:, j, :], bones, LD[:, j, :], w=[a, bank_free[j // 2]], inc=True)
        v = stt(LD[:, :, :], pair_banks(0), -1.0 / 64, LD[:, :, :], MUL, ADD, [t])
        for b in range(4):
            bank_free[b] = [v]
        a = act(KK[:, :, :], LD[:, :, :], ACT.Square, [v])
        for j in range(8):
            t = mm(pair_banks(4)[:, j, :], bones, KK[:, j, :], w=[a, bank_free[4 + j // 2]], inc=True)
        a = act(IC[:, :, :], pair_banks(4), ACT.Sqrt, [t], bias=col("eps64"), scale=1.0 / 64)
        for b in range(4, 8):
            bank_free[b] = [a]
        recip(IC[:, :, :], IC[:, :, :], [a])
        v = tt(V, LD[:, :, :], LD[:, :, :], IC[:, :, :], MUL)
        for j in range(8):
            a = act(LD[:, j, :], LD[:, j, :], ACT.Identity, [v], scale=col("ln_w", j), bias=col("ln_b", j))
        for j in range(8):
            for k in range(2):
                t = mm(pair_banks(0)[:, j, :], G2[:, k, 128 * j:128 * j + 128], U(26 + k), k == 0, k == 1,
                       w=[tk_g2, bank_free[j // 2]], inc=True)
        tt(V, LD[:, :, :], LD[:, :, :], UU(0, 8), ADD, [a])
        v = tt(V, LD[:, :, :], LD[:, :, :], pair_banks(0), MUL, [t])
        for b in range(4):
            bank_free[b] = [v]
        s2.close()
        s1a.close()
        if stop == 3:
            dump("ys", YS[:, :, :])
            dump("yr", LD[:, :, :])
            return end()
        XT = Scope("right")("xt", [P, 16, T])
        r0 = Scope("right")
        GH = r0("ghi", [P, 16, T], F32R)
        GL = r0("glo", [P, 16, T], F32R)
        tk_x = dma_g("d_x1", XT[:, :, :], A_["x"])
        mix_ok = []
        for src, o in ((YS, 0), (LD, 8)):
            h = act(GH[:, o:o + 8, :], src[:, :, :], ACT.Copy)
            mix_ok = [h, tt(V, GL[:, o:o + 8, :], src[:, :, :], GH[:, o:o + 8, :].bitcast(F32), SUB, [h])]
        s1.close()

        s4 = Scope()
        TM = s4("tm4", [P, 8, T])
        ACC = s4("acc4", [P, T])
        SQ2 = s4("sq4", [P, 2, T])
        RS = s4("rs4", [P, 2, T])
        SM = s4("sm4", [P, 8, 4])
        HH = s4("hhi", [P, 16, T], F32R)
        HL = s4("hlo", [P, 16, T], F32R)
        s5 = Scope()
        KX = s5("kx", [P, 16, T])
        VX = s5("vx", [P, 2, 2048])
        QT = s5("qt", [P, 16, T])
        tk_mem = dma_g("d_mem", QT[:, :, :], A_["mem"])
        m_ok, h_ok = {}, {}

        def mem_norm():
            sq = mean_square(QT, TM, [tk_mem])
            yield
            r = rstd_of([TM[:, i, :] for i in range(4)], 2048, "eps6", RS[:, 1, :], [sq])
            yield
            yield from normed(QT, RS[:, 1, :], lambda j: col("norm_mem_g", j), zcol, TM, HH, HL, [r], m_ok)

        ev, last = residual(XT, ACC[:, :], SQ2)
        side.append(mem_norm())
        gemm(PL["out"], [(GH, GL)], ev, [mix_ok, tk_x])
        drain()
        out_done = TE.now()
        if stop == 4:
            dump("x1", XT[:, :, :])
            return end()

        def x_norm(name, w):
            r = rstd_of([ACC[:, :]], 2048, "eps6", RS[:, 0, :], [last["g"], last["v"]])
            yield
            yield from normed(XT, RS[:, 0, :], lambda j: col(name, j), zcol, TM, GH, GL, [r, w], h_ok)

        side.append(x_norm("norm_x_g", out_done))

        def ev_copy(dst):
            return lambda t, r_, ps, tok: act(dst(t, r_), ps, ACT.Copy, [tok])

        gemm(PL["xk"], [(HH, HL)], ev_copy(lambda t, r_: KX[:, t, :]), m_ok)
        kx_ok = A.now()
        gemm_tok(PL["xv"], [(HH, HL, slice(0, 128)), (HH, HL, slice(128, 256))],
                 ev_copy(lambda b, r_: VX[:, r_, 512 * b:512 * b + 512]), m_ok)
        vx_ok = A.now()
        drain()
        q_tok = {}
        o_ok = []
        XSC = 512.0 ** -0.5
        PT = TM[:, 4:8, :].rearrange("p (a m) t -> p a m t", a=2)

        def soft(u, ps, n, dst, w):
            s = SM[:, u % 8, :]
            V.add(lambda e: e.reduce_max(s[:, 0:1], ps, AX_X), w)
            return s

        pt_free = {}

        def xattn(hd):
            for st in range(2):
                u = 2 * hd + st
                b = 4 + u % 2
                for k in range(4):
                    t = mm(PSUM[:, b, 0:T], QT[:, 4 * hd + k, 128 * st:128 * st + 128], KX[:, 4 * hd + k, :], k == 0, k == 3,
                           [q_tok[4 * hd + 3], kx_ok, bank_free[b]], inc=k == 3)
                ps = PSUM[:, b, 0:T]
                s = soft(u, ps, T, None, [t])
                v = ts(V, s[:, 1:2], s[:, 0:1], -XSC, None, MUL)
                p = TM[:, u % 4, :]
                a = act(p, ps, ACT.Exp, [v, pt_free.get(("p", u % 4))], bias=s[:, 1:2], scale=XSC, acc=s[:, 2:3])
                bank_free[b] = [a]
                recip(s[:, 3:4], s[:, 2:3], [a])
                v = ts(V, p, p, s[:, 3:4], None, MUL)
                yield
                b = 6
                for m in range(2):
                    t = tr(PSUM[:, b, 128 * m:128 * m + 128], p[:, 128 * m:128 * m + 128], ident, [v, bank_free[b]], inc=m == 1)
                pt_free[("p", u % 4)] = t
                a = act(PT[:, hd % 2, :, 128 * st:128 * st + 128], PSUM[:, b, 0:256].rearrange("p (m s) -> p m s", m=2),
                        ACT.Copy, [t, pt_free.get(hd % 2)])
                bank_free[b] = [a]
                yield
            for d in range(4):
                b = 4 + d if d < 2 else 7
                b = 7 if d % 2 else 5
                dt = 4 * hd + d
                for m in range(2):
                    t = mm(PSUM[:, b, 0:T], VX[:, m, 128 * dt:128 * dt + 128], PT[:, hd % 2, m, :], m == 0, m == 1,
                           [a, vx_ok, bank_free[b]], inc=m == 1)
                pt_free[hd % 2] = t
                h = act(HH[:, dt, :], PSUM[:, b, 0:T], ACT.Copy, [t, vx_done])
                v = tt(V, HL[:, dt, :], PSUM[:, b, 0:T], HH[:, dt, :].bitcast(F32), SUB, [h])
                bank_free[b] = [v]
                o_ok[:] = [h, v]
                yield

        vx_done = TE.now()

        def ev_q(t, r_, ps, tok):
            q_tok[t] = act(QT[:, t, :], ps, ACT.Copy, [tok])
            return q_tok[t]

        gemm(PL["xq"], [(GH, GL)], ev_q, h_ok)
        for hd in range(4):
            side.append(xattn(hd))
        drain()
        q_done = TE.now()
        ev, last = residual(XT, ACC[:, :], SQ2)
        gemm(PL["xo"], [(HH, HL)], ev, o_ok)
        xo_done = TE.now()
        s5.close()
        if stop == 5:
            dump("x2", XT[:, :, :])
            return end()

        r1 = Scope("right")
        CH = r1("chi", [P, 16, T], F32R)
        CL = r1("clo", [P, 16, T], F32R)
        s5 = Scope()
        CX = s5("cx", [P, 16, T])
        RB = s5("rb", [P, 4, T])
        TM5 = TM
        tk_cx = dma_g("d_cx", CX[:, :, :], A_["ctx"])
        h_ok = {}
        run(x_norm("norm_ffn_g", q_done))
        f_ok = {}
        hid = {}

        def mod_gain(i, g, m, c):
            return stt(GS[:, i, :], MOD[:, m:m + 16, c], 1.0, PK[:, off[g]:off[g] + 16], ADD, MUL)

        def ctx_norm():
            sq = mean_square(CX, TM5, [tk_cx, h_ok])
            mod_gain(0, "norm1_g", 16, 1)
            mod_gain(1, "norm1_g", 16, 0)
            v = mod_gain(2, "norm2_g", 64, 0)
            yield
            r = rstd_of([TM5[:, i, :] for i in range(4)], 2048, "eps6", RS[:, 1, :], [sq])
            yield
            yield from normed(CX, RS[:, 1, :], lambda j: GS[:, 0, j:j + 1], lambda j: MOD[:, j, 1:2], TM5, CH, CL,
                              [r, v], c_ok)

        c_ok = {}
        side.append(ctx_norm())
        dn_done = xo_done
        for i in range(4):
            def ev_up(t, r_, ps, tok):
                r = RB[:, t % 2, :]
                q = RB[:, 2 + t % 2, :]
                a = act(r, ps, ACT.Relu, [tok, hid.get(("g", t % 2))])
                hid[("g", t % 2)] = g = tt(G, q, r, r, MUL, [a, hid.get(("v", t % 2))])
                h = act(HH[:, t, :], q, ACT.Copy, [g, dn_done])
                hid[("v", t % 2)] = v = tt(V, HL[:, t, :], q, HH[:, t, :].bitcast(F32), SUB, [h])
                f_ok[i] = [h, v]
                return a

            gemm(PL[f"up{i}"], [(GH, GL)], ev_up, h_ok)
            ev, last = residual(XT, ACC[:, :] if i == 3 else None, SQ2)
            gemm(PL[f"dn{i}"], [(HH, HL)], ev, f_ok[i])
            dn_done = TE.now()
        drain()
        up_done = TE.now()
        if stop == 6:
            dump("x3", XT[:, :, :])
            return end()
        r = rstd_of([ACC[:, :]], 2048, "eps6", RS[:, 0, :], [last["g"], last["v"]])
        for j in range(16):
            v = stt(XT[:, j, :], XT[:, j, :], col("final_g", j), RS[:, 0, :], MUL, MUL)
        sq = mean_square(XT, TM5, [v])
        r = rstd_of([TM5[:, i, :] for i in range(4)], 2048, "eps6", RS[:, 0, :], [sq])
        h_ok = {}
        run(normed(XT, RS[:, 0, :], lambda j: GS[:, 1, j:j + 1], lambda j: MOD[:, j, 0:1], TM5, GH, GL, [r, up_done], h_ok))
        s5.close()
        s4.close()

        s6 = Scope()
        Y2 = s6("y2", [P, 16, T])
        SM = s6("sm6", [P, 8, 4])
        FT = s6("ft", [P, 4, T])
        HY = s6("hy", [P, 12, T + 2])
        s6c = Scope()
        K2 = s6c("k2", [P, 8, 512])
        V2 = s6c("v2", [P, 4, 1024])
        hpad = fill(G, HY[:, :, 0:1], 0.0)
        hpad = fill(G, HY[:, :, T + 1:T + 2], 0.0)
        gemm(PL["k2"], [(GH, GL), (CH, CL)], ev_copy(lambda t, r_: K2[:, t, T * r_:T * r_ + T]), [h_ok, c_ok])
        k2_ok = A.now()
        gemm_tok(PL["v2"], [(GH, GL, slice(0, 128)), (GH, GL, slice(128, 256)), (CH, CL, slice(0, 128)), (CH, CL, slice(128, 256))],
                 ev_copy(lambda b, r_: V2[:, r_, 512 * b:512 * b + 512]), [h_ok, c_ok])
        v2_ok = A.now()
        r1.close()
        s7 = Scope()
        QT2 = s7("q2", [P, 8, T])
        BI = s7("bi", [P, 2, 2, T])
        MS = s7("ms", [P, 2, T])
        PP = s7("pp", [P, 2, 512])
        PT2 = s7("pt2", [P, 2, 4, T])
        tk_ms = dma_g("d_ms", MS[:, :, :].rearrange("p a t -> p (a t)"), A_["namask"])
        NSC = 128.0 ** -0.5
        q2_tok, bi_free, pp_free, pt2_free, a_tok = {}, {}, {}, {}, {}

        def na(h):
            tk = dma_g(f"d_bi{h % 2}", BI[:, h % 2, :, :], A_["bias"][h].rearrange("(a p) t -> p a t", p=P), [bi_free.get(h % 2)])
            bi = tt(G, BI[:, h % 2, :, :], BI[:, h % 2, :, :], MS[:, :, :], ADD, [tk, tk_ms])
            yield
            for qt in range(2):
                u = 2 * h + qt
                b = 4 * turn[0]
                t = mm(PSUM[:, b, :], QT2[:, h, 128 * qt:128 * qt + 128], K2[:, h, :], w=[q2_tok[h], k2_ok, bank_free[b]], inc=True)
                p = PP[:, u % 2, :]
                c_ = ts(V, p[:, T:512], PSUM[:, b, T:512], NSC, None, MUL, w=[t, pp_free.get(u % 2)])
                v = stt(p[:, 0:T], PSUM[:, b, 0:T], NSC, BI[:, h % 2, qt, :], MUL, ADD, [bi])
                bank_free[b] = [v]
                bi_free[h % 2] = v
                s = soft(u, p, 512, None, [])
                v = ts(V, s[:, 1:2], s[:, 0:1], -1.0, None, MUL)
                a = act(p, p, ACT.Exp, [v], bias=s[:, 1:2], acc=s[:, 2:3])
                recip(s[:, 3:4], s[:, 2:3], [a])
                v = ts(V, p, p, s[:, 3:4], None, MUL)
                yield
                b = 4 * turn[0] + 1
                for k in range(4):
                    t = tr(PSUM[:, b, 128 * k:128 * k + 128], p[:, 128 * k:128 * k + 128], ident, [v, bank_free[b]], inc=k == 3)
                pp_free[u % 2] = t
                a = act(PT2[:, h % 2, :, 128 * qt:128 * qt + 128], PSUM[:, b, :].rearrange("p (k s) -> p k s", k=4),
                        ACT.Copy, [t, pt2_free.get(h % 2)])
                bank_free[b] = [a]
                yield
            b = 4 * turn[0] + 2
            for k in range(4):
                t = mm(PSUM[:, b, 0:T], V2[:, k, 128 * h:128 * h + 128], PT2[:, h % 2, k, :], k == 0, k == 3,
                       [a, v2_ok, bank_free[b]], inc=k == 3)
            pt2_free[h % 2] = t
            a_tok[h] = act(Y2[:, h, :], PSUM[:, b, 0:T], ACT.Copy, [t])
            bank_free[b] = [a_tok[h]]
            yield

        def ev_q2(t, r_, ps, tok):
            q2_tok[t] = act(QT2[:, t, :], ps, ACT.Copy, [tok])
            return q2_tok[t]

        gemm(PL["q2"], [(GH, GL)], ev_q2, h_ok)

        def ev_fh(t, r_, ps, tok):
            return act(FT[:, t, :] if t < 4 else HY[:, t - 4, 1:T + 1], ps, ACT.Copy, [tok, hpad])

        for h in range(8):
            side.append(na(h))
        gemm(PL["fh"], [(GH, GL)], ev_fh, h_ok)
        fh_ok = A.now()
        drain()
        s7.close()
        s6c.close()
        r0.close()

        s8 = Scope()
        SPEC = s8("spec", [P, 2, 2, 2, 512])
        DF = s8("dft", [P, 4, 2, T])
        FC = s8("fft", [P, 1280])
        CA = s8("ca", [P, 2, T])
        RG = s8("rg2", [P, 3, T])
        s9 = Scope()
        ZT = s9("zt", [33, T])
        W1 = s9("hw1", [33, 64])
        W2 = s9("hw2", [64, 64])
        W3 = s9("hw3", [64, 2048])
        WN = s9("win", [P, 2, 2, 512])
        HF = s9("hf", [P, 2, 2048])
        HD = s9("hd", [64, 4, T])
        tk_df = dma_g("d_df", DF[:, :, :, :].rearrange("p a b t -> p (a b t)"), A_["dft"])
        tk_fc = dma_g("d_fc", FC[:, :], A_["fft"])
        tk_h1 = [dma_g("d_zt", ZT[:, :], A_["zt"]), dma_g("d_hw1", W1[:, :], A_["hy_w1"]), dma_g("d_hw2", W2[:, :], A_["hy_w2"]),
                 dma_g("d_hw3", W3[:, :], A_["hy_w3"]),
                 dma_g("d_win", WN[:, :, :, :].rearrange("p a b t -> p (a b t)"), A_["win"])]
        conv = {}
        for j in range(12):
            b = CA[:, j % 2, :]
            ts(V, b, HY[:, j, 2:T + 2], col("hy_cw", 24 + j), None, MUL, w=[fh_ok, conv.get(j % 2)])
            for i in (1, 0):
                v = stt(b, HY[:, j, i:i + T], col("hy_cw", 12 * i + j), b, MUL, ADD)
            conv[j % 2] = hy_ok = act(HY[:, j, 1:T + 1], b, ACT.Identity, [v], bias=col("hy_cb", j))
        d = [HD[:, i, :] for i in range(4)]

        def layer(wt, rhs, bias, w):
            t = mm(PSUM[0:64, 0, 0:T], wt, rhs, w=[w, bank_free[0]], inc=True)
            v = ts(V, d[0], PSUM[0:64, 0, 0:T], col(bias, rows=64), col("hy_freq", rows=64), ADD, MUL, [t])
            bank_free[0] = [v]
            ts(V, d[1], d[0], 0.15915494309189535, 12582912.0, MUL, ADD)
            ts(V, d[1], d[1], 12582912.0, None, SUB)
            stt(d[0], d[1], -6.28125, d[0], MUL, ADD)
            stt(d[0], d[1], -0.0019353071795864769, d[0], MUL, ADD)
            v = ts(V, d[0], d[0], 3.1415925, -3.1415925, MIN, MAX)
            return act(d[2], d[0], ACT.Sin, [v])

        a = layer(W1[:, :], ZT[:, :], "hy_b1", tk_h1)
        a = layer(W2[:, :], d[2], "hy_b2", a)
        for o in range(2):
            for dr in range(2):
                n = 2 * o + dr
                for tq in range(2):
                    b = 2 * (n % 2) + tq
                    t = mm(PSUM[:, b, :], d[2][:, 128 * tq:128 * tq + 128], W3[:, 512 * n:512 * n + 512], w=[a, bank_free[b]], inc=True)
                    v = tt(V, HF[:, tq, 512 * n:512 * n + 512], PSUM[:, b, :], WN[:, dr, tq, :], MUL, [t])
                    bank_free[b] = [v]
        for o in range(2):
            f_, b_ = HF[:, :, 1024 * o:1024 * o + 512], HF[:, :, 1024 * o + 512:1024 * o + 1024]
            g = tt(G, f_, f_, b_, ADD, [v])
            h = stt(b_, b_, -2.0, f_, MUL, ADD, [g])
            for ri in range(2):
                for f in range(2):
                    b = 4 + 2 * ri + f
                    for k in range(2):
                        t = mm(PSUM[:, b, :], DF[:, ri, k, 128 * f:128 * f + 128], HF[:, k, 1024 * o + 512 * ri:1024 * o + 512 * ri + 512],
                               k == 0, k == 1, [h, tk_df, bank_free[b]], inc=k == 1)
                    sp_ok = act(SPEC[:, o, ri, f, :], PSUM[:, b, :], ACT.Copy, [t])
                    bank_free[b] = [sp_ok]
        s9.close()
        s9 = Scope()
        ZK = s9("zk", [P, 2, 512])
        YF = s9("yf", [P, 2, 2, 512])
        Q1 = s9("q1", [P, 2, 512])
        Q3 = s9("q3", [P, 2, 512])
        AB = s9("ab", [P, 2, 4, T])
        for g in range(4):
            for tq in range(2):
                t = mm(PSUM[:, g, T * tq:T * tq + T], FT[:, g, 128 * tq:128 * tq + 128], FC[:, 1024:1280],
                       w=[tk_fc, fh_ok, bank_free[g]], inc=tq == 1)
            a = act(AB[:, :, g, :], PSUM[:, g, :].rearrange("p (q t) -> p q t", q=2), ACT.Copy, [t])
            bank_free[g] = [a]
        for g in range(4):
            b = 4 + g
            for n in range(4):
                k, cs = n // 2, n % 2
                t = mm(PSUM[:, b, 0:T], AB[:, k, g, 128 * cs:128 * cs + 128], FC[:, 512 * cs + T * k:512 * cs + T * k + T],
                       n == 0, n == 3, [a, bank_free[b]], inc=n == 3)
            f_ok2 = act(Y2[:, 8 + g, :], PSUM[:, b, 0:T], ACT.Copy, [t])
            bank_free[b] = [f_ok2]
        src_ok = hy_ok
        for o in range(2):
            for tq in range(2):
                for j in range(4):
                    t = tr(PSUM[:, tq, 128 * j:128 * j + 128], HY[:, j, 1 + 128 * tq:129 + 128 * tq], ident,
                           [src_ok, bank_free[tq]], inc=j == 3)
                a = act(ZK[:, tq, :], PSUM[:, tq, :], ACT.Copy, [t])
                bank_free[tq] = [a]
            for ri in range(2):
                for f in range(2):
                    b = 4 + 2 * ri + f
                    for k in range(2):
                        t = mm(PSUM[:, b, :], DF[:, ri, k, 128 * f:128 * f + 128], ZK[:, k, :], k == 0, k == 1,
                               [a, tk_df, bank_free[b]], inc=k == 1)
            zr, zi = PSUM[:, 4:6, :], PSUM[:, 6:8, :]
            kr, ki = SPEC[:, o, 0, :, :], SPEC[:, o, 1, :, :]
            tt(V, YF[:, 0, :, :], zr, kr, MUL, [t, sp_ok])
            v = tt(V, Q1[:, :, :], zi, ki, MUL)
            g = tt(G, YF[:, 0, :, :], YF[:, 0, :, :], Q1[:, :, :], SUB, [v])
            tt(V, YF[:, 1, :, :], zr, ki, MUL)
            v = tt(V, Q3[:, :, :], zi, kr, MUL)
            for b in range(4, 8):
                bank_free[b] = [v]
            v = tt(V, YF[:, 1, :, :], YF[:, 1, :, :], Q3[:, :, :], ADD)
            for j in range(4):
                b = j
                for n in range(4):
                    ri, f = n // 2, n % 2
                    t = mm(PSUM[:, b, 0:T], YF[:, ri, f, 128 * j:128 * j + 128], DF[:, 2 + ri, f, :], n == 0, n == 3,
                           [g, v, bank_free[b]], inc=n == 3)
                u_ = HY[:, j, 1:T + 1]
                w_ = stt(u_, u_, col("hy_bias", 4 * o + j), PSUM[:, b, 0:T], MUL, ADD, [t])
                bank_free[b] = [w_]
                src_ok = tt(V, u_ if o == 0 else Y2[:, 12 + j, :], u_, HY[:, 4 + 4 * o + j, 1:T + 1], MUL)
        if stop == 7:
            dump("a", Y2[:, 0:8, :])
            dump("f", Y2[:, 8:12, :])
            dump("hy", Y2[:, 12:16, :])
            return end()
        s9.close()
        r0 = Scope("right")
        GH = r0("g2hi", [P, 16, T], F32R)
        GL = r0("g2lo", [P, 16, T], F32R)
        s9 = Scope()
        TM = s9("tm9", [P, 8, T])
        mg = [(0, 8, 1024), (8, 12, 512), (12, 16, 512)]
        y_ok = []
        for i, (a_, b_, n) in enumerate(mg):
            a = act(TM[:, 0:b_ - a_, :], Y2[:, a_:b_, :], ACT.Square)
            r = rstd_of([TM[:, k, :] for k in range(b_ - a_)], n, "eps6", RG[:, i, :], [a], b=i)
            for j in range(a_, b_):
                v = stt(Y2[:, j, :], Y2[:, j, :], col("mix_g", j), RG[:, i, :], MUL, MUL)
            h = act(GH[:, a_:b_, :], Y2[:, a_:b_, :], ACT.Copy, [v])
            y_ok = [h, tt(V, GL[:, a_:b_, :], Y2[:, a_:b_, :], GH[:, a_:b_, :].bitcast(F32), SUB, [h])]
        s9.close()
        s8.close()
        s6.close()

        s4 = Scope()
        TM = s4("tma", [P, 8, T])
        ACC = s4("acca", [P, T])
        SQ2 = s4("sqa", [P, 2, T])
        RS = s4("rsa", [P, 2, T])
        HH = s4("h2hi", [P, 11, T], F32R)
        HL = s4("h2lo", [P, 11, T], F32R)
        GA = s4("ga", [P, 11, T])
        GP = s4("gp", [P, 4, T + 2])
        CV = s4("cv", [P, 2, T])
        UB = s4("ub", [P, 2, T])
        gp0 = fill(G, GP[:, :, 0:1], 0.0)
        gp0 = fill(G, GP[:, :, T + 1:T + 2], 0.0)
        ev, last = residual(XT, ACC[:, :], SQ2, lambda t: MOD[:, 32 + t, 0:1])
        gemm(PL["out2"], [(GH, GL)], ev, y_ok)
        out_done = TE.now()
        h_ok = {}
        r = rstd_of([ACC[:, :]], 2048, "eps6", RS[:, 0, :], [last["g"], last["v"]])
        run(normed(XT, RS[:, 0, :], lambda j: GS[:, 2, j:j + 1], lambda j: MOD[:, 48 + j, 0:1], TM, GH, GL, [r, out_done], h_ok))
        if stop == 8:
            dump("x5", XT[:, :, :])
            return end()
        dn_done = out_done
        f_ok, hid = {}, {}
        for i in range(4):
            def ev_gate(t, r_, ps, tok):
                gt = 11 * i + t
                src = GP[:, t % 4, :]
                e_ = act(src[:, 1:T + 1], ps, ACT.Copy, [tok, gp0, hid.get(("c", t % 4))])
                b = CV[:, t % 2, :]
                ts(V, b, src[:, 2:T + 2], col("ff_cw", 88 + gt), None, MUL, w=[e_, hid.get(("a", t % 2))])
                stt(b, src[:, 1:T + 1], col("ff_cw", 44 + gt), b, MUL, ADD)
                hid[("c", t % 4)] = v = stt(b, src[:, 0:T], col("ff_cw", gt), b, MUL, ADD)
                hid[("a", t % 2)] = hid[("g", t)] = act(GA[:, t, :], b, ACT.Gelu_apprx_tanh, [v, hid.get(("u", t))], bias=col("ff_cb", gt))
                return e_

            def ev_uu(t, r_, ps, tok):
                q = UB[:, t % 2, :]
                hid[("u", t)] = v = tt(V, q, ps, GA[:, t, :], MUL, [tok, hid[("g", t)]])
                h = act(HH[:, t, :], q, ACT.Copy, [v, dn_done])
                f_ok[i] = [h, tt(V, HL[:, t, :], q, HH[:, t, :].bitcast(F32), SUB, [h])]
                return v

            gemm(PL[f"ga{i}"], [(GH, GL)], ev_gate, h_ok)
            gemm(PL[f"uu{i}"], [(GH, GL)], ev_uu, h_ok)
            ev, last = residual(XT, ACC[:, :] if i == 3 else None, SQ2, lambda t: MOD[:, 80 + t, 0:1])
            gemm(PL[f"dd{i}"], [(HH, HL)], ev, f_ok[i])
            dn_done = TE.now()
        r = rstd_of([ACC[:, :]], 2048, "eps6", RS[:, 0, :], [last["g"], last["v"]])
        for j in range(16):
            v = stt(XT[:, j, :], XT[:, j, :], col("final_g2", j), RS[:, 0, :], MUL, MUL)
            if j % 4 == 3:
                dma(SP, "d_out", out[:, j - 3:j + 1, :], XT[:, j - 3:j + 1, :], [v])
        end()


def _layout(inp):
    import numpy as np
    f = np.float32
    a = {k: np.asarray(v) for k, v in inp.items()}

    def cols(v, n=None):
        v = np.asarray(v).reshape(-1)
        return np.ascontiguousarray(v.reshape(-1, 128).T)

    def padded(v):
        o = np.zeros((128, 1), f)
        v = np.asarray(v).reshape(-1)
        o[:v.size, 0] = v
        return o

    def tiles(v):
        return np.concatenate([cols(r) for r in v], axis=1)

    mu = a["rwkv_mu"][0]
    mu = np.concatenate([cols(mu[:3072]), padded(mu[3072:3168]), padded(mu[3168:3264]), cols(mu[3264:])], axis=1)
    one = np.ones((128, 1), f)
    parts = {
        "norm_mix_g": cols(a["norm_mix_g"]), "conv_w": tiles(a["ssd_conv_w"][0, :, 0]), "conv_b": cols(a["ssd_conv_b"]),
        "ssd_g": cols(a["ssd_norm_g"]), "ssd_d": cols(np.repeat(a["ssd_d"][0], 64)), "dt_bias": padded(a["ssd_dt_bias"]),
        "a_log": padded(a["ssd_a_log"]), "mu": mu, "w0": cols(a["rwkv_w0"]), "a0": cols(a["rwkv_a0"]),
        "k_k": cols(a["rwkv_k_k"]), "k_a": cols(a["rwkv_k_a"]), "r_k": cols(a["rwkv_r_k"]), "ln_w": cols(a["rwkv_ln_w"]),
        "ln_b": cols(a["rwkv_ln_b"]), "norm_x_g": cols(a["norm_x_g"]), "norm_mem_g": cols(a["norm_mem_g"]),
        "norm_ffn_g": cols(a["norm_ffn_g"]), "final_g": cols(a["final_norm_g"]), "c": cols(a["c_2"]),
        "c_ctx": cols(a["c_ctx_2"]), "ada_b": cols(a["ada_b_2"]), "norm1_g": cols(a["norm1_g_2"]),
        "norm2_g": cols(a["norm2_g_2"]), "hy_cw": tiles(a["hy_conv_w_2"][0]), "hy_cb": cols(a["hy_conv_b_2"]),
        "mix_g": cols(a["mix_norm_g_2"]), "ff_cw": tiles(a["ffn_conv_w_2"][0]), "ff_cb": cols(a["ffn_conv_b_2"]),
        "hy_bias": tiles(a["hy_bias_2"][0]), "final_g2": cols(a["final_norm_g_2"]), "hy_b1": padded(a["hy_b1_2"]),
        "hy_b2": padded(a["hy_b2_2"]), "hy_freq": padded(a["hy_freq_2"]), "one": one, "eps6": one * f(1e-6),
        "eps64": one * f(64e-5), "zero": np.zeros((128, 1), f),
    }
    d = {"pack": np.concatenate([parts[n] for n, _ in COLS], axis=1)}

    i = np.arange(128)
    r, c = i[:, None], i[None, :]
    d["mats"] = np.concatenate([np.eye(128), np.ones((128, 128)), (r // 64 == c // 64)], axis=1).astype(f)

    def level(t, u, s):
        return (t // (2 * s) == u // (2 * s)) & (t // s % 2 == 1) & (u // s % 2 == 0)

    same = r // 64 == c // 64
    m1 = [c >= r, level(r, c, 1)] + [level(c, r, s) for s in (1, 2, 4, 8, 16, 32)] + [same & (r < c), same & (r <= c)]
    t = np.arange(256)
    m1 += [np.broadcast_to(t % 128 != 0, (128, 256)), np.broadcast_to(t % 64 != 0, (128, 256))]
    d["mats1"] = np.concatenate(m1, axis=1).astype(f)
    d["comb"] = np.array([[1, 0], [0, 1], [1, 0], [0, 1]], f)
    d["sel"] = np.repeat(np.eye(16), 128, axis=1).astype(f)

    def fm(v):
        return np.ascontiguousarray(v.T.reshape(-1, 128, v.shape[0]).transpose(1, 0, 2))

    d["x"], d["mem"], d["ctx"] = fm(a["x"][0]), fm(a["mem"][0]), fm(a["ctx_2"][0])
    for n in WEIGHTS:
        d[n] = a[n][0]
    k = np.arange(256)
    th = np.pi * np.outer(t, 2 * k + 1) / 512.0

    def km(m):
        return m.reshape(2, 128, -1).transpose(1, 0, 2).reshape(128, -1)

    d["dft"] = np.ascontiguousarray(np.concatenate([km(np.cos(th)), km(-np.sin(th)), km(np.cos(th).T / 256),
                                                    km(-np.sin(th).T / 256)], axis=1).astype(f))
    w = 2 * np.pi / 256
    cl, sl = np.cos(w * (np.outer(t, t) % 256)), np.sin(w * (np.outer(t, t) % 256))
    q = np.arange(128)
    cd, sd = (fn(2 * np.pi / 128 * (np.outer(q, q) % 128)) for fn in (np.cos, np.sin))
    n = 1 / np.sqrt(256.0 * 128.0)
    d["fft"] = np.ascontiguousarray(np.concatenate([km(cl * n), km(-sl * n), cd, sd], axis=1).astype(f))
    pos = np.arange(256, dtype=f)
    tl = pos / f(255)
    bands = np.linspace(1e-4, 15, 16).astype(f)
    ang = bands[None, :] * f(2.0 * np.pi / 256) * pos[:, None]
    d["zt"] = np.ascontiguousarray(np.concatenate([tl[:, None], np.cos(ang), -np.sin(ang)], axis=1).astype(f).T)
    lo, hi = np.log(1e-2) / 1.5, np.log(1e-2) / 0.3
    deltas = np.linspace(lo, hi, 512).astype(f)
    win = np.exp(-tl[:, None] * np.abs(deltas)[None, :]).astype(f)
    winb = win.copy()
    winb[0] = 0
    d["win"] = np.ascontiguousarray(np.concatenate([km(win), km(winb)], axis=1).astype(f))
    d["hy_w1"], d["hy_w2"], d["hy_w3"] = a["hy_w1_2"][0], a["hy_w2_2"][0], a["hy_w3_2"][0]
    d["rw2"], d["ra2"], d["rg2"] = a["rwkv_w2"][0], a["rwkv_a2"][0], a["rwkv_g2"][0]
    row, cc = t // 64, t % 64
    st = np.clip(cc - 8, 0, 48)
    inside = (cc[None, :] >= st[:, None]) & (cc[None, :] < st[:, None] + 16)
    dr = row[None, :] - row[:, None] + 7
    dc = np.clip(cc[None, :] - cc[:, None] + 15, 0, 30)
    d["bias"] = np.ascontiguousarray(a["na_rpb_2"][0][:, dr, dc])
    d["namask"] = np.ascontiguousarray(km(np.where(inside, 0.0, -1e30)).astype(f))
    return {k: np.ascontiguousarray(v) for k, v in d.items()}


WEIGHTS = ["w_in", "w_out", "xattn_wq", "xattn_wk", "xattn_wv", "xattn_wo", "ffn_w1", "ffn_w2", "ada_w_2", "w_in_2",
           "w_out_2", "ffn_w_up_2", "ffn_w_down_2"]
STOP = 99


def kernel(**inputs):
    import numpy as _np
    import concourse.bacc as _bacc
    from concourse import mybir as _mybir
    from concourse.bass_utils import run_bass_kernel_spmd as _run

    nc = _bacc.Bacc("TRN2", target_bir_lowering=False, num_devices=1)
    arrays, args = {}, {}
    for name, v in _layout(inputs).items():
        arrays["in_" + name] = v
        args[name] = nc.dram_tensor("in_" + name, v.shape, _mybir.dt.from_np(v.dtype), kind="ExternalInput").ap()
    out = nc.dram_tensor("out_0", (128, 16, 256), _mybir.dt.float32, kind="ExternalOutput").ap()
    build(nc, args, out, STOP)
    r = _run(nc, [arrays], core_ids=[0])
    y = r.results[0]["out_0"]
    return _np.ascontiguousarray(y.transpose(2, 1, 0).reshape(1, 256, 2048))
```

```python
from contextlib import ExitStack

import concourse.bass as bass
from concourse import mybir

F32 = mybir.dt.float32
F32R = mybir.dt.float32r
ACT = mybir.ActivationFunctionType
ALU = mybir.AluOpType
AX_X = mybir.AxisListType.X
ADD, SUB, MUL, MAX, MIN = ALU.add, ALU.subtract, ALU.mult, ALU.max, ALU.min
P = 128
T = 256
NR = 6
NH = 4
CS = 1024
NA0 = 6
NA1 = 9
NA2 = 12
CN = 512

COLS = [("norm_mix_g", 16), ("conv_w", 48), ("conv_b", 12), ("ssd_g", 8), ("ssd_d", 8), ("dt_bias", 1),
        ("a_log", 1), ("mu", 28), ("w0", 8), ("a0", 8), ("k_k", 8), ("k_a", 8), ("r_k", 8), ("ln_w", 8),
        ("ln_b", 8), ("norm_x_g", 16), ("norm_mem_g", 16), ("norm_ffn_g", 16), ("final_g", 16), ("c", 16),
        ("c_ctx", 16), ("ada_b", 96), ("norm1_g", 16), ("norm2_g", 16), ("hy_cw", 36), ("hy_cb", 12),
        ("mix_g", 16), ("ff_cw", 132), ("ff_cb", 44), ("hy_bias", 8), ("final_g2", 16), ("hy_b1", 1),
        ("hy_b2", 1), ("hy_freq", 1), ("one", 1), ("eps6", 1), ("eps64", 1), ("zero", 1)]
MATS = ["ident", "ones", "bones"]
MATS1 = ["cm", "l1", "t1", "t2", "t4", "t8", "t16", "t32", "strict", "incl"]
RMS = ["rm128", "rm64"]


def offsets(items):
    out, at = {}, 0
    for name, n in items:
        out[name] = at
        at += n
    return out, at


class Queue:

    def __init__(self, sem, chain):
        self.sem, self.chain, self.ops, self.n, self.seen, self.held = sem, chain, [], 0, {}, []

    def add(self, fn, w=(), inc=True):
        need = {}
        toks = list(w) + self.held + ([(self.sem, self.n)] if self.chain and self.n else [])
        self.held = []
        while toks:
            t = toks.pop()
            if isinstance(t, list):
                toks += t
            elif isinstance(t, dict):
                toks += t["g"]
            elif t is not None and t[1] > max(need.get(t[0], 0), self.seen.get(t[0], 0)):
                need[t[0]] = t[1]
        self.seen.update(need)
        self.ops.append((list(need.items()), fn, inc))
        self.n += 1 if inc else 0
        return (self.sem, self.n) if inc else None

    def now(self):
        assert self.chain or not self.ops or self.ops[-1][2]
        return (self.sem, self.n)

    def play(self, eng, sems):
        for need, fn, inc in self.ops:
            for s, v in need:
                eng.wait_ge(sems[s], v)
            ins = fn(eng)
            if inc:
                ins.then_inc(sems[self.sem], 1)


def build(nc, A_, out, stop=99):
    sems = {}
    top = ExitStack()
    with top:
        def sem(name):
            sems[name] = top.enter_context(nc.semaphore(name))
            return name

        class Scope:
            def __init__(self, side="left"):
                self.st, self.side = ExitStack(), side

            def __call__(self, name, shape, dt=F32):
                return self.st.enter_context(nc.sbuf_tensor(name, shape, dt, side=self.side))

            def close(self):
                self.st.close()
                fence()

        V, A, G, TE, SP = (Queue(sem("s_dve"), True), Queue(sem("s_act"), True), Queue(sem("s_pool"), True),
                           Queue(sem("s_pe"), False), Queue(sem("s_sp"), False))
        counts = {}

        def fence():
            toks = [q.now() for q in (V, A, G, TE)]
            for q in (V, A, G, TE):
                q.held += toks
            return toks

        def tt(q, o, a, b, op, w=()):
            return q.add(lambda e: e.tensor_tensor(o, a, b, op), w)

        def stt(o, a, s, b, op0, op1, w=()):
            return V.add(lambda e: e.scalar_tensor_tensor(o, a, s, b, op0, op1), w)

        def ts(q, o, a, s1, s2, op0, op1=None, w=()):
            if op1 is None:
                return q.add(lambda e: e.tensor_scalar(o, a, s1, None, op0), w)
            return q.add(lambda e: e.tensor_scalar(o, a, s1, s2, op0, op1), w)

        def cp(q, o, a, w=()):
            return q.add(lambda e: e.tensor_copy(o, a), w)

        def act(o, a, f, w=(), bias=None, scale=1.0, acc=None):
            if bias is None:
                if acc is None:
                    return A.add(lambda e: e.activation(o, a, f, scale=scale), w)
                return A.add(lambda e: e.activation(o, a, f, scale=scale, accum_out=acc), w)
            if acc is None:
                return A.add(lambda e: e.activation(o, a, f, bias=bias, scale=scale), w)
            return A.add(lambda e: e.activation(o, a, f, bias=bias, scale=scale, accum_out=acc), w)

        def recip(o, a, w=()):
            return V.add(lambda e: e.reciprocal(o, a), w)

        def scan(o, d0, d1, w=()):
            return V.add(lambda e: e.tensor_tensor_scan(o, d0, d1, 0.0, MUL, ADD), w)

        def fill(q, o, v, w=()):
            return q.add(lambda e: e.memset(o, v), w)

        def mm(o, l, r, start=True, stop=True, w=(), inc=False):
            return TE.add(lambda e: e.matmul(o, l, r, start=start, stop=stop), w, inc)

        def tr(o, i, ident, w=(), inc=False):
            return TE.add(lambda e: e.transpose(o, i, ident), w, inc)

        def dma(q, name, o, i, w=()):
            if name not in sems:
                sem(name)
            counts[name] = counts.get(name, 0) + 16
            v = counts[name]
            q.add(lambda e: e.dma_start(o, i).then_inc(sems[name], 16), w, inc=False)
            return (name, v)

        def dma_g(name, o, i, w=()):
            if name not in sems:
                sem(name)
            counts[name] = counts.get(name, 0) + 16
            v = counts[name]
            G.add(lambda e: e.dma_start(o, i).then_inc(sems[name], 16), w, inc=False)
            return (name, v)

        def dump(name, ap):
            o = nc.dram_tensor("dbg_" + name, tuple(ap.shape), F32, kind="ExternalOutput").ap()
            dma(SP, "d_dbg", o, ap, fence())

        def end():
            SP.add(lambda e: e.nop(), [(n, v) for n, v in counts.items() if n in ("d_out", "d_dbg")], inc=False)
            with nc.Block() as block:
                @block.sync
                def _(e):
                    SP.play(e, sems)

                @block.tensor
                def _(e):
                    TE.play(e, sems)

                @block.vector
                def _(e):
                    V.play(e, sems)

                @block.scalar
                def _(e):
                    A.play(e, sems)

                @block.gpsimd
                def _(e):
                    G.play(e, sems)

        base = Scope()
        PSUM = top.enter_context(nc.psum_tensor("psum", [P, 8, 512], F32))
        WRAW = [base(f"wraw{i}", [P, CS]) for i in range(NR)]
        WHI = [base(f"whi{i}", [P, CS], F32R) for i in range(NH)]
        WLO = [base(f"wlo{i}", [P, CS], F32R) for i in range(NH)]
        off, npk = offsets(COLS)
        PK = base("pk", [P, npk])
        MT = base("mats", [P, len(MATS) * P])
        MOD = base("mod", [P, 96, 2])
        GS = base("gs", [P, 3, 16])
        ident, ones, bones = (MT[:, i * P:(i + 1) * P] for i in range(3))

        def col(name, j=0, rows=P):
            return PK[0:rows, off[name] + j:off[name] + j + 1]

        bank_free = [[] for _ in range(8)]
        turn = [0]
        whole = [[0, 1, 2, 3], [4, 5, 6, 7]]
        lower = [[0, 1], [2, 3]]
        sets = [whole]

        def take(n):
            b = sets[0][turn[0]][:n]
            assert len(b) == n
            turn[0] ^= 1
            return b

        def spare(i=0):
            return sets[0][turn[0]][i]

        tk_pk = [dma(SP, "d_pk", PK[:, :], A_["pack"]), dma(SP, "d_mt", MT[:, :], A_["mats"])]

        chunks = []

        def plan(w, k0, kt, blocks):
            out = []
            for c0, n in blocks:
                ids = []
                ck = min(CS // n, 4)
                for k in range(0, kt, ck):
                    m = min(ck, kt - k)
                    ids.append((len(chunks), k, m))
                    chunks.append((A_[w][(k0 + k) * P:(k0 + k + m) * P, c0:c0 + n].rearrange("(k p) n -> p k n", p=P),
                                   m, n))
                out.append((c0, n, ids))
            return out

        def cols(a, b, step=CN):
            return [(c, min(step, b - c)) for c in range(a, b, step)]

        PL = {}
        PL["ada0"] = plan("ada_w_2", 0, 16, cols(0, 512 * NA0))
        PL["in_ssd"] = plan("w_in", 0, 16, cols(0, 2560) + [(2560, 128)])
        PL["in_rwkv"] = plan("w_in", 0, 16, cols(2576, 5648, 256) + [(5648, 224), (5840, 256)])
        PL["ada1"] = plan("ada_w_2", 0, 16, cols(512 * NA0, 512 * NA1))
        PL["ada2"] = plan("ada_w_2", 0, 16, cols(512 * NA1, 512 * NA2))
        PL["xk"] = plan("xattn_wk", 0, 16, cols(0, 2048, 256))
        PL["xv"] = plan("xattn_wv", 0, 16, cols(0, 2048))
        PL["out"] = plan("w_out", 0, 16, cols(0, 2048))
        PL["xq"] = plan("xattn_wq", 0, 16, cols(0, 2048))
        PL["xo"] = plan("xattn_wo", 0, 16, cols(0, 2048))
        for i in range(4):
            PL[f"up{i}"] = plan("ffn_w1", 0, 16, cols(2048 * i, 2048 * i + 2048))
            PL[f"dn{i}"] = plan("ffn_w2", 16 * i, 16, cols(0, 2048))
        PL["k2"] = plan("w_in_2", 0, 16, cols(1024, 2048, 256))
        PL["v2"] = plan("w_in_2", 0, 16, cols(2048, 3072))
        PL["q2"] = plan("w_in_2", 0, 16, cols(0, 1024))
        PL["fh"] = plan("w_in_2", 0, 16, cols(3072, 5120))
        PL["ada3"] = plan("ada_w_2", 0, 16, cols(512 * NA2, 12288))
        PL["out2"] = plan("w_out_2", 0, 16, cols(0, 2048))
        for i in range(4):
            PL[f"ga{i}"] = plan("ffn_w_up_2", 0, 16, cols(1408 * i, 1408 * i + 1408))
            PL[f"uu{i}"] = plan("ffn_w_up_2", 0, 16, cols(5632 + 1408 * i, 5632 + 1408 * i + 1408))
            PL[f"dd{i}"] = plan("ffn_w_down_2", 11 * i, 11, cols(0, 2048))

        loaded, hi_tok, lo_tok, used = {}, {}, {}, {}

        def view(t, i):
            _, m, n = chunks[i]
            return t[:, 0:m * n].rearrange("p (m n) -> p m n", n=n)

        def load(i):
            if i < len(chunks):
                loaded[i] = dma(SP, f"d_w{i % NR}", view(WRAW[i % NR], i), chunks[i][0], [hi_tok.get(i - NR), lo_tok.get(i - NR)])

        def split(i):
            for k in range(len(hi_tok), min(i + 4, len(chunks))):
                hi_tok[k] = act(view(WHI[k % NH], k), view(WRAW[k % NR], k), ACT.Copy, [loaded[k], used.get(k - NH)])
            for k in range(len(lo_tok), min(i + 3, len(chunks))):
                lo_tok[k] = tt(V, view(WLO[k % NH], k), view(WRAW[k % NR], k), view(WHI[k % NH], k).bitcast(F32), SUB,
                               [hi_tok[k], used.get(k - NH)])
                load(k + NR)

        for i in range(NR):
            load(i)

        side, tails = [], []

        def tail():
            if tails:
                tails.pop(0)[2]()

        def flush():
            while tails:
                tail()

        def step():
            while side:
                if next(side[0], "end") != "end":
                    return
                side.pop(0)

        part = [0.0]

        def pace(n):
            part[0] += n
            while part[0] >= 1:
                part[0] -= 1
                step()

        def both(*gens):
            live = list(gens)
            while live:
                for g in list(live):
                    if next(g, "end") == "end":
                        live.remove(g)
                yield

        def at(ready, k):
            if not isinstance(ready, dict):
                return ready
            while any(r is ready and g <= k // 4 for r, g, _ in tails):
                tail()
            return ready["g"][k // 4]

        def drain():
            while side:
                step()

        def run(gen):
            for _ in gen:
                pass

        def gemm(blocks, rhs, evac, ready, tiles=None, every=1):
            t = 0
            for c0, n, ids in blocks:
                starts = tiles(c0, n) if tiles else [(128 * j) for j in range(n // 128)]
                bs = take(len(starts) * len(rhs))
                ends = {}
                for i, k0, m in ids:
                    split(i)
                    hi, lo = view(WHI[i % NH], i), view(WLO[i % NH], i)
                    w = [hi_tok[i], lo_tok[i], at(ready, k0 + m - 1)]
                    for j, s in enumerate(starts):
                        for r, (HH, HL) in enumerate(rhs):
                            b = bs[j * len(rhs) + r]
                            for kk in range(m):
                                k = k0 + kk
                                last = k == blocks_k(ids) - 1
                                o = PSUM[:, b, 0:T]
                                if k == 0:
                                    w = w + [bank_free[b]]
                                mm(o, hi[:, kk, s:s + 128], HH[:, k, :], k == 0, False, w)
                                mm(o, hi[:, kk, s:s + 128], HL[:, k, :], False, False)
                                fin = last or (kk == m - 1 and j == len(starts) - 1 and r == len(rhs) - 1)
                                tok = mm(o, lo[:, kk, s:s + 128], HH[:, k, :], False, last, inc=fin)
                                w = []
                                if last:
                                    ends[(j, r)] = tok
                    used[i] = tok
                    tail()
                    pace(every)
                for j in range(len(starts)):
                    for r in range(len(rhs)):
                        b = bs[j * len(rhs) + r]
                        bank_free[b] = [evac(t, r, PSUM[:, b, 0:T], ends[(j, r)])]
                    t += 1

        def blocks_k(ids):
            return ids[-1][1] + ids[-1][2]

        def gemm_tok(blocks, lhs, evac, ready, every=1):
            for bi, (c0, n, ids) in enumerate(blocks):
                bs = take(len(lhs))
                ends = {}
                for i, k0, m in ids:
                    split(i)
                    hi, lo = view(WHI[i % NH], i), view(WLO[i % NH], i)
                    w = [hi_tok[i], lo_tok[i], at(ready, k0 + m - 1)]
                    for r, (HH, HL, sl) in enumerate(lhs):
                        for kk in range(m):
                            k = k0 + kk
                            last = k == blocks_k(ids) - 1
                            o = PSUM[0:sl.stop - sl.start, bs[r], 0:n]
                            if k == 0:
                                w = w + [bank_free[bs[r]]]
                            mm(o, HH[:, k, sl], hi[:, kk, 0:n], k == 0, False, w)
                            if HL is not None:
                                mm(o, HL[:, k, sl], hi[:, kk, 0:n], False, False)
                            fin = last or (kk == m - 1 and r == len(lhs) - 1)
                            tok = mm(o, HH[:, k, sl], lo[:, kk, 0:n], False, last, inc=fin)
                            w = []
                            if last:
                                ends[r] = tok
                    used[i] = tok
                    tail()
                    pace(every)
                for r in range(len(lhs)):
                    sl = lhs[r][2]
                    bank_free[bs[r]] = [evac(bi, r, PSUM[0:sl.stop - sl.start, bs[r], 0:n], ends[r])]

        def bc(ap, axis, shape):
            return ap.unsqueeze(axis).to_broadcast(shape)

        def mean_square(src, acc, w, n=16):
            a = act(acc[:, 0:4, :], src[:, 0:4, :], ACT.Square, w)
            for g in range(1, n // 4):
                s = act(acc[:, 4:8, :], src[:, 4 * g:4 * g + 4, :], ACT.Square, [a])
                a = tt(G, acc[:, 0:4, :], acc[:, 0:4, :], acc[:, 4:8, :], ADD, [s])
            return a

        def hold():
            toks = [q.now() for q in (V, A, G, TE)]
            for q in (V, A, G):
                q.held += toks

        def rstd_of(parts, n, eps, dst, w, b=None, mat=None):
            b = spare() if b is None else b
            for i, p in enumerate(parts):
                t = mm(PSUM[:, b, 0:T], ones if mat is None else mat, p, i == 0, i == len(parts) - 1,
                       [w, bank_free[b]], inc=i == len(parts) - 1)
            s = act(dst, PSUM[:, b, 0:T], ACT.Sqrt, [t], bias=col(eps), scale=1.0 / n)
            bank_free[b] = [s]
            return recip(dst, dst, [s])

        def normed(src, rstd, gain, shift, tmp, HH, HL, w, res):
            res["g"] = []

            def low(g, h):
                return tt(V, HL[:, 4 * g:4 * g + 4, :], tmp[:, (g % 2) * 4:(g % 2) * 4 + 4, :],
                          HH[:, 4 * g:4 * g + 4, :].bitcast(F32), SUB, [h])

            h = None
            for g in range(4):
                t = tmp[:, (g % 2) * 4:(g % 2) * 4 + 4, :]
                if shift is None:
                    for j in range(4):
                        a = stt(t[:, j, :], src[:, 4 * g + j, :], gain(4 * g + j), rstd, MUL, MUL, [w])
                else:
                    m = tt(V, t, src[:, 4 * g:4 * g + 4, :], bc(rstd, 1, [P, 4, T]), MUL, [w])
                if g:
                    res["g"].append([h, low(g - 1, h)])
                yield
                if shift is not None:
                    for j in range(4):
                        a = act(t[:, j, :], t[:, j, :], ACT.Identity, [m], bias=shift(4 * g + j), scale=gain(4 * g + j))
                h = act(HH[:, 4 * g:4 * g + 4, :], t, ACT.Copy, [a, w])
                yield
            res["g"].append([h, low(3, h)])
            yield

        def residual(XT, acc, sq, scale=None, nxt=None, sq2=None):
            last = {}
            for i in range(len(acc)):
                last[i] = {}
            if nxt:
                nxt[3]["g"] = [[], [], [], []]

            def squares(t, v):
                for i, (sm_, gain) in enumerate(acc):
                    u = last[i]
                    sc = 1.0 if gain is None else gain(t)
                    if t == 0:
                        u["g"] = act(sm_, XT[:, 0, :], ACT.Square, [v], scale=sc)
                    else:
                        d = (sq, sq2)[i][:, t % 2, :]
                        s = act(d, XT[:, t, :], ACT.Square, [v, u.get(t - 2)], scale=sc)
                        u["g"] = u[t] = tt(G, sm_, sm_, d, ADD, [s, u["g"]])
                last["done"] = [last[i]["g"] for i in range(len(acc))]

            def operand(t, v):
                gain, hi, lo, ready, w = nxt
                h = act(hi[:, t, :], XT[:, t, :], ACT.Copy, [v, w], scale=gain(t))
                ready["g"][t // 4] += [h, stt(lo[:, t, :], XT[:, t, :], gain(t), hi[:, t, :].bitcast(F32), MUL, SUB, [h])]

            def ev(t, r, ps, tok):
                if scale is None:
                    v = tt(V, XT[:, t, :], ps, XT[:, t, :], ADD, [tok])
                else:
                    v = stt(XT[:, t, :], ps, scale(t), XT[:, t, :], MUL, ADD, [tok])
                if nxt:
                    tails.append((nxt[3], t // 4, lambda: (squares(t, v), operand(t, v))))
                elif acc:
                    tails.append((None, 0, lambda: squares(t, v)))
                return v
            return ev, last

        ad = {}

        def ada_open(sc, n):
            S4 = sc(f"s4_{n}", [P, 16, 4], F32R)
            SI = sc(f"si_{n}", [P, 2, 16])
            ad["mo"] = sc(f"mo_{n}", [4, 2, CN])
            ad["cb"] = sc(f"comb_{n}", [4, 2])
            ad["tk"] = dma_g(f"d_cb{n}", ad["cb"][:, :], A_["comb"])
            act(SI[:, 0, :], PK[:, off["c"]:off["c"] + 16], ACT.Silu, [tk_pk])
            a = act(SI[:, 1, :], PK[:, off["c_ctx"]:off["c_ctx"] + 16], ACT.Silu)
            s4 = S4[:, :, :].rearrange("p k m -> p m k")
            a = act(s4[:, 0:2, :], SI[:, :, :], ACT.Copy)
            ad["s4"] = S4
            ad["ok"] = tt(V, s4[:, 2:4, :], SI[:, :, :], s4[:, 0:2, :].bitcast(F32), SUB, [a])

        ada_mm, ada_late = {}, []

        def ada_flush():
            while ada_late:
                n, v = ada_late.pop(0)
                b = 1 + 2 * (n % 2)
                for j in range(4):
                    t = mm(PSUM[:, b, 2 * j:2 * j + 2], ad["mo"][0:4, n % 2, 128 * j:128 * j + 128], ad["cb"][:, :],
                           w=[v, ad["tk"], bank_free[b]], inc=j == 3)
                ada_mm[n] = t
                v = tt(V, MOD[:, 4 * n:4 * n + 4, :], PSUM[:, b, 0:8].rearrange("p (n c) -> p n c", c=2),
                       bc(PK[:, off["ada_b"] + 4 * n:off["ada_b"] + 4 * n + 4], 2, [P, 4, 2]), ADD, [t])
                bank_free[b] = [v]

        def ada(name, n0, every=1):
            def ev(bi, r_, ps, tok):
                n = n0 + bi
                ada_flush()
                v = act(ad["mo"][:, n % 2, :], ps, ACT.Copy, [tok, ada_mm.get(n - 2)])
                ada_late.append((n, v))
                return v

            gemm_tok(PL[name], [(ad["s4"], None, slice(0, 4))], ev, ad["ok"], every)
            ada_flush()

        KXD = nc.dram_tensor("kx_scratch", (P, 16, T), F32).ap()
        VXD = nc.dram_tensor("vx_scratch", (P, 2, 2048), F32).ap()
        SPD = nc.dram_tensor("spec_scratch", (P, 4096), F32).ap()
        s1 = Scope()
        HH = s1("h1hi", [P, 16, T], F32R)
        HL = s1("h1lo", [P, 16, T], F32R)
        sm = Scope()
        M1 = sm("m1", [P, len(MATS1) * P + 2 * T])
        m1 = {n: M1[:, i * P:(i + 1) * P] for i, n in enumerate(MATS1)}
        rm128 = M1[:, len(MATS1) * P:len(MATS1) * P + T]
        rm64 = M1[:, len(MATS1) * P + T:len(MATS1) * P + 2 * T]
        YS = sm("ys", [P, 8, T])
        ada_open(sm, 0)
        s1c = Scope()
        X0 = s1c("x0", [P, 16, T])
        TM = s1c("tm1", [P, 8, T])
        RS = s1c("rs1", [P, T])
        tk_x0 = dma_g("d_x0", X0[:, :, :], A_["x"])
        tk_m1 = dma_g("d_m1", M1[:, :], A_["mats1"])

        def spectrum():
            SPEC = s9("spec", [P, 2, 2, 2, 512])
            DF = s9("dft0", [P, 2, 2, T])
            ZT = s9("zt", [33, T])
            W1 = s9("hw1", [33, 64])
            W2 = s9("hw2", [64, 64])
            W3 = s9("hw3", [64, 2048])
            WN = s9("win", [P, 2, 2, 512])
            HF = s9("hf", [P, 2, 2048])
            HD = s9("hd", [64, 3, T])
            tk_h1 = [dma_g("d_zt", ZT[:, :], A_["zt"]), dma_g("d_hw1", W1[:, :], A_["hy_w1"]), dma_g("d_hw2", W2[:, :], A_["hy_w2"])]
            tk_h3 = [dma_g("d_hw3", W3[:, :], A_["hy_w3"]),
                     dma_g("d_win", WN[:, :, :, :].rearrange("p a b t -> p (a b t)"), A_["win"])]
            tk_df = dma_g("d_df0", DF[:, :, :, :].rearrange("p a b t -> p (a b t)"), A_["dft"][:, 0:1024])
            yield
            d = [HD[:, i, :] for i in range(3)]
            a = tk_h1
            for wt, rhs, bias in ((W1, ZT[:, :], "hy_b1"), (W2, d[2], "hy_b2")):
                b = spare()
                t = mm(PSUM[0:64, b, 0:T], wt[:, :], rhs, w=[a, bank_free[b]], inc=True)
                v = ts(V, d[0], PSUM[0:64, b, 0:T], col(bias, rows=64), col("hy_freq", rows=64), ADD, MUL, [t])
                bank_free[b] = [v]
                ts(V, d[1], d[0], 0.15915494309189535, 12582912.0, MUL, ADD)
                ts(V, d[1], d[1], 12582912.0, None, SUB)
                stt(d[0], d[1], -6.28125, d[0], MUL, ADD)
                stt(d[0], d[1], -0.0019353071795864769, d[0], MUL, ADD)
                v = ts(V, d[0], d[0], 3.1415925, -3.1415925, MIN, MAX)
                a = act(d[2], d[0], ACT.Sin, [v])
                yield
            for n in range(4):
                for tq in range(2):
                    b = spare(2 + tq)
                    t = mm(PSUM[:, b, :], d[2][:, 128 * tq:128 * tq + 128], W3[:, 512 * n:512 * n + 512], w=[a, tk_h3, bank_free[b]], inc=True)
                    v = tt(V, HF[:, tq, 512 * n:512 * n + 512], PSUM[:, b, :], WN[:, n % 2, tq, :], MUL, [t])
                    bank_free[b] = [v]
                yield
            for o in range(2):
                f_, b_ = HF[:, :, 1024 * o:1024 * o + 512], HF[:, :, 1024 * o + 512:1024 * o + 1024]
                g = tt(G, f_, f_, b_, ADD, [v])
                h = stt(b_, b_, -2.0, f_, MUL, ADD, [g])
                yield
                for ri in range(2):
                    for f in range(2):
                        b = spare(2 + f)
                        for k in range(2):
                            t = mm(PSUM[:, b, :], DF[:, ri, k, 128 * f:128 * f + 128],
                                   HF[:, k, 1024 * o + 512 * ri:1024 * o + 512 * ri + 512],
                                   k == 0, k == 1, [h, tk_df, bank_free[b]], inc=k == 1)
                        a = act(SPEC[:, o, ri, f, :], PSUM[:, b, :], ACT.Copy, [t])
                        bank_free[b] = [a]
                    yield
            spec_tok.append(dma_g("d_spec", SPD, SPEC[:, :, :, :, :].rearrange("p a b c n -> p (a b c n)"), [a]))

        spec_tok = []
        s9 = Scope()
        ready = {}

        def first_norm():
            sq = mean_square(X0, TM, [tk_x0, tk_pk])
            yield
            r = rstd_of([TM[:, i, :] for i in range(4)], 2048, "eps6", RS[:, :], [sq, tk_pk])
            yield
            yield from normed(X0, RS[:, :], lambda j: col("norm_mix_g", j), None, TM, HH, HL, [r], ready)

        side.append(first_norm())
        side.append(spectrum())
        ada("ada0", 0)
        drain()
        s9.st.close()
        s1c.st.close()
        for q in (V, A, G, TE):
            q.held += spec_tok
        fence()

        rk = Scope("right")
        RK = rk("rk", [P, 28, T + 1])
        s1b = Scope()
        ZZ = s1b("zz", [P, 8, T])
        XB = s1b("xb", [P, 12, T + 3])
        DT = s1b("dt", [16, 4, T])
        xpad = fill(G, XB[:, :, 0:3], 0.0)
        zpad = fill(G, RK[:, :, 0:1], 0.0)

        def ev_ssd(t, r_, ps, tok):
            if t < 8:
                return act(ZZ[:, t, :], ps, ACT.Silu, [tok])
            if t < 20:
                return act(XB[:, t - 8, 3:T + 3], ps, ACT.Copy, [tok])
            return act(DT[:, 0, :], ps[0:16, :], ACT.Copy, [tok])

        gemm(PL["in_ssd"], [(HH, HL)], ev_ssd, ready)
        tk_ssd = A.now()

        def ev_rwkv(t, r_, ps, tok):
            return act(RK[:, t, 1:T + 1], ps, ACT.Copy, [tok])

        s1c = Scope()
        AC = s1c("cacc", [P, 2, T])
        SEL = s1c("sel", [16, 16 * P])
        DTT = s1c("dtt", [P, 2, 16])
        CST = s1c("cst", [P, 2, 16])
        DE = s1c("de", [P, 2, 16])
        CBM = s1c("cbm", [P, 4, P])
        E = s1c("e", [P, 16, P])
        XD = s1c("xd", [P, 2, 1024])
        BM = s1c("bm", [P, 2, P])
        ST = s1c("st", [P, 2, 512])
        YK = s1c("yk", [P, 2, 1024])
        RG = ST[:, :, 0:T]
        XE = YK[:, 1, :]
        tk_sel = dma_g("d_sel", SEL[:, :], A_["sel"])
        def ssd():
            conv = {}
            xq = XB
            for j in [8, 9, 10, 11] + list(range(8)):
                b = AC[:, j % 2, :]
                ts(V, b, xq[:, j, 3:T + 3], col("conv_w", 36 + j), None, MUL, w=[tk_ssd, xpad, conv.get(j % 2)])
                for i in (2, 1, 0):
                    v = stt(b, xq[:, j, i:i + T], col("conv_w", 12 * i + j), b, MUL, ADD)
                conv[j % 2] = xs_ok = act(xq[:, j, 3:T + 3], b, ACT.Silu, [v], bias=col("conv_b", j))
                if j == 11:
                    bc_ok = xs_ok
                if j % 2:
                    yield
            d = [DT[0:16, i, :] for i in range(4)]
            ts(V, d[0], d[0], col("dt_bias", rows=16), None, ADD)
            v = stt(d[1], d[0], -1.0, d[0], MUL, MAX)
            act(d[1], d[1], ACT.Exp, [v], scale=-1.0)
            act(d[2][:, 0:1], col("a_log", rows=16), ACT.Exp)
            a = act(d[1], d[1], ACT.Ln, bias=col("one", rows=16))
            v = stt(d[0], d[0], 0.0, d[1], MAX, ADD, [a])
            v = ts(V, d[3], d[0], d[2][:, 0:1], -1.0, MUL, MUL)
            CSR = d[1]
            v = scan(CSR, rm128[0:16, :], d[3], [tk_m1])
            yield
            for c in range(2):
                tr(PSUM[:, 4, 32 * c:32 * c + 16], d[0][:, 128 * c:128 * c + 128], ident[0:16, 0:16], [v, bank_free[4]])
                t = tr(PSUM[:, 4, 32 * c + 16:32 * c + 32], CSR[:, 128 * c:128 * c + 128], ident[0:16, 0:16], inc=True)
            v2 = PSUM[:, 4, 0:64].rearrange("p (c a h) -> p c a h", c=2, a=2)
            cp(V, DTT[:, :, :], v2[:, :, 0, :], [t])
            cst_ok = cp(V, CST[:, :, :], v2[:, :, 1, :])
            bank_free[4] = [cst_ok]
            for c in range(2):
                for g in range(2):
                    sl = slice(3 + 128 * c, 131 + 128 * c)
                    t = mm(PSUM[:, 5, (2 * c + g) * 128:(2 * c + g) * 128 + 128], XB[:, 8 + g, sl], XB[:, 10 + g, sl],
                           w=[bc_ok, bank_free[5]], inc=True)
            cb_ok = tt(V, CBM[:, :, :], PSUM[:, 5, :].rearrange("p (a l) -> p a l", l=P), bc(m1["cm"], 1, [P, 4, P]), MUL, [t, tk_m1])
            bank_free[5] = [cb_ok]
            for g in range(2):
                t = tr(PSUM[:, 6, g * 128:g * 128 + 128], XB[:, 8 + g, 3:131], ident, [bc_ok, bank_free[6]], inc=True)
            bm_ok = act(BM[:, :, :], PSUM[:, 6, 0:256].rearrange("p (g n) -> p g n", g=2), ACT.Copy, [t])
            bank_free[6] = [bm_ok]
            yield
            xd_ok = []
            for c in range(2):
                bs = [4 + 2 * c, 5 + 2 * c]
                for j in range(8):
                    t = tr(PSUM[:, bs[j // 4], (j % 4) * 128:(j % 4) * 128 + 128], XB[:, j, 3 + 128 * c:131 + 128 * c], ident,
                           [xs_ok, bank_free[bs[j // 4]]], inc=True)
                v = tt(V, XD[:, c, :].rearrange("p (h d) -> p h d", d=64),
                       PSUM[:, bs[0]:bs[0] + 2, :].rearrange("p b (h d) -> p (b h) d", d=64),
                       bc(DTT[:, c, :], 2, [P, 16, 64]), MUL, [t])
                bank_free[bs[0]] = bank_free[bs[1]] = [v]
                xd_ok.append(v)
                yield
            y_ok = []
            e_free = None
            for c in range(2):
                for h in range(16):
                    b = 4 + h // 4
                    t = mm(PSUM[:, b, (h % 4) * 128:(h % 4) * 128 + 128], SEL[:, h * P:(h + 1) * P], CSR[:, 128 * c:128 * c + 128],
                           w=[tk_sel, bank_free[b]], inc=h == 15)
                csb = PSUM[:, 4:8, :].rearrange("p b (h l) -> p (b h) l", l=P)
                if c == 0:
                    v = tt(V, DE[:, 0, :], csb[:, :, 127], CST[:, 0, :], SUB, [t])
                    de_ok = act(DE[:, 0, :], DE[:, 0, :], ACT.Exp, [v])
                    de_ok = act(DE[:, 1, :], CST[:, 1, :], ACT.Exp, [cst_ok])
                v = tt(V, E[:, :, :], csb, bc(CST[:, c, :], 2, [P, 16, P]), SUB, [t, e_free])
                for b in range(4, 8):
                    bank_free[b] = [v]
                v = ts(V, E[:, :, :], E[:, :, :], 0.0, None, MIN)
                a = act(E[:, :, :], E[:, :, :], ACT.Exp, [v])
                yield
                for g in range(2):
                    em_ok = tt(V, E[:, 8 * g:8 * g + 8, :], E[:, 8 * g:8 * g + 8, :],
                               bc(CBM[:, 2 * c + g, :], 1, [P, 8, P]), MUL, [a, cb_ok])
                if c == 0:
                    x_ = tt(V, XE.rearrange("p (h d) -> p h d", d=64), XD[:, 0, :].rearrange("p (h d) -> p h d", d=64),
                            bc(DE[:, 0, :], 2, [P, 16, 64]), MUL, [de_ok])
                    yield
                    for g in range(2):
                        t = mm(PSUM[:, 4 + g, :], BM[:, g, :], XE[:, g * 512:g * 512 + 512], w=[x_, bm_ok, bank_free[4 + g]], inc=True)
                        st_ok = act(ST[:, g, :], PSUM[:, 4 + g, :], ACT.Copy, [t])
                        bank_free[4 + g] = [st_ok]
                yield
                for h in range(16):
                    b = 6 + h // 8
                    t = mm(PSUM[:, b, (h % 8) * 64:(h % 8) * 64 + 64], E[:, h, :], XD[:, c, h * 64:h * 64 + 64],
                           w=[em_ok, xd_ok[c], bank_free[b]], inc=h == 15)
                e_free = t
                yd = PSUM[:, 6:8, :].rearrange("p b n -> p (b n)")
                if c == 0:
                    y = act(YK[:, 0, :], yd, ACT.Copy, [t])
                else:
                    for g in range(2):
                        t2 = mm(PSUM[:, 4 + g, :], XB[:, 10 + g, 131:259], ST[:, g, :], w=[st_ok, bank_free[4 + g]], inc=True)
                    v = tt(V, YK[:, 1, :].rearrange("p (h d) -> p h d", d=64),
                           PSUM[:, 4:6, :].rearrange("p b (h d) -> p (b h) d", d=64), bc(DE[:, 1, :], 2, [P, 16, 64]), MUL, [t2, de_ok])
                    bank_free[4] = bank_free[5] = [v]
                    y = tt(V, YK[:, 1, :], YK[:, 1, :], yd, ADD, [t])
                bank_free[6] = bank_free[7] = [y]
                y_ok.append(y)
                yield
            for b in range(4, 8):
                for j in (2 * b - 8, 2 * b - 7):
                    for c in range(2):
                        t = tr(PSUM[:, b, (j % 2) * T + 128 * c:(j % 2) * T + 128 * c + 128], YK[:, c, 128 * j:128 * j + 128],
                               ident, [y_ok, bank_free[b]], inc=True)
                for j in (2 * b - 8, 2 * b - 7):
                    v = stt(YS[:, j, :], XB[:, j, 3:T + 3], col("ssd_d", j), PSUM[:, b, (j % 2) * T:(j % 2) * T + T], MUL, ADD, [t])
                bank_free[b] = [v]
            yield
            v = tt(V, YS[:, :, :], YS[:, :, :], ZZ[:, :, :], MUL)
            for g in range(2):
                a = act(ZZ[:, 4 * g:4 * g + 4, :], YS[:, 4 * g:4 * g + 4, :], ACT.Square, [v])
                yield
                r = rstd_of([ZZ[:, 4 * g + i, :] for i in range(4)], 512, "eps6", RG[:, g, :], [a], b=4 + g)
                for j in range(4 * g, 4 * g + 4):
                    stt(YS[:, j, :], YS[:, j, :], col("ssd_g", j), RG[:, g, :], MUL, MUL)
                yield

        sets[0] = lower
        side.append(ssd())
        gemm(PL["in_rwkv"], [(HH, HL)], ev_rwkv, ready, tiles=lambda c0, n: [0, 96] if n == 224 else [0, 128])
        drain()
        h_done = TE.now()
        s1c.close()
        s1b.close()
        if stop == 1:
            dump("ys", YS[:, :, :])
            dump("rk", RK[:, :, :])
            return end()
        s1c = Scope()
        X0 = s1c("mem0", [P, 16, T])
        TM = s1c("tm2", [P, 8, T])
        RS = s1c("rs2", [P, T])
        tk_mem = dma_g("d_mem", X0[:, :, :], A_["mem"])
        m_ok = {}

        def mem_norm():
            sq = mean_square(X0, TM, [tk_mem])
            yield
            r = rstd_of([TM[:, i, :] for i in range(4)], 2048, "eps6", RS[:, :], [sq], b=7)
            yield
            yield from normed(X0, RS[:, :], lambda j: col("norm_mem_g", j), None, TM, HH, HL, [r, h_done], m_ok)

        side.append(mem_norm())
        ada("ada1", NA0)
        drain()
        s1c.close()

        s2 = Scope()
        LD, C, IC, KK, RT = (s2(n, [P, 4, T]) for n in ("rld", "rc", "ric", "rkk", "rrt"))
        VT, BT, KT = (s2(n, [P, 512]) for n in ("rvt", "rbt", "rkt"))
        LA, MB, MK, XT_ = (s2(n, [P, 8, P]) for n in ("rla", "rmb", "rmk", "rxt"))
        US, SS = (s2(n, [P, 512]) for n in ("rus", "rss"))
        S = s2("rs", [P, 4, P])
        TW = s2("rtw", [96, T])
        PCE = s2("rpce", [P, 4, 4])
        OK = s2("romka", [P, 8])
        X4 = s2("rx4", [P, 4, 512])
        STG = s2("stage", [P, 2, 512])

        def UU(a, b):
            return RK[:, a:b, 1:T + 1]

        def U(j):
            return RK[:, j, 1:T + 1]

        def two(b):
            return PSUM[:, b:b + 2, :].rearrange("p b (j t) -> p (b j) t", t=T)

        def free(v, *bs):
            for b in bs:
                bank_free[b] = [v]

        def slot(h):
            return 4 * (h % 2) + h // 2

        def rwkv():
            om = ts(V, OK[:, :], PK[:, off["k_a"]:off["k_a"] + 8], -1.0, 1.0, MUL, ADD)
            ring = [t[:, :].rearrange("p (a t) -> p a t", t=T) for t in (US, SS, VT)]
            rfree = {}
            for n, g in enumerate([12, 13] + list(range(12))):
                d = ring[n % 3]
                g_ = tt(G, d, RK[:, 2 * g:2 * g + 2, 0:T], UU(2 * g, 2 * g + 2), SUB, [zpad, rfree.get(n % 3)])
                for j in range(2):
                    v = stt(U(2 * g + j), d[:, j, :], col("mu", 2 * g + j), U(2 * g + j), MUL, ADD, [g_])
                rfree[n % 3] = v
                if n == 1:
                    a = act(TW[:, :], RK[0:96, 24, 1:T + 1], ACT.Tanh, [v])
                    pg_ok = act(UU(26, 28), UU(26, 28), ACT.Sigmoid)
                if n % 3 == 2:
                    yield
            sh_ok, tw_ok = v, a
            for hf in range(2):
                yield from half(hf, sh_ok, tw_ok, om)

        def half(hf, sh_ok, tw_ok, om):
            hold()
            c0, p0 = 512 * hf, 4 * hf
            rr, kq, vv = UU(p0, p0 + 4), UU(8 + p0, 12 + p0), UU(16 + p0, 20 + p0)
            tk_w2 = dma_g("d_rw2", BT[0:96, :], A_["rw2"][:, c0:c0 + 512])
            tk_a2 = dma_g("d_ra2", KT[0:96, :], A_["ra2"][:, c0:c0 + 512])
            s0 = fill(G, S[:, :, :], 0.0)
            yield
            for j in range(4):
                t = mm(two(4)[:, j, :], BT[0:96, 128 * j:128 * j + 128], TW[:, :], w=[tw_ok, tk_w2, bank_free[4 + j // 2]], inc=True)
            for j in range(4):
                t2 = mm(two(6)[:, j, :], KT[0:96, 128 * j:128 * j + 128], RK[0:96, 25, 1:T + 1],
                        w=[tk_a2, sh_ok, bank_free[6 + j // 2]], inc=True)
            for j in range(4):
                ld_ok = act(LD[:, j, :], two(4)[:, j, :], ACT.Sigmoid, [t], bias=col("w0", p0 + j))
            free(ld_ok, 4, 5)
            for j in range(4):
                ic_ok = act(IC[:, j, :], two(6)[:, j, :], ACT.Sigmoid, [t2], bias=col("a0", p0 + j))
            free(ic_ok, 6, 7)
            yield
            SQ, RN, KM = (t[:, :, :].rearrange("p a b -> p (a b)").rearrange("p (j t) -> p j t", t=T) for t in (LA, MB, MK))
            for j in range(4):
                a = act(KK[:, j, :], U(8 + p0 + j), ACT.Copy, [sh_ok], scale=col("k_k", p0 + j))
            a = act(SQ, KK[:, :, :], ACT.Square)
            ts(V, LD[:, :, :], LD[:, :, :], -0.6065306597126334, None, MUL, w=[ld_ok])
            for j in range(4):
                scan(C[:, j, :], rm64, LD[:, j, :])
            v = tt(V, LD[:, :, :], C[:, :, :], LD[:, :, :], SUB)
            for j in range(4):
                km = act(KM[:, j, :], IC[:, j, :], ACT.Identity, [om], scale=col("k_a", p0 + j), bias=OK[:, p0 + j:p0 + j + 1])
            yield
            for j in range(4):
                t = mm(two(4)[:, j, :], bones, SQ[:, j, :], w=[a, bank_free[4 + j // 2]], inc=True)
            a_ld = act(LD[:, :, :], LD[:, :, :], ACT.Exp, [v])
            a_rt = act(RT[:, :, :], C[:, :, :], ACT.Exp)
            a_c = act(C[:, :, :], C[:, :, :], ACT.Exp, scale=-1.0)
            rn = act(RN, two(4), ACT.Sqrt, [t])
            free(rn, 4, 5)
            km_ok = tt(V, kq, kq, KM, MUL, [km])
            cp(V, PCE[:, :, :], RT[:, :, 63::64], [a_rt])
            r_ok = tt(V, RT[:, :, :], RT[:, :, :], rr, MUL)
            g_rk = tt(G, rr, rr, kq, MUL, [r_ok, km_ok])
            yield
            ts(V, RN, RN, 1e-12, None, MAX, w=[rn])
            recip(RN, RN)
            kk_ok = tt(V, KK[:, :, :], KK[:, :, :], RN, MUL)
            al_ok = stt(LD[:, :, :], LD[:, :, :], -1.0, KK[:, :, :], MUL, MUL, [a_ld])
            g_ic = tt(G, IC[:, :, :], IC[:, :, :], KK[:, :, :], MUL, [kk_ok, km])
            for j in range(4):
                a = act(U(p0 + j), U(p0 + j), ACT.Copy, [g_rk], scale=col("r_k", p0 + j))
            yield
            b_ok = tt(V, IC[:, :, :], IC[:, :, :], C[:, :, :], MUL, [g_ic, a_c])
            kt_ok = tt(V, C[:, :, :], C[:, :, :], kq, MUL)
            for j in range(4):
                t = mm(two(6)[:, j, :], bones, U(p0 + j), w=[a, bank_free[6 + j // 2]], inc=True)
            bo_ok = tt(V, rr, two(6), vv, MUL, [t])
            free(bo_ok, 6, 7)
            in_ok = [al_ok, r_ok, b_ok, kt_ok, bo_ok]
            yield
            tmp4 = [[t[:, :].rearrange("p (h t) -> p h t", t=P) for t in (KK[:, 0:2, :].rearrange("p a t -> p (a t)"),
                                                                           KK[:, 2:4, :].rearrange("p a t -> p (a t)"),
                                                                           X4[:, 0, :], X4[:, 1, :])],
                    [RK[:, 8 + p0:12 + p0, :].rearrange("p a t -> p (a t)")[:, 512 * i:512 * i + 512].rearrange("p (h t) -> p h t", t=P)
                     for i in range(2)] + [X4[:, i, :].rearrange("p (h t) -> p h t", t=P) for i in (2, 3)]]
            seq_ok, s_ok = None, [s0]
            for tq in range(2):
                tsl = slice(128 * tq, 128 * tq + 128)
                toks = []
                for i, (src, dst) in enumerate(((vv, VT), (IC, BT), (C, KT))):
                    for j in range(4):
                        t = tr(PSUM[:, 4 + i, j * 128:j * 128 + 128], src[:, j, tsl], ident, [in_ok, bank_free[4 + i]], inc=True)
                    a = act(dst[:, :], PSUM[:, 4 + i, :], ACT.Copy, [t, seq_ok])
                    free(a, 4 + i)
                    toks.append(a)
                yield
                done = []

                def chain(ch):
                    LT, X, Z, ML = tmp4[ch]
                    hs = slice(4 * ch, 4 * ch + 4)
                    XT = XT_[:, hs, :]
                    b0, b1 = 4 + 2 * ch, 5 + 2 * ch

                    def view4(b):
                        return PSUM[:, b, :].rearrange("p (h t) -> p h t", t=P)

                    def four(b, lsrc, rsrc):
                        for i in range(4):
                            p = slice(64 * ch, 64 * ch + 64)
                            t = mm(PSUM[:, b, 128 * i:128 * i + 128], lsrc[p, i, tsl], rsrc[p, i, tsl],
                                   w=[in_ok, bank_free[b]], inc=i == 3)
                        return t

                    def m4(n):
                        return bc(m1[n], 1, [P, 4, P])

                    t = four(b0, IC, LD)
                    lt_ok = act(LT, view4(b0), ACT.Copy, [t])
                    free(lt_ok, b0)
                    t = four(b1, LD, IC)
                    v = tt(V, X, view4(b1), m4("l1"), MUL, [t])
                    free(v, b1)
                    eye = bc(ident, 1, [P, 4, P])
                    x_ok = tt(V, X, X, eye, ADD)
                    ml = tt(G, ML, LT, m4("t2"), MUL, [lt_ok])
                    yield
                    tt(V, XT, LT, m4("t1"), MUL, [lt_ok, seq_ok])
                    xt_ok = tt(V, XT, XT, eye, ADD)
                    rest = [(C, LD, LA, "strict"), (IC, RT, MB, "incl"), (C, RT, MK, "incl")]
                    for s in (2, 4, 8, 16, 32):
                        for i in range(4):
                            t = mm(PSUM[:, b0, 128 * i:128 * i + 128], ML[:, i, :], X[:, i, :], w=[ml, x_ok, bank_free[b0]], inc=i == 3)
                        lv = t
                        z = act(Z, view4(b0), ACT.Copy, [t, xt_ok, x_ok])
                        free(z, b0)
                        if rest:
                            ls, rs_, dst, msk = rest.pop(0)
                            t = four(b1, ls, rs_)
                            v = tt(V, dst[:, hs, :], view4(b1), m4(msk), MUL, [t, seq_ok])
                            free(v, b1)
                            done.append(v)
                        yield
                        for i in range(4):
                            t = mm(PSUM[:, b0, 128 * i:128 * i + 128], Z[:, i, :], XT[:, i, :], w=[z, xt_ok, bank_free[b0]], inc=i == 3)
                        if s < 32:
                            for i in range(4):
                                t = mm(PSUM[:, b1, 128 * i:128 * i + 128], XT[:, i, :], Z[:, i, :], w=[bank_free[b1]], inc=i == 3)
                        xt_ok = tt(V, XT, XT, view4(b0), ADD, [t])
                        free(xt_ok, b0)
                        if s < 32:
                            x_ok = tt(V, X, X, view4(b1), ADD)
                            free(x_ok, b1)
                            ml = tt(G, ML, LT, m4(f"t{2 * s}"), MUL, [lv])
                        yield
                    done.append(xt_ok)

                yield from both(chain(0), chain(1))
                for cl in range(2):
                    R = slice(64 * cl, 64 * cl + 64)
                    for j in range(4):
                        o = j * 128
                        mm(PSUM[:, 4, o:o + 128], LD[:, j, tsl], S[:, j, :], True, False, [done, toks, s_ok, bank_free[4]])
                        for q in range(2):
                            h = 2 * j + q
                            t = mm(PSUM[:, 4, o + 64 * q:o + 64 * q + 64], LA[R, slot(h), :], VT[R, 64 * h:64 * h + 64], False, q == 1, inc=True)
                    u_ok = act(US[R, :], PSUM[R, 4, :], ACT.Copy, [t, seq_ok])
                    free(u_ok, 4)
                    yield
                    for h in range(8):
                        t = mm(PSUM[:, 5, h * 64:h * 64 + 64], XT_[R, slot(h), :], US[R, 64 * h:64 * h + 64], w=[u_ok, bank_free[5]], inc=True)
                    sa_ok = act(SS[R, :], PSUM[R, 5, :], ACT.Copy, [t])
                    free(sa_ok, 5)
                    yield
                    for j in range(4):
                        js = slice(128 * j, 128 * j + 128)
                        mm(PSUM[:, 7, js], BT[R, js], SS[R, js], True, False, [sa_ok, bank_free[7]])
                        mm(PSUM[:, 7, js], KT[R, js], VT[R, js], False, True, inc=True)
                    for j in range(4):
                        o = j * 128
                        mm(PSUM[:, 6, o:o + 128], RT[:, j, tsl], S[:, j, :], True, False, [bank_free[6]])
                        for q in range(2):
                            h = 2 * j + q
                            hc = slice(64 * h, 64 * h + 64)
                            mm(PSUM[:, 6, o + 64 * q:o + 64 * q + 64], MB[R, slot(h), :], SS[R, hc], False, False)
                            t = mm(PSUM[:, 6, o + 64 * q:o + 64 * q + 64], MK[R, slot(h), :], VT[R, hc], False, q == 1, inc=True)
                    sp = PSUM[:, 7, :].rearrange("p (j n) -> p j n", n=P)
                    for q in range(2):
                        p = slice(64 * q, 64 * q + 64)
                        tt(V, S[p, :, p], S[p, :, p], sp[p, :, p], ADD, [t])
                        v = tt(V, S[p, :, p], S[p, :, p], bc(PCE[p, :, 2 * tq + cl], 2, [64, 4, 64]), MUL)
                    s_ok = [v]
                    free(v, 7)
                    y_ok = act(US[R, :], PSUM[R, 6, :], ACT.Copy, [t])
                    free(y_ok, 6)
                    yield
                for j in range(4):
                    t = tr(PSUM[:, 4, j * 128:j * 128 + 128], US[:, 128 * j:128 * j + 128], ident, [y_ok, bank_free[4]], inc=True)
                a = act(LD[:, :, tsl], PSUM[:, 4, :].rearrange("p (j n) -> p j n", n=P), ACT.Copy, [t])
                free(a, 4)
                seq_ok = t
            G2 = C[:, :, :].rearrange("p a t -> p (a t)").rearrange("p (k n) -> p k n", k=2)
            tk_g2 = dma_g("d_rg2", G2, A_["rg2"].rearrange("(k p) n -> p k n", p=P)[:, :, c0:c0 + 512], [seq_ok])
            yield
            for j in range(4):
                t = mm(two(4)[:, j, :], bones, LD[:, j, :], w=[a, bank_free[4 + j // 2]], inc=True)
            v = stt(LD[:, :, :], two(4), -1.0 / 64, LD[:, :, :], MUL, ADD, [t])
            free(v, 4, 5)
            a = act(KK[:, :, :], LD[:, :, :], ACT.Square, [v])
            yield
            for j in range(4):
                t = mm(two(6)[:, j, :], bones, KK[:, j, :], w=[a, bank_free[6 + j // 2]], inc=True)
            a = act(IC[:, :, :], two(6), ACT.Sqrt, [t], bias=col("eps64"), scale=1.0 / 64)
            free(a, 6, 7)
            recip(IC[:, :, :], IC[:, :, :], [a])
            v = tt(V, LD[:, :, :], LD[:, :, :], IC[:, :, :], MUL)
            for j in range(4):
                a = act(LD[:, j, :], LD[:, j, :], ACT.Identity, [v], scale=col("ln_w", p0 + j), bias=col("ln_b", p0 + j))
            yield
            for j in range(4):
                for k in range(2):
                    t = mm(two(4)[:, j, :], G2[:, k, 128 * j:128 * j + 128], U(26 + k), k == 0, k == 1,
                           w=[tk_g2, bank_free[4 + j // 2]], inc=True)
            tt(V, rr, rr, LD[:, :, :], ADD, [a])
            v = tt(V, rr, rr, two(4), MUL, [t])
            free(v, 4, 5)
            yr_ok.append(v)
            yield

        yr_ok, stg, scr = [], {}, []

        def ev_kx(t, r_, ps, tok):
            s = STG[:, t % 2, 0:T]
            a = act(s, ps, ACT.Copy, [tok, stg.get(t % 2)])
            stg[t % 2] = dma(A, f"d_stg{t % 2}", KXD[:, t, :], s, [a])
            return a

        def ev_vx(bi, r_, ps, tok):
            s = STG[:, r_, :]
            a = act(s, ps, ACT.Copy, [tok, stg.get(r_)])
            stg[r_] = dma(A, f"d_stg{r_}", VXD[:, r_, 512 * bi:512 * bi + 512], s, [a])
            return a

        side.append(rwkv())
        ada("ada2", NA1, 1.5)
        gemm(PL["xk"], [(HH, HL)], ev_kx, m_ok, every=1.5)
        gemm_tok(PL["xv"], [(HH, HL, slice(0, 128)), (HH, HL, slice(128, 256))], ev_vx, m_ok, every=1.5)
        m_done = TE.now()
        drain()
        if stop == 3:
            dump("ys", YS[:, :, :])
            dump("yr", UU(0, 8))
            SP.held += [stg[0], stg[1], *spec_tok]
            return end()
        mix_ok = {"g": []}
        for g in range(4):
            src = YS[:, 4 * g:4 * g + 4, :] if g < 2 else UU(4 * g - 8, 4 * g - 4)
            h = act(HH[:, 4 * g:4 * g + 4, :], src, ACT.Copy, [m_done, yr_ok])
            mix_ok["g"].append([h, tt(V, HL[:, 4 * g:4 * g + 4, :], src, HH[:, 4 * g:4 * g + 4, :].bitcast(F32), SUB, [h])])
        for q in (V, A, G, TE):
            q.held += [stg[0], stg[1]]
        s2.close()
        sm.close()
        rk.close()
        sets[0] = whole
        XT = Scope("right")("xt", [P, 16, T])
        r0 = Scope("right")
        GH = r0("ghi", [P, 16, T], F32R)
        GL = r0("glo", [P, 16, T], F32R)
        tk_x = dma_g("d_x1", XT[:, :, :], A_["x"])

        s4 = Scope()
        TM = s4("tm4", [P, 8, T])
        ACC = s4("acc4", [P, T])
        AC2 = s4("acc4b", [P, T])
        SQ2 = s4("sq4", [P, 2, T])
        RS = s4("rs4", [P, 2, T])
        SM = s4("sm4", [P, 8, 4])
        s5 = Scope()
        KX = s5("kx", [P, 16, T])
        VX = s5("vx", [P, 2, 2048])
        QT = s5("qt", [P, 16, T])
        kx_ok = dma_g("d_kx", KX[:, :, :], KXD, [stg[0], stg[1]])
        vx_ok = dma_g("d_vx", VX[:, :, :], VXD)

        def factor(last):
            def go():
                rs_ok[0] = rstd_of([ACC[:, :]], 2048, "eps6", RS[:, 0, :], [last["done"]])
            rs_ok[0] = None
            tails.append((None, 0, go))

        rs_ok = [None]
        h_ok = {}
        ev, last = residual(XT, [(ACC[:, :], None)], SQ2, nxt=(lambda t: col("norm_x_g", t), GH, GL, h_ok, None))
        V.held.append(tk_x)
        gemm(PL["out"], [(HH, HL)], ev, mix_ok)
        out_done = TE.now()
        if stop == 4:
            flush()
            dump("x1", XT[:, :, :])
            return end()
        factor(last)

        def ev_copy(dst):
            return lambda t, r_, ps, tok: act(dst(t, r_), ps, ACT.Copy, [tok])

        q_tok = {}
        o_ok = []
        XSC = 512.0 ** -0.5
        PT = TM[:, 4:8, :].rearrange("p (a m) t -> p a m t", a=2)

        pt_free = {}

        def xattn():
            for hd in range(4):
                while 4 * hd + 3 not in q_tok:
                    yield
                yield from xhead(hd)

        def xhead(hd):
            for st in range(2):
                u = 2 * hd + st
                b = spare()
                for k in range(4):
                    t = mm(PSUM[:, b, 0:T], QT[:, 4 * hd + k, 128 * st:128 * st + 128], KX[:, 4 * hd + k, :], k == 0, k == 3,
                           [q_tok[4 * hd + 3], kx_ok, bank_free[b]], inc=k == 3)
                ps = PSUM[:, b, 0:T]
                s = SM[:, u % 8, :]
                V.add(lambda e, s=s, ps=ps: e.reduce_max(s[:, 0:1], ps, AX_X), [t])
                v = ts(V, s[:, 1:2], s[:, 0:1], -XSC, None, MUL)
                p = TM[:, u % 4, :]
                a = act(p, ps, ACT.Exp, [v, pt_free.get(("p", u % 4))], bias=s[:, 1:2], scale=XSC, acc=s[:, 2:3])
                bank_free[b] = [a]
                recip(s[:, 3:4], s[:, 2:3], [a])
                v = ts(V, p, p, s[:, 3:4], None, MUL)
                yield
                b = spare(1)
                for m in range(2):
                    t = tr(PSUM[:, b, 128 * m:128 * m + 128], p[:, 128 * m:128 * m + 128], ident, [v, bank_free[b]], inc=m == 1)
                pt_free[("p", u % 4)] = t
                a = act(PT[:, hd % 2, :, 128 * st:128 * st + 128], PSUM[:, b, 0:256].rearrange("p (m s) -> p m s", m=2),
                        ACT.Copy, [t, pt_free.get(hd % 2)])
                bank_free[b] = [a]
                yield
            for d in range(4):
                b = spare(2 + d % 2)
                dt = 4 * hd + d
                for m in range(2):
                    t = mm(PSUM[:, b, 0:T], VX[:, m, 128 * dt:128 * dt + 128], PT[:, hd % 2, m, :], m == 0, m == 1,
                           [a, vx_ok, bank_free[b]], inc=m == 1)
                pt_free[hd % 2] = t
                h = act(HH[:, dt, :], PSUM[:, b, 0:T], ACT.Copy, [t, out_done])
                v = tt(V, HL[:, dt, :], PSUM[:, b, 0:T], HH[:, dt, :].bitcast(F32), SUB, [h])
                bank_free[b] = [v]
                o_ok[:] = [h, v]
                yield

        def ev_q(t, r_, ps, tok):
            assert rs_ok[0]
            q_tok[t] = tt(V, QT[:, t, :], ps, RS[:, 0, :], MUL, [tok, rs_ok[0]])
            return q_tok[t]

        side.append(xattn())
        gemm(PL["xq"], [(GH, GL)], ev_q, h_ok)
        drain()
        q_done = TE.now()
        h_ok = {}
        ev, last = residual(XT, [(ACC[:, :], None)], SQ2, nxt=(lambda t: col("norm_ffn_g", t), GH, GL, h_ok, q_done))
        gemm(PL["xo"], [(HH, HL)], ev, o_ok)
        xo_done = TE.now()
        factor(last)
        s5.close()
        if stop == 5:
            flush()
            dump("x2", XT[:, :, :])
            return end()

        r1 = Scope("right")
        CH = r1("chi", [P, 16, T], F32R)
        CL = r1("clo", [P, 16, T], F32R)
        s5 = Scope()
        CX = s5("cx", [P, 16, T])
        RB = s5("rb", [P, 4, T])
        TM5 = TM
        tk_cx = dma_g("d_cx", CX[:, :, :], A_["ctx"])
        hid = {}

        def mod_gain(i, g, m, c):
            return stt(GS[:, i, :], MOD[:, m:m + 16, c], 1.0, PK[:, off[g]:off[g] + 16], ADD, MUL)

        def ctx_norm():
            sq = mean_square(CX, TM5, [tk_cx])
            mod_gain(0, "norm1_g", 16, 1)
            mod_gain(1, "norm1_g", 16, 0)
            v = tt(V, GS[:, 1, :], GS[:, 1, :], PK[:, off["final_g"]:off["final_g"] + 16], MUL)
            yield
            r = rstd_of([TM5[:, i, :] for i in range(4)], 2048, "eps6", RS[:, 1, :], [sq])
            yield
            yield from normed(CX, RS[:, 1, :], lambda j: GS[:, 0, j:j + 1], lambda j: MOD[:, j, 1:2], TM5, CH, CL,
                              [r, v], c_ok)

        c_ok = {}
        side.append(ctx_norm())
        dn_done = xo_done
        for i in range(4):
            f_ok = {"g": [[], [], [], []]}

            def ev_up(t, r_, ps, tok):
                if t % 4 == 0:
                    flush()
                assert rs_ok[0]
                q = RB[:, t % 4, :]
                v = stt(q, ps, 0.0, RS[:, 0, :], MAX, MUL, [tok, rs_ok[0], hid.get(t % 4)])

                def rest():
                    a = act(q, q, ACT.Square, [v])
                    h = act(HH[:, t, :], q, ACT.Copy, [a, dn_done])
                    hid[t % 4] = tt(V, HL[:, t, :], q, HH[:, t, :].bitcast(F32), SUB, [h])
                    f_ok["g"][t // 4] += [h, hid[t % 4]]
                tails.append((f_ok, t // 4, rest))
                return v

            gemm(PL[f"up{i}"], [(GH, GL)], ev_up, h_ok)
            acc = [(ACC[:, :], None), (AC2[:, :], lambda t: col("final_g", t))] if i == 3 else []
            ev, last = residual(XT, acc, SQ2, sq2=TM)
            gemm(PL[f"dn{i}"], [(HH, HL)], ev, f_ok)
            dn_done = TE.now()
        drain()
        flush()
        up_done = TE.now()
        if stop == 6:
            dump("x3", XT[:, :, :])
            return end()
        rx, xa, xb = RS[:, 0, :], RB[:, 0, :], RB[:, 1, :]
        b2 = spare(1)
        r = rstd_of([ACC[:, :]], 2048, "eps6", rx, [last["done"]])
        t = mm(PSUM[:, b2, 0:T], ones, AC2[:, :], w=[bank_free[b2]], inc=True)
        tt(V, xa, rx, rx, MUL, [r])
        v = tt(V, xa, xa, PSUM[:, b2, 0:T], MUL, [t])
        bank_free[b2] = [v]
        a = act(xb, xa, ACT.Sqrt, [v], bias=col("eps6"), scale=1.0 / 2048)
        recip(xb, xb, [a])
        r = tt(V, RS[:, 1, :], xb, rx, MUL)
        h_ok = {}
        run(normed(XT, RS[:, 1, :], lambda j: GS[:, 1, j:j + 1], lambda j: MOD[:, j, 0:1], TM5, GH, GL, [r, up_done], h_ok))
        for j in range(16):
            v = stt(XT[:, j, :], XT[:, j, :], col("final_g", j), rx, MUL, MUL)
        s5.close()
        s4.close()
        s1.close()


        s6 = Scope()
        Y2 = s6("y2", [P, 16, T])
        SM = s6("sm6", [P, 8, 4])
        FT = s6("ft", [P, 4, T])
        HY = s6("hy", [P, 12, T + 2])
        s6c = Scope()
        K2 = s6c("k2", [P, 8, 512])
        V2 = s6c("v2", [P, 4, 1024])
        hpad = fill(G, HY[:, :, 0:1], 0.0)
        hpad = fill(G, HY[:, :, T + 1:T + 2], 0.0)
        gemm(PL["k2"], [(GH, GL), (CH, CL)], ev_copy(lambda t, r_: K2[:, t, T * r_:T * r_ + T]), [h_ok, c_ok])
        k2_ok = A.now()
        gemm_tok(PL["v2"], [(GH, GL, slice(0, 128)), (GH, GL, slice(128, 256)), (CH, CL, slice(0, 128)), (CH, CL, slice(128, 256))],
                 ev_copy(lambda b, r_: V2[:, r_, 512 * b:512 * b + 512]), [h_ok, c_ok])
        v2_ok = A.now()
        r1.close()
        s7 = Scope()
        QT2 = s7("q2", [P, 8, T])
        BI = s7("bi", [P, 2, 2, T])
        MS = s7("ms", [P, 2, T])
        PP = s7("pp", [P, 2, 512])
        PT2 = s7("pt2", [P, 2, 4, T])
        tk_ms = dma_g("d_ms", MS[:, :, :].rearrange("p a t -> p (a t)"), A_["namask"])
        NSC = 128.0 ** -0.5
        q2_tok, bi_free, pp_free, pt2_free, a_tok = {}, {}, {}, {}, {}

        def na(h):
            tk = dma_g(f"d_bi{h % 2}", BI[:, h % 2, :, :], A_["bias"][h].rearrange("(a p) t -> p a t", p=P), [bi_free.get(h % 2)])
            bi = tt(G, BI[:, h % 2, :, :], BI[:, h % 2, :, :], MS[:, :, :], ADD, [tk, tk_ms])
            yield
            for qt in range(2):
                u = 2 * h + qt
                b = spare()
                t = mm(PSUM[:, b, :], QT2[:, h, 128 * qt:128 * qt + 128], K2[:, h, :], w=[q2_tok[h], k2_ok, bank_free[b]], inc=True)
                p = PP[:, u % 2, :]
                c_ = ts(V, p[:, T:512], PSUM[:, b, T:512], NSC, None, MUL, w=[t, pp_free.get(u % 2)])
                v = stt(p[:, 0:T], PSUM[:, b, 0:T], NSC, BI[:, h % 2, qt, :], MUL, ADD, [bi])
                bank_free[b] = [v]
                bi_free[h % 2] = v
                s = SM[:, u % 8, :]
                V.add(lambda e, s=s, p=p: e.reduce_max(s[:, 0:1], p, AX_X))
                v = ts(V, s[:, 1:2], s[:, 0:1], -1.0, None, MUL)
                a = act(p, p, ACT.Exp, [v], bias=s[:, 1:2], acc=s[:, 2:3])
                recip(s[:, 3:4], s[:, 2:3], [a])
                v = ts(V, p, p, s[:, 3:4], None, MUL)
                yield
                b = spare(1)
                for k in range(4):
                    t = tr(PSUM[:, b, 128 * k:128 * k + 128], p[:, 128 * k:128 * k + 128], ident, [v, bank_free[b]], inc=k == 3)
                pp_free[u % 2] = t
                a = act(PT2[:, h % 2, :, 128 * qt:128 * qt + 128], PSUM[:, b, :].rearrange("p (k s) -> p k s", k=4),
                        ACT.Copy, [t, pt2_free.get(h % 2)])
                bank_free[b] = [a]
                yield
            b = spare(2)
            for k in range(4):
                t = mm(PSUM[:, b, 0:T], V2[:, k, 128 * h:128 * h + 128], PT2[:, h % 2, k, :], k == 0, k == 3,
                       [a, v2_ok, bank_free[b]], inc=k == 3)
            pt2_free[h % 2] = t
            a_tok[h] = act(Y2[:, h, :], PSUM[:, b, 0:T], ACT.Copy, [t])
            bank_free[b] = [a_tok[h]]
            yield

        def ev_q2(t, r_, ps, tok):
            q2_tok[t] = act(QT2[:, t, :], ps, ACT.Copy, [tok])
            return q2_tok[t]

        gemm(PL["q2"], [(GH, GL)], ev_q2, h_ok)

        def ev_fh(t, r_, ps, tok):
            return act(FT[:, t, :] if t < 4 else HY[:, t - 4, 1:T + 1], ps, ACT.Copy, [tok, hpad])

        for h in range(8):
            side.append(na(h))
        gemm(PL["fh"], [(GH, GL)], ev_fh, h_ok)
        fh_ok = A.now()
        drain()
        s7.close()
        s6c.close()
        r0.close()

        s8 = Scope()
        ada_open(s8, 1)
        SPEC = s8("spec2", [P, 2, 2, 2, 512])
        DF = s8("dft", [P, 4, 2, T])
        FC = s8("fft", [P, 1280])
        CA = s8("ca", [P, 2, T])
        RG = s8("rg2", [P, 3, T])
        tk_df = dma_g("d_df", DF[:, :, :, :].rearrange("p a b t -> p (a b t)"), A_["dft"])
        tk_fc = dma_g("d_fc", FC[:, :], A_["fft"])
        sp_ok = dma_g("d_sp", SPEC[:, :, :, :, :].rearrange("p a b c n -> p (a b c n)"), SPD, [spec_tok])
        s9 = Scope()
        ZK = s9("zk", [P, 2, 512])
        YF = s9("yf", [P, 2, 2, 512])
        Q1 = s9("q1", [P, 2, 512])
        Q3 = s9("q3", [P, 2, 512])
        AB = s9("ab", [P, 2, 4, T])

        def fourier():
            for g in range(4):
                b = g % 2
                for tq in range(2):
                    t = mm(PSUM[:, b, T * tq:T * tq + T], FT[:, g, 128 * tq:128 * tq + 128], FC[:, 1024:1280],
                           w=[tk_fc, fh_ok, bank_free[b]], inc=tq == 1)
                a = act(AB[:, :, g, :], PSUM[:, b, :].rearrange("p (q t) -> p q t", q=2), ACT.Copy, [t])
                bank_free[b] = [a]
                if g % 2:
                    yield
            for g in range(4):
                b = g % 2
                for n in range(4):
                    k, cs = n // 2, n % 2
                    t = mm(PSUM[:, b, 0:T], AB[:, k, g, 128 * cs:128 * cs + 128], FC[:, 512 * cs + T * k:512 * cs + T * k + T],
                           n == 0, n == 3, [a, bank_free[b]], inc=n == 3)
                a2 = act(Y2[:, 8 + g, :], PSUM[:, b, 0:T], ACT.Copy, [t])
                bank_free[b] = [a2]
                if g % 2:
                    yield

        def hyena():
            conv = {}
            for j in range(12):
                b = CA[:, j % 2, :]
                ts(V, b, HY[:, j, 2:T + 2], col("hy_cw", 24 + j), None, MUL, w=[fh_ok, conv.get(j % 2)])
                for i in (1, 0):
                    v = stt(b, HY[:, j, i:i + T], col("hy_cw", 12 * i + j), b, MUL, ADD)
                conv[j % 2] = src_ok = act(HY[:, j, 1:T + 1], b, ACT.Identity, [v], bias=col("hy_cb", j))
                if j % 2:
                    yield
            for o in range(2):
                for tq in range(2):
                    for j in range(4):
                        t = tr(PSUM[:, 2 + tq, 128 * j:128 * j + 128], HY[:, j, 1 + 128 * tq:129 + 128 * tq], ident,
                               [src_ok, bank_free[2 + tq]], inc=j == 3)
                    a = act(ZK[:, tq, :], PSUM[:, 2 + tq, :], ACT.Copy, [t])
                    bank_free[2 + tq] = [a]
                yield
                kr, ki = SPEC[:, o, 0, :, :], SPEC[:, o, 1, :, :]
                for ri in range(2):
                    for f in range(2):
                        b = 2 + f
                        for k in range(2):
                            t = mm(PSUM[:, b, :], DF[:, ri, k, 128 * f:128 * f + 128], ZK[:, k, :], k == 0, k == 1,
                                   [a, tk_df, bank_free[b]], inc=k == 1)
                    z = PSUM[:, 2:4, :]
                    if ri == 0:
                        tt(V, YF[:, 0, :, :], z, kr, MUL, [t, sp_ok])
                        v = tt(V, YF[:, 1, :, :], z, ki, MUL)
                    else:
                        v1 = tt(V, Q1[:, :, :], z, ki, MUL, [t])
                        v = tt(V, Q3[:, :, :], z, kr, MUL)
                        g = tt(G, YF[:, 0, :, :], YF[:, 0, :, :], Q1[:, :, :], SUB, [v1])
                    bank_free[2] = bank_free[3] = [v]
                    yield
                v = tt(V, YF[:, 1, :, :], YF[:, 1, :, :], Q3[:, :, :], ADD)
                for j in range(4):
                    b = 2 + j % 2
                    for n in range(4):
                        ri, f = n // 2, n % 2
                        t = mm(PSUM[:, b, 0:T], YF[:, ri, f, 128 * j:128 * j + 128], DF[:, 2 + ri, f, :], n == 0, n == 3,
                               [g, v, bank_free[b]], inc=n == 3)
                    u_ = HY[:, j, 1:T + 1]
                    w_ = stt(u_, u_, col("hy_bias", 4 * o + j), PSUM[:, b, 0:T], MUL, ADD, [t])
                    bank_free[b] = [w_]
                    src_ok = tt(V, u_ if o == 0 else Y2[:, 12 + j, :], u_, HY[:, 4 + 4 * o + j, 1:T + 1], MUL)
                    yield

        sets[0] = [[4, 5], [6, 7]]
        turn[0] = 0
        side.append(both(fourier(), hyena()))
        ada("ada3", NA2)
        drain()
        sets[0] = whole
        mod_gain(2, "norm2_g", 64, 0)
        if stop == 7:
            dump("a", Y2[:, 0:8, :])
            dump("f", Y2[:, 8:12, :])
            dump("hy", Y2[:, 12:16, :])
            return end()
        s9.close()
        r0 = Scope("right")
        GH = r0("g2hi", [P, 16, T], F32R)
        GL = r0("g2lo", [P, 16, T], F32R)
        s9 = Scope()
        TM = s9("tm9", [P, 8, T])
        mg = [(0, 8, 1024), (8, 12, 512), (12, 16, 512)]
        y_ok = []
        for i, (a_, b_, n) in enumerate(mg):
            a = act(TM[:, 0:b_ - a_, :], Y2[:, a_:b_, :], ACT.Square)
            r = rstd_of([TM[:, k, :] for k in range(b_ - a_)], n, "eps6", RG[:, i, :], [a], b=i)
            for j in range(a_, b_):
                v = stt(Y2[:, j, :], Y2[:, j, :], col("mix_g", j), RG[:, i, :], MUL, MUL)
            h = act(GH[:, a_:b_, :], Y2[:, a_:b_, :], ACT.Copy, [v])
            y_ok = [h, tt(V, GL[:, a_:b_, :], Y2[:, a_:b_, :], GH[:, a_:b_, :].bitcast(F32), SUB, [h])]
        s9.close()
        s8.close()
        s6.close()

        s4 = Scope()
        TM = s4("tma", [P, 8, T])
        ACC = s4("acca", [P, T])
        SQ2 = s4("sqa", [P, 2, T])
        RS = s4("rsa", [P, 2, T])
        HH = s4("h2hi", [P, 11, T], F32R)
        HL = s4("h2lo", [P, 11, T], F32R)
        GA = s4("ga", [P, 11, T])
        GP = s4("gp", [P, 4, T + 2])
        CV = s4("cv", [P, 2, T])
        UB = s4("ub", [P, 4, T])
        gp0 = fill(G, GP[:, :, 0:1], 0.0)
        gp0 = fill(G, GP[:, :, T + 1:T + 2], 0.0)
        ev, last = residual(XT, [(ACC[:, :], None)], SQ2, lambda t: MOD[:, 32 + t, 0:1])
        gemm(PL["out2"], [(GH, GL)], ev, y_ok)
        out_done = TE.now()
        h_ok = {}
        flush()
        r = rstd_of([ACC[:, :]], 2048, "eps6", RS[:, 0, :], [last["done"]])
        run(normed(XT, RS[:, 0, :], lambda j: GS[:, 2, j:j + 1], lambda j: MOD[:, 48 + j, 0:1], TM, GH, GL, [r, out_done], h_ok))
        if stop == 8:
            dump("x5", XT[:, :, :])
            return end()
        dn_done = out_done
        hid = {}
        for i in range(4):
            f_ok = {"g": [[], [], []]}

            def ev_gate(t, r_, ps, tok):
                if t % 4 == 0:
                    flush()
                gt = 11 * i + t
                src = GP[:, t % 4, :]
                e_ = act(src[:, 1:T + 1], ps, ACT.Copy, [tok, gp0, hid.get(("c", t % 4))])

                def rest():
                    b = CV[:, t % 2, :]
                    ts(V, b, src[:, 2:T + 2], col("ff_cw", 88 + gt), None, MUL, w=[e_, hid.get(("a", t % 2))])
                    stt(b, src[:, 1:T + 1], col("ff_cw", 44 + gt), b, MUL, ADD)
                    hid[("c", t % 4)] = v = stt(b, src[:, 0:T], col("ff_cw", gt), b, MUL, ADD)
                    hid[("a", t % 2)] = hid[("g", gt)] = act(GA[:, t, :], b, ACT.Gelu_apprx_tanh, [v, hid.get(("u", t))],
                                                             bias=col("ff_cb", gt))
                tails.append((None, 0, rest))
                return e_

            def ev_uu(t, r_, ps, tok):
                if t % 4 == 0:
                    flush()
                q = UB[:, t % 4, :]
                hid[("u", t)] = v = tt(V, q, ps, GA[:, t, :], MUL, [tok, hid[("g", 11 * i + t)], hid.get(("q", t % 4))])

                def rest():
                    h = act(HH[:, t, :], q, ACT.Copy, [v, dn_done])
                    hid[("q", t % 4)] = tt(V, HL[:, t, :], q, HH[:, t, :].bitcast(F32), SUB, [h])
                    f_ok["g"][t // 4] += [h, hid[("q", t % 4)]]
                tails.append((f_ok, t // 4, rest))
                return v

            gemm(PL[f"ga{i}"], [(GH, GL)], ev_gate, h_ok)
            gemm(PL[f"uu{i}"], [(GH, GL)], ev_uu, h_ok)
            ev, last = residual(XT, [(ACC[:, :], None)] if i == 3 else [], SQ2, lambda t: MOD[:, 80 + t, 0:1])
            gemm(PL[f"dd{i}"], [(HH, HL)], ev, f_ok)
            dn_done = TE.now()
        flush()
        r = rstd_of([ACC[:, :]], 2048, "eps6", RS[:, 0, :], [last["done"]])
        for j in range(16):
            v = stt(XT[:, j, :], XT[:, j, :], col("final_g2", j), RS[:, 0, :], MUL, MUL)
            if j % 4 == 3:
                dma(SP, "d_out", out[:, j - 3:j + 1, :], XT[:, j - 3:j + 1, :], [v])
        end()


def _layout(inp):
    import numpy as np
    f = np.float32
    a = {k: np.asarray(v) for k, v in inp.items()}

    def cols(v, n=None):
        v = np.asarray(v).reshape(-1)
        return np.ascontiguousarray(v.reshape(-1, 128).T)

    def padded(v):
        o = np.zeros((128, 1), f)
        v = np.asarray(v).reshape(-1)
        o[:v.size, 0] = v
        return o

    def tiles(v):
        return np.concatenate([cols(r) for r in v], axis=1)

    mu = a["rwkv_mu"][0]
    mu = np.concatenate([cols(mu[:3072]), padded(mu[3072:3168]), padded(mu[3168:3264]), cols(mu[3264:])], axis=1)
    one = np.ones((128, 1), f)
    parts = {
        "norm_mix_g": cols(a["norm_mix_g"]), "conv_w": tiles(a["ssd_conv_w"][0, :, 0]), "conv_b": cols(a["ssd_conv_b"]),
        "ssd_g": cols(a["ssd_norm_g"]), "ssd_d": cols(np.repeat(a["ssd_d"][0], 64)), "dt_bias": padded(a["ssd_dt_bias"]),
        "a_log": padded(a["ssd_a_log"]), "mu": mu, "w0": cols(a["rwkv_w0"]), "a0": cols(a["rwkv_a0"]),
        "k_k": cols(a["rwkv_k_k"]), "k_a": cols(a["rwkv_k_a"]), "r_k": cols(a["rwkv_r_k"]), "ln_w": cols(a["rwkv_ln_w"]),
        "ln_b": cols(a["rwkv_ln_b"]), "norm_x_g": cols(a["norm_x_g"]), "norm_mem_g": cols(a["norm_mem_g"]),
        "norm_ffn_g": cols(a["norm_ffn_g"]), "final_g": cols(a["final_norm_g"]), "c": cols(a["c_2"]),
        "c_ctx": cols(a["c_ctx_2"]), "ada_b": cols(a["ada_b_2"]), "norm1_g": cols(a["norm1_g_2"]),
        "norm2_g": cols(a["norm2_g_2"]), "hy_cw": tiles(a["hy_conv_w_2"][0]), "hy_cb": cols(a["hy_conv_b_2"]),
        "mix_g": cols(a["mix_norm_g_2"]), "ff_cw": tiles(a["ffn_conv_w_2"][0]), "ff_cb": cols(a["ffn_conv_b_2"]),
        "hy_bias": tiles(a["hy_bias_2"][0]), "final_g2": cols(a["final_norm_g_2"]), "hy_b1": padded(a["hy_b1_2"]),
        "hy_b2": padded(a["hy_b2_2"]), "hy_freq": padded(a["hy_freq_2"]), "one": one, "eps6": one * f(1e-6),
        "eps64": one * f(64e-5), "zero": np.zeros((128, 1), f),
    }
    d = {"pack": np.concatenate([parts[n] for n, _ in COLS], axis=1)}

    i = np.arange(128)
    r, c = i[:, None], i[None, :]
    d["mats"] = np.concatenate([np.eye(128), np.ones((128, 128)), (r // 64 == c // 64)], axis=1).astype(f)

    def level(t, u, s):
        return (t // (2 * s) == u // (2 * s)) & (t // s % 2 == 1) & (u // s % 2 == 0)

    same = r // 64 == c // 64
    m1 = [c >= r, level(r, c, 1)] + [level(c, r, s) for s in (1, 2, 4, 8, 16, 32)] + [same & (r < c), same & (r <= c)]
    t = np.arange(256)
    m1 += [np.broadcast_to(t % 128 != 0, (128, 256)), np.broadcast_to(t % 64 != 0, (128, 256))]
    d["mats1"] = np.concatenate(m1, axis=1).astype(f)
    d["comb"] = np.array([[1, 0], [0, 1], [1, 0], [0, 1]], f)
    d["sel"] = np.repeat(np.eye(16), 128, axis=1).astype(f)

    def fm(v):
        return np.ascontiguousarray(v.T.reshape(-1, 128, v.shape[0]).transpose(1, 0, 2))

    d["x"], d["mem"], d["ctx"] = fm(a["x"][0]), fm(a["mem"][0]), fm(a["ctx_2"][0])
    for n in WEIGHTS:
        d[n] = a[n][0]
    k = np.arange(256)
    th = np.pi * np.outer(t, 2 * k + 1) / 512.0

    def km(m):
        return m.reshape(2, 128, -1).transpose(1, 0, 2).reshape(128, -1)

    d["dft"] = np.ascontiguousarray(np.concatenate([km(np.cos(th)), km(-np.sin(th)), km(np.cos(th).T / 256),
                                                    km(-np.sin(th).T / 256)], axis=1).astype(f))
    w = 2 * np.pi / 256
    cl, sl = np.cos(w * (np.outer(t, t) % 256)), np.sin(w * (np.outer(t, t) % 256))
    q = np.arange(128)
    cd, sd = (fn(2 * np.pi / 128 * (np.outer(q, q) % 128)) for fn in (np.cos, np.sin))
    n = 1 / np.sqrt(256.0 * 128.0)
    d["fft"] = np.ascontiguousarray(np.concatenate([km(cl * n), km(-sl * n), cd, sd], axis=1).astype(f))
    pos = np.arange(256, dtype=f)
    tl = pos / f(255)
    bands = np.linspace(1e-4, 15, 16).astype(f)
    ang = bands[None, :] * f(2.0 * np.pi / 256) * pos[:, None]
    d["zt"] = np.ascontiguousarray(np.concatenate([tl[:, None], np.cos(ang), -np.sin(ang)], axis=1).astype(f).T)
    lo, hi = np.log(1e-2) / 1.5, np.log(1e-2) / 0.3
    deltas = np.linspace(lo, hi, 512).astype(f)
    win = np.exp(-tl[:, None] * np.abs(deltas)[None, :]).astype(f)
    winb = win.copy()
    winb[0] = 0
    d["win"] = np.ascontiguousarray(np.concatenate([km(win), km(winb)], axis=1).astype(f))
    d["hy_w1"], d["hy_w2"], d["hy_w3"] = a["hy_w1_2"][0], a["hy_w2_2"][0], a["hy_w3_2"][0]
    d["rw2"], d["ra2"], d["rg2"] = a["rwkv_w2"][0], a["rwkv_a2"][0], a["rwkv_g2"][0]
    row, cc = t // 64, t % 64
    st = np.clip(cc - 8, 0, 48)
    inside = (cc[None, :] >= st[:, None]) & (cc[None, :] < st[:, None] + 16)
    dr = row[None, :] - row[:, None] + 7
    dc = np.clip(cc[None, :] - cc[:, None] + 15, 0, 30)
    d["bias"] = np.ascontiguousarray(a["na_rpb_2"][0][:, dr, dc])
    d["namask"] = np.ascontiguousarray(km(np.where(inside, 0.0, -1e30)).astype(f))
    return {k: np.ascontiguousarray(v) for k, v in d.items()}


WEIGHTS = ["w_in", "w_out", "xattn_wq", "xattn_wk", "xattn_wv", "xattn_wo", "ffn_w1", "ffn_w2", "ada_w_2", "w_in_2",
           "w_out_2", "ffn_w_up_2", "ffn_w_down_2"]
STOP = 99


def kernel(**inputs):
    import numpy as _np
    import concourse.bacc as _bacc
    from concourse import mybir as _mybir
    from concourse.bass_utils import run_bass_kernel_spmd as _run

    nc = _bacc.Bacc("TRN2", target_bir_lowering=False, num_devices=1)
    arrays, args = {}, {}
    for name, v in _layout(inputs).items():
        arrays["in_" + name] = v
        args[name] = nc.dram_tensor("in_" + name, v.shape, _mybir.dt.from_np(v.dtype), kind="ExternalInput").ap()
    out = nc.dram_tensor("out_0", (128, 16, 256), _mybir.dt.float32, kind="ExternalOutput").ap()
    build(nc, args, out, STOP)
    r = _run(nc, [arrays], core_ids=[0])
    y = r.results[0]["out_0"]
    return _np.ascontiguousarray(y.transpose(2, 1, 0).reshape(1, 256, 2048))
```

```python
from contextlib import ExitStack

import concourse.bass as bass
from concourse import mybir

F32 = mybir.dt.float32
F32R = mybir.dt.float32r
ACT = mybir.ActivationFunctionType
ALU = mybir.AluOpType
AX_X = mybir.AxisListType.X
ADD, SUB, MUL, MAX, MIN = ALU.add, ALU.subtract, ALU.mult, ALU.max, ALU.min
P = 128
T = 256
NR = 6
NH = 4
CS = 1024
NA0 = 6
NA1 = 9
NA2 = 12
NA3 = 15
NA4 = 22
CN = 512

COLS = [("norm_mix_g", 16), ("conv_w", 48), ("conv_b", 12), ("ssd_g", 8), ("ssd_d", 8), ("dt_bias", 1),
        ("a_log", 1), ("mu", 28), ("w0", 8), ("a0", 8), ("k_k", 8), ("k_a", 8), ("r_k", 8), ("ln_w", 8),
        ("ln_b", 8), ("norm_x_g", 16), ("norm_mem_g", 16), ("norm_ffn_g", 16), ("final_g", 16), ("c", 16),
        ("c_ctx", 16), ("ada_b", 96), ("norm1_g", 16), ("norm2_g", 16), ("hy_cw", 36), ("hy_cb", 12),
        ("mix_g", 16), ("ff_cw", 132), ("ff_cb", 44), ("hy_bias", 8), ("final_g2", 16), ("hy_b1", 1),
        ("hy_b2", 1), ("hy_freq", 1), ("one", 1), ("eps6", 1), ("eps64", 1), ("zero", 1)]
MATS = ["ident", "ones", "bones"]
MATS1 = ["cm", "l1", "t1", "t2", "t4", "t8", "t16", "t32", "strict", "incl"]


def offsets(items):
    out, at = {}, 0
    for name, n in items:
        out[name] = at
        at += n
    return out, at


class Queue:

    def __init__(self, sem, chain):
        self.sem, self.chain, self.ops, self.n, self.seen, self.held = sem, chain, [], 0, {}, []

    def add(self, fn, w=(), inc=True):
        need = {}
        toks = list(w) + self.held + ([(self.sem, self.n)] if self.chain and self.n else [])
        self.held = []
        while toks:
            t = toks.pop()
            if isinstance(t, list):
                toks += t
            elif isinstance(t, dict):
                toks += t["g"]
            elif t is not None and t[1] > max(need.get(t[0], 0), self.seen.get(t[0], 0)):
                need[t[0]] = t[1]
        self.seen.update(need)
        self.ops.append((list(need.items()), fn, inc))
        self.n += 1 if inc else 0
        return (self.sem, self.n) if inc else None

    def now(self):
        assert self.chain or not self.ops or self.ops[-1][2]
        return (self.sem, self.n)

    def play(self, eng, sems):
        for need, fn, inc in self.ops:
            for s, v in need:
                eng.wait_ge(sems[s], v)
            ins = fn(eng)
            if inc:
                ins.then_inc(sems[self.sem], 1)


def build(nc, A_, out):
    sems = {}
    top = ExitStack()
    with top:
        def sem(name):
            sems[name] = top.enter_context(nc.semaphore(name))
            return name

        class Scope:
            def __init__(self, side="left"):
                self.st, self.side = ExitStack(), side

            def __call__(self, name, shape, dt=F32):
                return self.st.enter_context(nc.sbuf_tensor(name, shape, dt, side=self.side))

            def close(self):
                self.st.close()
                fence()

        V, A, G, TE, SP = (Queue(sem("s_dve"), True), Queue(sem("s_act"), True), Queue(sem("s_pool"), True),
                           Queue(sem("s_pe"), False), Queue(sem("s_sp"), False))
        counts = {}

        def fence():
            toks = [q.now() for q in (V, A, G, TE)]
            for q in (V, A, G):
                q.held += toks
            return toks

        def tt(q, o, a, b, op, w=()):
            return q.add(lambda e: e.tensor_tensor(o, a, b, op), w)

        def stt(o, a, s, b, op0, op1, w=()):
            return V.add(lambda e: e.scalar_tensor_tensor(o, a, s, b, op0, op1), w)

        def ts(q, o, a, s1, s2, op0, op1=None, w=()):
            if op1 is None:
                return q.add(lambda e: e.tensor_scalar(o, a, s1, None, op0), w)
            return q.add(lambda e: e.tensor_scalar(o, a, s1, s2, op0, op1), w)

        def cp(q, o, a, w=()):
            return q.add(lambda e: e.tensor_copy(o, a), w)

        def act(o, a, f, w=(), bias=None, scale=1.0, acc=None):
            if bias is None:
                if acc is None:
                    return A.add(lambda e: e.activation(o, a, f, scale=scale), w)
                return A.add(lambda e: e.activation(o, a, f, scale=scale, accum_out=acc), w)
            if acc is None:
                return A.add(lambda e: e.activation(o, a, f, bias=bias, scale=scale), w)
            return A.add(lambda e: e.activation(o, a, f, bias=bias, scale=scale, accum_out=acc), w)

        def recip(o, a, w=()):
            return V.add(lambda e: e.reciprocal(o, a), w)

        def scan(o, d0, d1, w=()):
            return V.add(lambda e: e.tensor_tensor_scan(o, d0, d1, 0.0, MUL, ADD), w)

        def fill(q, o, v, w=()):
            return q.add(lambda e: e.memset(o, v), w)

        def mm(o, l, r, start=True, stop=True, w=(), inc=False):
            return TE.add(lambda e: e.matmul(o, l, r, start=start, stop=stop), w, inc)

        def tr(o, i, ident, w=(), inc=False):
            return TE.add(lambda e: e.transpose(o, i, ident), w, inc)

        def dma(q, name, o, i, w=()):
            if name not in sems:
                sem(name)
            counts[name] = counts.get(name, 0) + 16
            v = counts[name]
            q.add(lambda e: e.dma_start(o, i).then_inc(sems[name], 16), w, inc=False)
            return (name, v)

        def dma_g(name, o, i, w=()):
            if name not in sems:
                sem(name)
            counts[name] = counts.get(name, 0) + 16
            v = counts[name]
            G.add(lambda e: e.dma_start(o, i).then_inc(sems[name], 16), w, inc=False)
            return (name, v)

        def end():
            SP.add(lambda e: e.nop(), [(n, v) for n, v in counts.items() if n == "d_out"], inc=False)
            with nc.Block() as block:
                @block.sync
                def _(e):
                    SP.play(e, sems)

                @block.tensor
                def _(e):
                    TE.play(e, sems)

                @block.vector
                def _(e):
                    V.play(e, sems)

                @block.scalar
                def _(e):
                    A.play(e, sems)

                @block.gpsimd
                def _(e):
                    G.play(e, sems)

        base = Scope()
        PSUM = top.enter_context(nc.psum_tensor("psum", [P, 8, 512], F32))
        WRAW = [base(f"wraw{i}", [P, CS]) for i in range(NR)]
        WHI = [base(f"whi{i}", [P, CS], F32R) for i in range(NH)]
        WLO = [base(f"wlo{i}", [P, CS], F32R) for i in range(NH)]
        off, npk = offsets(COLS)
        PK = base("pk", [P, npk])
        MT = base("mats", [P, len(MATS) * P])
        MOD = base("mod", [P, 96, 2])
        GS = base("gs", [P, 3, 16])
        ident, ones, bones = (MT[:, i * P:(i + 1) * P] for i in range(3))

        def col(name, j=0, rows=P):
            return PK[0:rows, off[name] + j:off[name] + j + 1]

        bank_free = [[] for _ in range(8)]
        turn = [0]
        whole = [[0, 1, 2, 3], [4, 5, 6, 7]]
        lower = [[0, 1], [2, 3]]
        sets = [whole]

        def take(n):
            b = sets[0][turn[0]][:n]
            assert len(b) == n
            turn[0] ^= 1
            return b

        def spare(i=0):
            return sets[0][turn[0]][i]

        tk_pk = [dma(SP, "d_pk", PK[:, :], A_["pack"]), dma(SP, "d_mt", MT[:, :], A_["mats"])]

        chunks = []

        def plan(w, k0, kt, blocks):
            out = []
            for c0, n in blocks:
                ids = []
                ck = min(CS // n, 4)
                for k in range(0, kt, ck):
                    m = min(ck, kt - k)
                    ids.append((len(chunks), k, m))
                    chunks.append((A_[w][(k0 + k) * P:(k0 + k + m) * P, c0:c0 + n].rearrange("(k p) n -> p k n", p=P),
                                   m, n))
                out.append((c0, n, ids))
            return out

        def cols(a, b, step=CN):
            return [(c, min(step, b - c)) for c in range(a, b, step)]

        PL = {}
        PL["ada0"] = plan("ada_w_2", 0, 16, cols(0, 512 * NA0))
        PL["in_ssd"] = plan("w_in", 0, 16, cols(0, 2560) + [(2560, 128)])
        PL["in_rwkv"] = plan("w_in", 0, 16, cols(2576, 5648, 256) + [(5648, 224), (5840, 256)])
        PL["ada1"] = plan("ada_w_2", 0, 16, cols(512 * NA0, 512 * NA1))
        PL["xk"] = plan("xattn_wk", 0, 16, cols(0, 2048, 256))
        PL["xv"] = plan("xattn_wv", 0, 16, cols(0, 2048))
        PL["ada2"] = plan("ada_w_2", 0, 16, cols(512 * NA1, 512 * NA2))
        PL["out"] = plan("w_out", 0, 16, cols(0, 2048))
        PL["xq"] = plan("xattn_wq", 0, 16, cols(0, 2048))
        PL["xo"] = plan("xattn_wo", 0, 16, cols(0, 2048))
        for i in range(4):
            PL[f"up{i}"] = plan("ffn_w1", 0, 16, cols(2048 * i, 2048 * i + 2048))
            PL[f"dn{i}"] = plan("ffn_w2", 16 * i, 16, cols(0, 2048))
        PL["ada3"] = plan("ada_w_2", 0, 16, cols(512 * NA2, 512 * NA3))
        PL["k2"] = plan("w_in_2", 0, 16, cols(1024, 2048, 256))
        PL["v2"] = plan("w_in_2", 0, 16, cols(2048, 3072))
        PL["q2"] = plan("w_in_2", 0, 16, cols(0, 1024))
        PL["fh"] = plan("w_in_2", 0, 16, cols(3072, 5120))
        PL["ada4"] = plan("ada_w_2", 0, 16, cols(512 * NA3, 512 * NA4))
        PL["out2"] = plan("w_out_2", 0, 16, cols(0, 2048))
        PL["ada5"] = plan("ada_w_2", 0, 16, cols(512 * NA4, 12288))
        for i in range(4):
            PL[f"ga{i}"] = plan("ffn_w_up_2", 0, 16, cols(1408 * i, 1408 * i + 1408))
            PL[f"uu{i}"] = plan("ffn_w_up_2", 0, 16, cols(5632 + 1408 * i, 5632 + 1408 * i + 1408))
            PL[f"dd{i}"] = plan("ffn_w_down_2", 11 * i, 11, cols(0, 2048))

        plain = {i for n in ("ada0", "ada1", "ada3", "ada4", "ada5") for _, _, ids in PL[n] for i, _, _ in ids if i % 2}
        loaded, hi_tok, lo_tok, used = {}, {}, {}, {}

        def view(t, i):
            _, m, n = chunks[i]
            return t[:, 0:m * n].rearrange("p (m n) -> p m n", n=n)

        def load(i):
            if i < len(chunks):
                j = i - NR
                loaded[i] = dma(SP, f"d_w{i % NR}", view(WRAW[i % NR], i), chunks[i][0],
                                [used[j]] if j in plain else [hi_tok.get(j), lo_tok.get(j)])

        def split(i):
            for k in range(len(hi_tok), min(i + 4, len(chunks))):
                if k in plain:
                    hi_tok[k] = loaded[k]
                    continue
                hi_tok[k] = act(view(WHI[k % NH], k), view(WRAW[k % NR], k), ACT.Copy, [loaded[k], used.get(k - NH)])
            for k in range(len(lo_tok), min(i + 3, len(chunks))):
                if k in plain:
                    lo_tok[k] = loaded[k]
                    continue
                lo_tok[k] = tt(V, view(WLO[k % NH], k), view(WRAW[k % NR], k), view(WHI[k % NH], k).bitcast(F32), SUB,
                               [hi_tok[k], used.get(k - NH)])
                load(k + NR)

        for i in range(NR):
            load(i)

        side, tails = [], []

        def tail():
            if tails:
                tails.pop(0)[2]()

        def flush():
            while tails:
                tail()

        def step():
            while side:
                n = next(side[0], "end")
                if n != "end":
                    return 1.0 if n is None else n
                side.pop(0)
            return 1.0

        part = [0.0]

        def pace(n):
            part[0] = min(part[0], 0.0) + n
            while part[0] > 0 and side:
                part[0] -= step()

        def both(*gens):
            live = list(gens)
            while live:
                for g in list(live):
                    n = next(g, "end")
                    if n == "end":
                        live.remove(g)
                    yield None if n == "end" else n

        def at(ready, k):
            if not isinstance(ready, dict):
                return ready
            while any(r is ready and g <= k // 4 for r, g, _ in tails):
                tail()
            while not ready["g"][k // 4]:
                step()
            return ready["g"][k // 4]

        def drain():
            while side:
                step()

        def run(gen):
            for _ in gen:
                pass

        def gemm(blocks, rhs, evac, ready, tiles=None, every=1):
            t = 0
            for c0, n, ids in blocks:
                starts = tiles(c0, n) if tiles else [(128 * j) for j in range(n // 128)]
                bs = take(len(starts) * len(rhs))
                ends = {}
                for i, k0, m in ids:
                    split(i)
                    hi, lo = view(WHI[i % NH], i), view(WLO[i % NH], i)
                    w = [hi_tok[i], lo_tok[i], at(ready, k0 + m - 1)]
                    for j, s in enumerate(starts):
                        for r, (HH, HL) in enumerate(rhs):
                            b = bs[j * len(rhs) + r]
                            for kk in range(m):
                                k = k0 + kk
                                last = k == blocks_k(ids) - 1
                                o = PSUM[:, b, 0:T]
                                if k == 0:
                                    w = w + [bank_free[b]]
                                mm(o, hi[:, kk, s:s + 128], HH[:, k, :], k == 0, False, w)
                                mm(o, hi[:, kk, s:s + 128], HL[:, k, :], False, False)
                                fin = last or (kk == m - 1 and j == len(starts) - 1 and r == len(rhs) - 1)
                                tok = mm(o, lo[:, kk, s:s + 128], HH[:, k, :], False, last, inc=fin)
                                w = []
                                if last:
                                    ends[(j, r)] = tok
                    used[i] = tok
                    tail()
                    pace(every)
                for j in range(len(starts)):
                    for r in range(len(rhs)):
                        b = bs[j * len(rhs) + r]
                        bank_free[b] = [evac(t, r, PSUM[:, b, 0:T], ends[(j, r)])]
                    t += 1

        def blocks_k(ids):
            return ids[-1][1] + ids[-1][2]

        def gemm_tok(blocks, lhs, evac, ready, every=1):
            for bi, (c0, n, ids) in enumerate(blocks):
                bs = take(len(lhs))
                ends = {}
                for i, k0, m in ids:
                    split(i)
                    hi, lo = view(WHI[i % NH], i), view(WLO[i % NH], i)
                    w = [hi_tok[i], lo_tok[i], at(ready, k0 + m - 1)]
                    for r, (HH, HL, sl) in enumerate(lhs):
                        for kk in range(m):
                            k = k0 + kk
                            last = k == blocks_k(ids) - 1
                            o = PSUM[0:sl.stop - sl.start, bs[r], 0:n]
                            if k == 0:
                                w = w + [bank_free[bs[r]]]
                            mm(o, HH[:, k, sl], hi[:, kk, 0:n], k == 0, False, w)
                            mm(o, HL[:, k, sl], hi[:, kk, 0:n], False, False)
                            fin = last or (kk == m - 1 and r == len(lhs) - 1)
                            tok = mm(o, HH[:, k, sl], lo[:, kk, 0:n], False, last, inc=fin)
                            w = []
                            if last:
                                ends[r] = tok
                    used[i] = tok
                    tail()
                    pace(every)
                for r in range(len(lhs)):
                    sl = lhs[r][2]
                    bank_free[bs[r]] = [evac(bi, r, PSUM[0:sl.stop - sl.start, bs[r], 0:n], ends[r])]

        def bc(ap, axis, shape):
            return ap.unsqueeze(axis).to_broadcast(shape)

        def mean_square(src, acc, w, n=16):
            a = act(acc[:, 0:4, :], src[:, 0:4, :], ACT.Square, w)
            yield
            for g in range(1, n // 4):
                s = act(acc[:, 4:8, :], src[:, 4 * g:4 * g + 4, :], ACT.Square, [a])
                yield
                a = tt(G, acc[:, 0:4, :], acc[:, 0:4, :], acc[:, 4:8, :], ADD, [s])
                yield
            return a

        def pause(n):
            for _ in range(n):
                yield

        def hold():
            toks = [q.now() for q in (V, A, G, TE)]
            for q in (V, A, G):
                q.held += toks

        def rstd_of(parts, n, eps, dst, w, b=None, mat=None):
            b = spare() if b is None else b
            for i, p in enumerate(parts):
                t = mm(PSUM[:, b, 0:T], ones if mat is None else mat, p, i == 0, i == len(parts) - 1,
                       [w, bank_free[b]], inc=i == len(parts) - 1)
            s = act(dst, PSUM[:, b, 0:T], ACT.Sqrt, [t], bias=col(eps), scale=1.0 / n)
            bank_free[b] = [s]
            return recip(dst, dst, [s])

        def normed(src, rstd, gain, shift, tmp, HH, HL, w, res):
            res["g"] = []

            def low(g, h):
                return tt(V, HL[:, 4 * g:4 * g + 4, :], tmp[:, (g % 2) * 4:(g % 2) * 4 + 4, :],
                          HH[:, 4 * g:4 * g + 4, :].bitcast(F32), SUB, [h])

            h = None
            for g in range(4):
                t = tmp[:, (g % 2) * 4:(g % 2) * 4 + 4, :]
                if shift is None:
                    for j in range(4):
                        a = stt(t[:, j, :], src[:, 4 * g + j, :], gain(4 * g + j), rstd, MUL, MUL, [w])
                else:
                    m = tt(V, t, src[:, 4 * g:4 * g + 4, :], bc(rstd, 1, [P, 4, T]), MUL, [w])
                yield
                if g:
                    res["g"].append([h, low(g - 1, h)])
                    yield
                if shift is not None:
                    for j in range(4):
                        a = act(t[:, j, :], t[:, j, :], ACT.Identity, [m], bias=shift(4 * g + j), scale=gain(4 * g + j))
                h = act(HH[:, 4 * g:4 * g + 4, :], t, ACT.Copy, [a, w])
                yield
            res["g"].append([h, low(3, h)])
            yield

        def residual(XT, acc, sq, scale=None, nxt=None, sq2=None, here=None):
            last = {}
            for i in range(len(acc)):
                last[i] = {}
            if nxt:
                nxt[3]["g"] = [[], [], [], []]

            def squares(t, v):
                for i, (sm_, gain) in enumerate(acc):
                    u = last[i]
                    sc = 1.0 if gain is None else gain(t)
                    if t == 0:
                        u["g"] = act(sm_, XT[:, 0, :], ACT.Square, [v], scale=sc)
                    else:
                        d = (sq, sq2)[i][:, t % 2, :]
                        s = act(d, XT[:, t, :], ACT.Square, [v, u.get(t - 2)], scale=sc)
                        u["g"] = u[t] = tt(G, sm_, sm_, d, ADD, [s, u["g"]])
                last["done"] = [last[i]["g"] for i in range(len(acc))]

            def operand(t, v):
                gain, hi, lo, ready, w = nxt
                h = act(hi[:, t, :], XT[:, t, :], ACT.Copy, [v, w], scale=gain(t))
                ready["g"][t // 4] += [h, stt(lo[:, t, :], XT[:, t, :], gain(t), hi[:, t, :].bitcast(F32), MUL, SUB, [h])]

            def ev(t, r, ps, tok):
                if scale is None:
                    v = tt(V, XT[:, t, :], ps, XT[:, t, :], ADD, [tok, here])
                else:
                    v = stt(XT[:, t, :], ps, scale(t), XT[:, t, :], MUL, ADD, [tok])
                if nxt:
                    tails.append((nxt[3], t // 4, lambda: (squares(t, v), operand(t, v))))
                elif acc:
                    tails.append((None, 0, lambda: squares(t, v)))
                return v
            return ev, last

        ad = {}

        def ada_open(sc, n, mo=None):
            S4 = sc(f"s4_{n}", [P, 16, 4], F32R)
            SF = sc(f"sf_{n}", [P, 16, 4])
            ad["mo"] = sc(f"mo_{n}", [4, 2, CN]) if mo is None else mo
            ad["cb"] = sc(f"comb_{n}", [4, 2])
            ad["tk"] = dma_g(f"d_cb{n}", ad["cb"][:, :], A_["comb"])
            z = fill(G, SF[:, :, :], 0.0)
            sf = SF[:, :, :].rearrange("p k m -> p m k")
            act(sf[:, 0, :], PK[:, off["c"]:off["c"] + 16], ACT.Silu, [tk_pk, z])
            a = act(sf[:, 1, :], PK[:, off["c_ctx"]:off["c_ctx"] + 16], ACT.Silu)
            s4 = S4[:, :, :].rearrange("p k m -> p m k")
            a = act(s4[:, 0:2, :], sf[:, 0:2, :], ACT.Copy)
            ad["s4"], ad["sf"] = S4, SF
            ad["ok"] = tt(V, s4[:, 2:4, :], sf[:, 0:2, :], s4[:, 0:2, :].bitcast(F32), SUB, [a])

        ada_mm, ada_late = {}, []

        def ada_flush():
            while ada_late:
                n, v = ada_late.pop(0)
                b = 1 + 2 * (n % 2)
                for j in range(4):
                    t = mm(PSUM[:, b, 2 * j:2 * j + 2], ad["mo"][0:4, n % 2, 128 * j:128 * j + 128], ad["cb"][:, :],
                           w=[v, ad["tk"], bank_free[b]], inc=j == 3)
                ada_mm[n] = t
                v = tt(V, MOD[:, 4 * n:4 * n + 4, :], PSUM[:, b, 0:8].rearrange("p (n c) -> p n c", c=2),
                       bc(PK[:, off["ada_b"] + 4 * n:off["ada_b"] + 4 * n + 4], 2, [P, 4, 2]), ADD, [t])
                bank_free[b] = [v]

        def ada(name, n0, every=1):
            def ev(bi, r_, ps, tok):
                n = n0 + bi
                ada_flush()
                v = act(ad["mo"][:, n % 2, :], ps, ACT.Copy, [tok, ada_mm.get(n - 2)])
                ada_late.append((n, v))
                return v

            for bi, (c0, n, ids) in enumerate(PL[name]):
                b = take(1)[0]
                o = PSUM[0:4, b, :]
                for i, k0, m in ids:
                    split(i)
                    w = [hi_tok[i], lo_tok[i], ad["ok"]] + ([bank_free[b]] if k0 == 0 else [])
                    for kk in range(m):
                        k = k0 + kk
                        first, last = k == 0, k == 15
                        if i in plain:
                            tok = mm(o, ad["sf"][:, k, :], view(WRAW[i % NR], i)[:, kk, :], first, last, w, inc=kk == m - 1)
                        else:
                            mm(o, ad["s4"][:, k, :], view(WHI[i % NH], i)[:, kk, :], first, False, w)
                            tok = mm(o, ad["s4"][:, k, :], view(WLO[i % NH], i)[:, kk, :], False, last, inc=kk == m - 1)
                        w = []
                    used[i] = tok
                    if i in plain:
                        load(i + NR)
                    tail()
                    pace(every)
                bank_free[b] = [ev(bi, 0, o, tok)]
            ada_flush()

        KXD = nc.dram_tensor("kx_scratch", (P, 16, T), F32).ap()
        VXD = nc.dram_tensor("vx_scratch", (P, 2, 2048), F32).ap()
        SPD = nc.dram_tensor("spec_scratch", (P, 4096), F32).ap()
        s1 = Scope()
        HH = s1("h1hi", [P, 16, T], F32R)
        HL = s1("h1lo", [P, 16, T], F32R)
        sm = Scope()
        M1 = sm("m1", [P, len(MATS1) * P + 2 * T])
        m1 = {n: M1[:, i * P:(i + 1) * P] for i, n in enumerate(MATS1)}
        rm128 = M1[:, len(MATS1) * P:len(MATS1) * P + T]
        rm64 = M1[:, len(MATS1) * P + T:len(MATS1) * P + 2 * T]
        YS = sm("ys", [P, 8, T])
        ada_open(sm, 0)
        s1c = Scope()
        X0 = s1c("x0", [P, 16, T])
        TM = s1c("tm1", [P, 8, T])
        RS = s1c("rs1", [P, T])
        tk_x0 = dma_g("d_x0", X0[:, :, :], A_["x"])

        def spectrum():
            SPEC = s9("spec", [P, 2, 2, 2, 512])
            DF = s9("dft0", [P, 2, 2, T])
            ZT = s9("zt", [33, T])
            W1 = s9("hw1", [33, 64])
            W2 = s9("hw2", [64, 64])
            W3 = s9("hw3", [64, 2048])
            WN = s9("win", [P, 2, 2, 512])
            HF = s9("hf", [P, 2, 2048])
            HD = s9("hd", [64, 3, T])
            tk_h1 = [dma_g("d_zt", ZT[:, :], A_["zt"]), dma_g("d_hw1", W1[:, :], A_["hy_w1"]), dma_g("d_hw2", W2[:, :], A_["hy_w2"])]
            tk_h3 = [dma_g("d_hw3", W3[:, :], A_["hy_w3"]),
                     dma_g("d_win", WN[:, :, :, :].rearrange("p a b t -> p (a b t)"), A_["win"])]
            tk_df = dma_g("d_df0", DF[:, :, :, :].rearrange("p a b t -> p (a b t)"), A_["dft"][:, 0:1024])
            yield
            d = [HD[:, i, :] for i in range(3)]
            a = tk_h1
            for wt, rhs, bias in ((W1, ZT[:, :], "hy_b1"), (W2, d[2], "hy_b2")):
                b = spare()
                t = mm(PSUM[0:64, b, 0:T], wt[:, :], rhs, w=[a, bank_free[b]], inc=True)
                v = ts(V, d[0], PSUM[0:64, b, 0:T], col(bias, rows=64), col("hy_freq", rows=64), ADD, MUL, [t])
                bank_free[b] = [v]
                ts(V, d[1], d[0], 0.15915494309189535, 12582912.0, MUL, ADD)
                ts(V, d[1], d[1], 12582912.0, None, SUB)
                stt(d[0], d[1], -6.28125, d[0], MUL, ADD)
                stt(d[0], d[1], -0.0019353071795864769, d[0], MUL, ADD)
                v = ts(V, d[0], d[0], 3.1415925, -3.1415925, MIN, MAX)
                a = act(d[2], d[0], ACT.Sin, [v])
                yield
            for n in range(4):
                for tq in range(2):
                    b = spare(2 + tq)
                    t = mm(PSUM[:, b, :], d[2][:, 128 * tq:128 * tq + 128], W3[:, 512 * n:512 * n + 512], w=[a, tk_h3, bank_free[b]], inc=True)
                    v = tt(V, HF[:, tq, 512 * n:512 * n + 512], PSUM[:, b, :], WN[:, n % 2, tq, :], MUL, [t])
                    bank_free[b] = [v]
                yield
            for o in range(2):
                f_, b_ = HF[:, :, 1024 * o:1024 * o + 512], HF[:, :, 1024 * o + 512:1024 * o + 1024]
                g = tt(G, f_, f_, b_, ADD, [v])
                h = stt(b_, b_, -2.0, f_, MUL, ADD, [g])
                yield
                for ri in range(2):
                    for f in range(2):
                        b = spare(2 + f)
                        for k in range(2):
                            t = mm(PSUM[:, b, :], DF[:, ri, k, 128 * f:128 * f + 128],
                                   HF[:, k, 1024 * o + 512 * ri:1024 * o + 512 * ri + 512],
                                   k == 0, k == 1, [h, tk_df, bank_free[b]], inc=k == 1)
                        a = act(SPEC[:, o, ri, f, :], PSUM[:, b, :], ACT.Copy, [t])
                        bank_free[b] = [a]
                    yield
            spec_tok.append(dma_g("d_spec", SPD, SPEC[:, :, :, :, :].rearrange("p a b c n -> p (a b c n)"), [a]))

        spec_tok = []
        s9 = Scope()
        ready = {}

        def first_norm():
            yield from pause(5)
            sq = yield from mean_square(X0, TM, [tk_x0, tk_pk])
            yield
            r = rstd_of([TM[:, i, :] for i in range(4)], 2048, "eps6", RS[:, :], [sq, tk_pk])
            yield
            yield from normed(X0, RS[:, :], lambda j: col("norm_mix_g", j), None, TM, HH, HL, [r], ready)

        side.append(first_norm())
        side.append(spectrum())
        ada("ada0", 0)
        drain()
        s9.st.close()
        s1c.st.close()
        for q in (V, A, G):
            q.held += spec_tok
        fence()

        rk = Scope("right")
        RK = rk("rk", [P, 28, T + 1])
        s1b = Scope()
        ZZ = s1b("zz", [P, 8, T])
        XB = s1b("xb", [P, 12, T + 3])
        DT = s1b("dt", [16, 4, T])
        xpad = fill(G, XB[:, :, 0:3], 0.0)
        zpad = fill(G, RK[:, :, 0:1], 0.0)

        def ev_ssd(t, r_, ps, tok):
            if t < 8:
                return act(ZZ[:, t, :], ps, ACT.Silu, [tok])
            if t < 20:
                return act(XB[:, t - 8, 3:T + 3], ps, ACT.Copy, [tok])
            return act(DT[:, 0, :], ps[0:16, :], ACT.Copy, [tok])

        tk_m1 = dma_g("d_m1", M1[:, :], A_["mats1"])
        gemm(PL["in_ssd"], [(HH, HL)], ev_ssd, ready)
        tk_ssd = A.now()

        def ev_rwkv(t, r_, ps, tok):
            return act(RK[:, t, 1:T + 1], ps, ACT.Copy, [tok])

        s1c = Scope()
        AC = s1c("cacc", [P, 2, T])
        SEL = s1c("sel", [16, 16 * P])
        DTT = s1c("dtt", [P, 2, 16])
        CST = s1c("cst", [P, 2, 16])
        DE = s1c("de", [P, 2, 16])
        CBM = s1c("cbm", [P, 4, P])
        E = s1c("e", [P, 16, P])
        XD = s1c("xd", [P, 2, 1024])
        BM = s1c("bm", [P, 2, P])
        ST = s1c("st", [P, 2, 512])
        YK = s1c("yk", [P, 2, 1024])
        RG = ST[:, :, 0:T]
        XE = YK[:, 1, :]
        tk_sel = dma_g("d_sel", SEL[:, :], A_["sel"])
        def ssd():
            conv = {}
            xq = XB
            for j in [8, 9, 10, 11] + list(range(8)):
                b = AC[:, j % 2, :]
                ts(V, b, xq[:, j, 3:T + 3], col("conv_w", 36 + j), None, MUL, w=[tk_ssd, xpad, conv.get(j % 2)])
                for i in (2, 1, 0):
                    v = stt(b, xq[:, j, i:i + T], col("conv_w", 12 * i + j), b, MUL, ADD)
                conv[j % 2] = xs_ok = act(xq[:, j, 3:T + 3], b, ACT.Silu, [v], bias=col("conv_b", j))
                if j == 11:
                    bc_ok = xs_ok
                yield
            d = [DT[0:16, i, :] for i in range(4)]
            ts(V, d[0], d[0], col("dt_bias", rows=16), None, ADD)
            v = stt(d[1], d[0], -1.0, d[0], MUL, MAX)
            act(d[1], d[1], ACT.Exp, [v], scale=-1.0)
            act(d[2][:, 0:1], col("a_log", rows=16), ACT.Exp)
            yield
            a = act(d[1], d[1], ACT.Ln, bias=col("one", rows=16))
            yield
            v = stt(d[0], d[0], 0.0, d[1], MAX, ADD, [a])
            v = ts(V, d[3], d[0], d[2][:, 0:1], -1.0, MUL, MUL)
            CSR = d[1]
            v = scan(CSR, rm128[0:16, :], d[3], [tk_m1])
            yield
            for c in range(2):
                tr(PSUM[:, 4, 32 * c:32 * c + 16], d[0][:, 128 * c:128 * c + 128], ident[0:16, 0:16], [v, bank_free[4]])
                t = tr(PSUM[:, 4, 32 * c + 16:32 * c + 32], CSR[:, 128 * c:128 * c + 128], ident[0:16, 0:16], inc=True)
            v2 = PSUM[:, 4, 0:64].rearrange("p (c a h) -> p c a h", c=2, a=2)
            cp(V, DTT[:, :, :], v2[:, :, 0, :], [t])
            cst_ok = cp(V, CST[:, :, :], v2[:, :, 1, :])
            bank_free[4] = [cst_ok]
            for c in range(2):
                for g in range(2):
                    sl = slice(3 + 128 * c, 131 + 128 * c)
                    t = mm(PSUM[:, 5, (2 * c + g) * 128:(2 * c + g) * 128 + 128], XB[:, 8 + g, sl], XB[:, 10 + g, sl],
                           w=[bc_ok, bank_free[5]], inc=True)
            cb_ok = tt(V, CBM[:, :, :], PSUM[:, 5, :].rearrange("p (a l) -> p a l", l=P), bc(m1["cm"], 1, [P, 4, P]), MUL, [t, tk_m1])
            bank_free[5] = [cb_ok]
            for g in range(2):
                t = tr(PSUM[:, 6, g * 128:g * 128 + 128], XB[:, 8 + g, 3:131], ident, [bc_ok, bank_free[6]], inc=True)
            bm_ok = act(BM[:, :, :], PSUM[:, 6, 0:256].rearrange("p (g n) -> p g n", g=2), ACT.Copy, [t])
            bank_free[6] = [bm_ok]
            yield
            xd_ok = []
            for c in range(2):
                bs = [4 + 2 * c, 5 + 2 * c]
                for j in range(8):
                    t = tr(PSUM[:, bs[j // 4], (j % 4) * 128:(j % 4) * 128 + 128], XB[:, j, 3 + 128 * c:131 + 128 * c], ident,
                           [xs_ok, bank_free[bs[j // 4]]], inc=True)
                v = tt(V, XD[:, c, :].rearrange("p (h d) -> p h d", d=64),
                       PSUM[:, bs[0]:bs[0] + 2, :].rearrange("p b (h d) -> p (b h) d", d=64),
                       bc(DTT[:, c, :], 2, [P, 16, 64]), MUL, [t])
                bank_free[bs[0]] = bank_free[bs[1]] = [v]
                xd_ok.append(v)
                yield
            y_ok = []
            e_free = None
            for c in range(2):
                for h in range(16):
                    b = 4 + h // 4
                    t = mm(PSUM[:, b, (h % 4) * 128:(h % 4) * 128 + 128], SEL[:, h * P:(h + 1) * P], CSR[:, 128 * c:128 * c + 128],
                           w=[tk_sel, bank_free[b]], inc=h == 15)
                csb = PSUM[:, 4:8, :].rearrange("p b (h l) -> p (b h) l", l=P)
                if c == 0:
                    v = tt(V, DE[:, 0, :], csb[:, :, 127], CST[:, 0, :], SUB, [t])
                    de_ok = act(DE[:, 0, :], DE[:, 0, :], ACT.Exp, [v])
                    de_ok = act(DE[:, 1, :], CST[:, 1, :], ACT.Exp, [cst_ok])
                ea = []
                for b in range(4, 8):
                    h4 = slice(4 * b - 16, 4 * b - 12)
                    v = tt(V, E[:, h4, :], csb[:, h4, :], bc(CST[:, c, h4], 2, [P, 4, P]), SUB, [t, e_free])
                    bank_free[b] = [v]
                    v = ts(V, E[:, h4, :], E[:, h4, :], 0.0, None, MIN)
                    ea.append(act(E[:, h4, :], E[:, h4, :], ACT.Exp, [v]))
                    yield
                for q in range(4):
                    em_ok = tt(V, E[:, 4 * q:4 * q + 4, :], E[:, 4 * q:4 * q + 4, :],
                               bc(CBM[:, 2 * c + q // 2, :], 1, [P, 4, P]), MUL, [ea[q], cb_ok])
                    if q % 2:
                        yield
                if c == 0:
                    x_ = tt(V, XE.rearrange("p (h d) -> p h d", d=64), XD[:, 0, :].rearrange("p (h d) -> p h d", d=64),
                            bc(DE[:, 0, :], 2, [P, 16, 64]), MUL, [de_ok])
                    yield
                    for g in range(2):
                        t = mm(PSUM[:, 4 + g, :], BM[:, g, :], XE[:, g * 512:g * 512 + 512], w=[x_, bm_ok, bank_free[4 + g]], inc=True)
                        st_ok = act(ST[:, g, :], PSUM[:, 4 + g, :], ACT.Copy, [t])
                        bank_free[4 + g] = [st_ok]
                yield
                for h in range(16):
                    b = 6 + h // 8
                    t = mm(PSUM[:, b, (h % 8) * 64:(h % 8) * 64 + 64], E[:, h, :], XD[:, c, h * 64:h * 64 + 64],
                           w=[em_ok, xd_ok[c], bank_free[b]], inc=h == 15)
                e_free = t
                yd = PSUM[:, 6:8, :].rearrange("p b n -> p (b n)")
                if c == 0:
                    y = act(YK[:, 0, :], yd, ACT.Copy, [t])
                else:
                    for g in range(2):
                        t2 = mm(PSUM[:, 4 + g, :], XB[:, 10 + g, 131:259], ST[:, g, :], w=[st_ok, bank_free[4 + g]], inc=True)
                    v = tt(V, YK[:, 1, :].rearrange("p (h d) -> p h d", d=64),
                           PSUM[:, 4:6, :].rearrange("p b (h d) -> p (b h) d", d=64), bc(DE[:, 1, :], 2, [P, 16, 64]), MUL, [t2, de_ok])
                    bank_free[4] = bank_free[5] = [v]
                    y = tt(V, YK[:, 1, :], YK[:, 1, :], yd, ADD, [t])
                bank_free[6] = bank_free[7] = [y]
                y_ok.append(y)
                yield
            for b in range(4, 8):
                for j in (2 * b - 8, 2 * b - 7):
                    for c in range(2):
                        t = tr(PSUM[:, b, (j % 2) * T + 128 * c:(j % 2) * T + 128 * c + 128], YK[:, c, 128 * j:128 * j + 128],
                               ident, [y_ok, bank_free[b]], inc=True)
                for j in (2 * b - 8, 2 * b - 7):
                    v = stt(YS[:, j, :], XB[:, j, 3:T + 3], col("ssd_d", j), PSUM[:, b, (j % 2) * T:(j % 2) * T + T], MUL, ADD, [t])
                bank_free[b] = [v]
            yield
            v = tt(V, YS[:, :, :], YS[:, :, :], ZZ[:, :, :], MUL)
            for g in range(2):
                a = act(ZZ[:, 4 * g:4 * g + 4, :], YS[:, 4 * g:4 * g + 4, :], ACT.Square, [v])
                yield
                r = rstd_of([ZZ[:, 4 * g + i, :] for i in range(4)], 512, "eps6", RG[:, g, :], [a], b=4 + g)
                for j in range(4 * g, 4 * g + 4):
                    stt(YS[:, j, :], YS[:, j, :], col("ssd_g", j), RG[:, g, :], MUL, MUL)
                yield

        sets[0] = lower
        side.append(ssd())
        gemm(PL["in_rwkv"], [(HH, HL)], ev_rwkv, ready, tiles=lambda c0, n: [0, 96] if n == 224 else [0, 128],
             every=1.25)
        drain()
        h_done = TE.now()
        s1c.close()
        s1b.close()
        s1c = Scope()
        X0 = s1c("mem0", [P, 16, T])
        TM = s1c("tm2", [P, 8, T])
        RS = s1c("rs2", [P, T])
        tk_mem = dma_g("d_mem", X0[:, :, :], A_["mem"])
        m_ok = {}

        def mem_norm():
            yield from pause(8)
            sq = yield from mean_square(X0, TM, [tk_mem])
            yield
            r = rstd_of([TM[:, i, :] for i in range(4)], 2048, "eps6", RS[:, :], [sq], b=7)
            yield
            yield from normed(X0, RS[:, :], lambda j: col("norm_mem_g", j), None, TM, HH, HL, [r, h_done], m_ok)

        side.append(mem_norm())
        ada("ada1", NA0)
        drain()
        s1c.close()

        s2 = Scope()
        LD, C, IC, KK, RT = (s2(n, [P, 4, T]) for n in ("rld", "rc", "ric", "rkk", "rrt"))
        VT, BT, KT = (s2(n, [P, 512]) for n in ("rvt", "rbt", "rkt"))
        LA, MB, MK, XT_ = (s2(n, [P, 8, P]) for n in ("rla", "rmb", "rmk", "rxt"))
        US, SS = (s2(n, [P, 512]) for n in ("rus", "rss"))
        S = s2("rs", [P, 4, P])
        TW = s2("rtw", [96, T])
        PCE = s2("rpce", [P, 4, 4])
        OK = s2("romka", [P, 8])
        X4 = s2("rx4", [P, 4, 512])
        STG = s2("stage", [P, 2, 512])

        def UU(a, b):
            return RK[:, a:b, 1:T + 1]

        def U(j):
            return RK[:, j, 1:T + 1]

        def two(b):
            return PSUM[:, b:b + 2, :].rearrange("p b (j t) -> p (b j) t", t=T)

        def free(v, *bs):
            for b in bs:
                bank_free[b] = [v]

        def slot(h):
            return 4 * (h % 2) + h // 2

        def rwkv():
            w2_ok = load_w2(0, [])
            om = ts(V, OK[:, :], PK[:, off["k_a"]:off["k_a"] + 8], -1.0, 1.0, MUL, ADD)
            ring = [t[:, :].rearrange("p (a t) -> p a t", t=T) for t in (US, SS, VT)]
            rfree = {}
            for n, g in enumerate([12, 13] + list(range(12))):
                d = ring[n % 3]
                g_ = tt(G, d, RK[:, 2 * g:2 * g + 2, 0:T], UU(2 * g, 2 * g + 2), SUB, [zpad, rfree.get(n % 3)])
                for j in range(2):
                    v = stt(U(2 * g + j), d[:, j, :], col("mu", 2 * g + j), U(2 * g + j), MUL, ADD, [g_])
                rfree[n % 3] = v
                if n == 1:
                    a = act(TW[:, :], RK[0:96, 24, 1:T + 1], ACT.Tanh, [v])
                    act(UU(26, 28), UU(26, 28), ACT.Sigmoid)
                if n % 2:
                    yield
            sh_ok, tw_ok = v, a
            for hf in range(2):
                w2_ok = yield from half(hf, sh_ok, tw_ok, om, w2_ok)

        def load_w2(hf, w):
            c = slice(512 * hf, 512 * hf + 512)
            return [dma_g("d_rw2", BT[0:96, :], A_["rw2"][:, c], w), dma_g("d_ra2", KT[0:96, :], A_["ra2"][:, c])]

        def half(hf, sh_ok, tw_ok, om, w2_ok):
            hold()
            c0, p0 = 512 * hf, 4 * hf
            tk_w2, tk_a2 = w2_ok
            rr, kq, vv = UU(p0, p0 + 4), UU(8 + p0, 12 + p0), UU(16 + p0, 20 + p0)
            s0 = fill(G, S[:, :, :], 0.0)
            yield
            for j in range(4):
                t = mm(two(4)[:, j, :], BT[0:96, 128 * j:128 * j + 128], TW[:, :], w=[tw_ok, tk_w2, bank_free[4 + j // 2]], inc=True)
            for j in range(4):
                t2 = mm(two(6)[:, j, :], KT[0:96, 128 * j:128 * j + 128], RK[0:96, 25, 1:T + 1],
                        w=[tk_a2, sh_ok, bank_free[6 + j // 2]], inc=True)
            for j in range(4):
                ld_ok = act(LD[:, j, :], two(4)[:, j, :], ACT.Sigmoid, [t], bias=col("w0", p0 + j))
            free(ld_ok, 4, 5)
            yield 0.5
            for j in range(4):
                ic_ok = act(IC[:, j, :], two(6)[:, j, :], ACT.Sigmoid, [t2], bias=col("a0", p0 + j))
            free(ic_ok, 6, 7)
            yield
            SQ, RN, KM = (t[:, :, :].rearrange("p a b -> p (a b)").rearrange("p (j t) -> p j t", t=T) for t in (LA, MB, MK))
            for j in range(4):
                a = act(KK[:, j, :], U(8 + p0 + j), ACT.Copy, [sh_ok], scale=col("k_k", p0 + j))
            yield 0.5
            a = act(SQ, KK[:, :, :], ACT.Square)
            ts(V, LD[:, :, :], LD[:, :, :], -0.6065306597126334, None, MUL, w=[ld_ok])
            for j in range(4):
                scan(C[:, j, :], rm64, LD[:, j, :])
            yield 0.5
            v = tt(V, LD[:, :, :], C[:, :, :], LD[:, :, :], SUB)
            for j in range(4):
                km = act(KM[:, j, :], IC[:, j, :], ACT.Identity, [om], scale=col("k_a", p0 + j), bias=OK[:, p0 + j:p0 + j + 1])
            yield
            for j in range(4):
                t = mm(two(4)[:, j, :], bones, SQ[:, j, :], w=[a, bank_free[4 + j // 2]], inc=True)
            a_ld = act(LD[:, :, :], LD[:, :, :], ACT.Exp, [v])
            yield 0.5
            a_rt = act(RT[:, :, :], C[:, :, :], ACT.Exp)
            a_c = act(C[:, :, :], C[:, :, :], ACT.Exp, scale=-1.0)
            yield 0.5
            rn = act(RN, two(4), ACT.Sqrt, [t])
            free(rn, 4, 5)
            km_ok = tt(V, kq, kq, KM, MUL, [km])
            cp(V, PCE[:, :, :], RT[:, :, 63::64], [a_rt])
            yield 0.5
            r_ok = tt(V, RT[:, :, :], RT[:, :, :], rr, MUL)
            g_rk = tt(G, rr, rr, kq, MUL, [r_ok, km_ok])
            yield
            ts(V, RN, RN, 1e-12, None, MAX, w=[rn])
            recip(RN, RN)
            yield 0.5
            kk_ok = tt(V, KK[:, :, :], KK[:, :, :], RN, MUL)
            al_ok = stt(LD[:, :, :], LD[:, :, :], -1.0, KK[:, :, :], MUL, MUL, [a_ld])
            g_ic = tt(G, IC[:, :, :], IC[:, :, :], KK[:, :, :], MUL, [kk_ok, km])
            for j in range(4):
                a = act(U(p0 + j), U(p0 + j), ACT.Copy, [g_rk], scale=col("r_k", p0 + j))
            yield
            b_ok = tt(V, IC[:, :, :], IC[:, :, :], C[:, :, :], MUL, [g_ic, a_c])
            kt_ok = tt(V, C[:, :, :], C[:, :, :], kq, MUL)
            for j in range(4):
                t = mm(two(6)[:, j, :], bones, U(p0 + j), w=[a, bank_free[6 + j // 2]], inc=True)
            bo_ok = tt(V, rr, two(6), vv, MUL, [t])
            free(bo_ok, 6, 7)
            in_ok = [al_ok, r_ok, b_ok, kt_ok, bo_ok]
            yield
            tmp4 = [[t[:, :].rearrange("p (h t) -> p h t", t=P) for t in (KK[:, 0:2, :].rearrange("p a t -> p (a t)"),
                                                                           KK[:, 2:4, :].rearrange("p a t -> p (a t)"),
                                                                           X4[:, 0, :], X4[:, 1, :])],
                    [RK[:, 8 + p0:12 + p0, :].rearrange("p a t -> p (a t)")[:, 512 * i:512 * i + 512].rearrange("p (h t) -> p h t", t=P)
                     for i in range(2)] + [X4[:, i, :].rearrange("p (h t) -> p h t", t=P) for i in (2, 3)]]
            seq_ok, s_ok = None, [s0]
            for tq in range(2):
                tsl = slice(128 * tq, 128 * tq + 128)
                toks = []
                for i, (src, dst) in enumerate(((vv, VT), (IC, BT), (C, KT))):
                    for j in range(4):
                        t = tr(PSUM[:, 4 + i, j * 128:j * 128 + 128], src[:, j, tsl], ident, [in_ok, bank_free[4 + i]], inc=True)
                    a = act(dst[:, :], PSUM[:, 4 + i, :], ACT.Copy, [t, seq_ok])
                    free(a, 4 + i)
                    toks.append(a)
                yield
                done = []

                def chain(ch):
                    LT, X, Z, ML = tmp4[ch]
                    hs = slice(4 * ch, 4 * ch + 4)
                    XT = XT_[:, hs, :]
                    b0, b1 = 4 + 2 * ch, 5 + 2 * ch

                    def view4(b):
                        return PSUM[:, b, :].rearrange("p (h t) -> p h t", t=P)

                    def four(b, lsrc, rsrc):
                        for i in range(4):
                            p = slice(64 * ch, 64 * ch + 64)
                            t = mm(PSUM[:, b, 128 * i:128 * i + 128], lsrc[p, i, tsl], rsrc[p, i, tsl],
                                   w=[in_ok, bank_free[b]], inc=i == 3)
                        return t

                    def m4(n):
                        return bc(m1[n], 1, [P, 4, P])

                    t = four(b0, IC, LD)
                    lt_ok = act(LT, view4(b0), ACT.Copy, [t])
                    free(lt_ok, b0)
                    t = four(b1, LD, IC)
                    v = tt(V, X, view4(b1), m4("l1"), MUL, [t])
                    free(v, b1)
                    eye = bc(ident, 1, [P, 4, P])
                    x_ok = tt(V, X, X, eye, ADD)
                    ml = tt(G, ML, LT, m4("t2"), MUL, [lt_ok])
                    yield 0.3
                    tt(V, XT, LT, m4("t1"), MUL, [lt_ok, seq_ok])
                    xt_ok = tt(V, XT, XT, eye, ADD)
                    rest = [(C, LD, LA, "strict"), (IC, RT, MB, "incl"), (C, RT, MK, "incl")]
                    for s in (2, 4, 8, 16, 32):
                        for i in range(4):
                            t = mm(PSUM[:, b0, 128 * i:128 * i + 128], ML[:, i, :], X[:, i, :], w=[ml, x_ok, bank_free[b0]], inc=i == 3)
                        lv = t
                        z = act(Z, view4(b0), ACT.Copy, [t, xt_ok, x_ok])
                        free(z, b0)
                        if rest:
                            ls, rs_, dst, msk = rest.pop(0)
                            t = four(b1, ls, rs_)
                            v = tt(V, dst[:, hs, :], view4(b1), m4(msk), MUL, [t, seq_ok])
                            free(v, b1)
                            done.append(v)
                        yield 0.3
                        for i in range(4):
                            t = mm(PSUM[:, b0, 128 * i:128 * i + 128], Z[:, i, :], XT[:, i, :], w=[z, xt_ok, bank_free[b0]], inc=i == 3)
                        if s < 32:
                            for i in range(4):
                                t = mm(PSUM[:, b1, 128 * i:128 * i + 128], XT[:, i, :], Z[:, i, :], w=[bank_free[b1]], inc=i == 3)
                        xt_ok = tt(V, XT, XT, view4(b0), ADD, [t])
                        free(xt_ok, b0)
                        if s < 32:
                            x_ok = tt(V, X, X, view4(b1), ADD)
                            free(x_ok, b1)
                            ml = tt(G, ML, LT, m4(f"t{2 * s}"), MUL, [lv])
                        yield 0.3
                    done.append(xt_ok)

                yield from both(chain(0), chain(1))
                for cl in range(2):
                    R = slice(64 * cl, 64 * cl + 64)
                    for j in range(4):
                        o = j * 128
                        mm(PSUM[:, 4, o:o + 128], LD[:, j, tsl], S[:, j, :], True, False, [done, toks, s_ok, bank_free[4]])
                        for q in range(2):
                            h = 2 * j + q
                            t = mm(PSUM[:, 4, o + 64 * q:o + 64 * q + 64], LA[R, slot(h), :], VT[R, 64 * h:64 * h + 64], False, q == 1, inc=True)
                    u_ok = act(US[R, :], PSUM[R, 4, :], ACT.Copy, [t, seq_ok])
                    free(u_ok, 4)
                    yield
                    for h in range(8):
                        t = mm(PSUM[:, 5, h * 64:h * 64 + 64], XT_[R, slot(h), :], US[R, 64 * h:64 * h + 64], w=[u_ok, bank_free[5]], inc=True)
                    sa_ok = act(SS[R, :], PSUM[R, 5, :], ACT.Copy, [t])
                    free(sa_ok, 5)
                    yield
                    for j in range(4):
                        js = slice(128 * j, 128 * j + 128)
                        mm(PSUM[:, 7, js], BT[R, js], SS[R, js], True, False, [sa_ok, bank_free[7]])
                        mm(PSUM[:, 7, js], KT[R, js], VT[R, js], False, True, inc=True)
                    for j in range(4):
                        o = j * 128
                        mm(PSUM[:, 6, o:o + 128], RT[:, j, tsl], S[:, j, :], True, False, [bank_free[6]])
                        for q in range(2):
                            h = 2 * j + q
                            hc = slice(64 * h, 64 * h + 64)
                            mm(PSUM[:, 6, o + 64 * q:o + 64 * q + 64], MB[R, slot(h), :], SS[R, hc], False, False)
                            t = mm(PSUM[:, 6, o + 64 * q:o + 64 * q + 64], MK[R, slot(h), :], VT[R, hc], False, q == 1, inc=True)
                    sp = PSUM[:, 7, :].rearrange("p (j n) -> p j n", n=P)
                    for q in range(2):
                        p = slice(64 * q, 64 * q + 64)
                        tt(V, S[p, :, p], S[p, :, p], sp[p, :, p], ADD, [t])
                        v = tt(V, S[p, :, p], S[p, :, p], bc(PCE[p, :, 2 * tq + cl], 2, [64, 4, 64]), MUL)
                    s_ok = [v]
                    free(v, 7)
                    y_ok = act(US[R, :], PSUM[R, 6, :], ACT.Copy, [t])
                    free(y_ok, 6)
                    yield
                for j in range(4):
                    t = tr(PSUM[:, 4, j * 128:j * 128 + 128], US[:, 128 * j:128 * j + 128], ident, [y_ok, bank_free[4]], inc=True)
                a = act(LD[:, :, tsl], PSUM[:, 4, :].rearrange("p (j n) -> p j n", n=P), ACT.Copy, [t])
                free(a, 4)
                seq_ok = t
            G2 = C[:, :, :].rearrange("p a t -> p (a t)").rearrange("p (k n) -> p k n", k=2)
            tk_g2 = dma_g("d_rg2", G2, A_["rg2"].rearrange("(k p) n -> p k n", p=P)[:, :, c0:c0 + 512], [seq_ok])
            w2_ok = load_w2(1, [seq_ok]) if hf == 0 else None
            yield
            for j in range(4):
                t = mm(two(4)[:, j, :], bones, LD[:, j, :], w=[a, bank_free[4 + j // 2]], inc=True)
            v = stt(LD[:, :, :], two(4), -1.0 / 64, LD[:, :, :], MUL, ADD, [t])
            free(v, 4, 5)
            a = act(KK[:, :, :], LD[:, :, :], ACT.Square, [v])
            yield
            for j in range(4):
                t = mm(two(6)[:, j, :], bones, KK[:, j, :], w=[a, bank_free[6 + j // 2]], inc=True)
            a = act(IC[:, :, :], two(6), ACT.Sqrt, [t], bias=col("eps64"), scale=1.0 / 64)
            free(a, 6, 7)
            recip(IC[:, :, :], IC[:, :, :], [a])
            v = tt(V, LD[:, :, :], LD[:, :, :], IC[:, :, :], MUL)
            for j in range(4):
                a = act(LD[:, j, :], LD[:, j, :], ACT.Identity, [v], scale=col("ln_w", p0 + j), bias=col("ln_b", p0 + j))
            yield
            for j in range(4):
                for k in range(2):
                    t = mm(two(4)[:, j, :], G2[:, k, 128 * j:128 * j + 128], U(26 + k), k == 0, k == 1,
                           w=[tk_g2, bank_free[4 + j // 2]], inc=True)
            tt(V, rr, rr, LD[:, :, :], ADD, [a])
            v = tt(V, rr, rr, two(4), MUL, [t])
            free(v, 4, 5)
            yr_ok.append(v)
            yield
            return w2_ok

        yr_ok, stg = [], {}

        def ev_kx(t, r_, ps, tok):
            s = STG[:, t % 2, 0:T]
            a = act(s, ps, ACT.Copy, [tok, stg.get(t % 2)])
            stg[t % 2] = dma(A, f"d_stg{t % 2}", KXD[:, t, :], s, [a])
            return a

        def ev_vx(bi, r_, ps, tok):
            s = STG[:, r_, :]
            a = act(s, ps, ACT.Copy, [tok, stg.get(r_)])
            stg[r_] = dma(A, f"d_stg{r_}", VXD[:, r_, 512 * bi:512 * bi + 512], s, [a])
            return a

        side.append(rwkv())
        gemm(PL["xk"], [(HH, HL)], ev_kx, m_ok, every=1.25)
        gemm_tok(PL["xv"], [(HH, HL, slice(0, 128)), (HH, HL, slice(128, 256))], ev_vx, m_ok, every=1.25)
        m_done = TE.now()
        mix_ok = {"g": [None] * 4}

        def mix(g):
            src = YS[:, 4 * g:4 * g + 4, :] if g < 2 else UU(4 * g - 8, 4 * g - 4)
            h = act(HH[:, 4 * g:4 * g + 4, :], src, ACT.Copy, [m_done, yr_ok])
            mix_ok["g"][g] = [h, tt(V, HL[:, 4 * g:4 * g + 4, :], src, HH[:, 4 * g:4 * g + 4, :].bitcast(F32), SUB, [h])]

        while not yr_ok:
            step()
        for g in range(3):
            mix(g)
        ada("ada2", NA1, 1.5)
        drain()
        mix(3)
        for q in (V, A, G):
            q.held += [stg[0], stg[1]]
        s2.close()
        sm.close()
        rk.close()
        sets[0] = whole
        XT = Scope("right")("xt", [P, 16, T])
        r0 = Scope("right")
        GH = r0("ghi", [P, 16, T], F32R)
        GL = r0("glo", [P, 16, T], F32R)
        tk_x = dma_g("d_x1", XT[:, :, :], A_["x"])

        s4 = Scope()
        TM = s4("tm4", [P, 8, T])
        ACC = s4("acc4", [P, T])
        AC2 = s4("acc4b", [P, T])
        SQ2 = s4("sq4", [P, 2, T])
        RS = s4("rs4", [P, 2, T])
        SM = s4("sm4", [P, 8, 4])
        s5 = Scope()
        KX = s5("kx", [P, 16, T])
        VX = s5("vx", [P, 2, 2048])
        QT = s5("qt", [P, 16, T])
        kx_ok = dma_g("d_kx", KX[:, :, :], KXD, [stg[0], stg[1]])
        vx_ok = dma_g("d_vx", VX[:, :, :], VXD)

        def factor(last):
            def go():
                rs_ok[0] = rstd_of([ACC[:, :]], 2048, "eps6", RS[:, 0, :], [last["done"]])
            rs_ok[0] = None
            tails.append((None, 0, go))

        rs_ok = [None]
        h_ok = {}
        ev, last = residual(XT, [(ACC[:, :], None)], SQ2, nxt=(lambda t: col("norm_x_g", t), GH, GL, h_ok, None), here=tk_x)
        gemm(PL["out"], [(HH, HL)], ev, mix_ok)
        out_done = TE.now()
        factor(last)

        def ev_copy(dst):
            return lambda t, r_, ps, tok: act(dst(t, r_), ps, ACT.Copy, [tok])

        q_tok = {}
        o_ok = {"g": [None] * 4}
        XSC = 512.0 ** -0.5
        PT = TM[:, 4:8, :].rearrange("p (a m) t -> p a m t", a=2)

        pt_free = {}

        def xattn():
            for hd in range(4):
                while 4 * hd + 3 not in q_tok:
                    yield
                yield from xhead(hd)

        def xhead(hd):
            for st in range(2):
                u = 2 * hd + st
                b = spare()
                for k in range(4):
                    t = mm(PSUM[:, b, 0:T], QT[:, 4 * hd + k, 128 * st:128 * st + 128], KX[:, 4 * hd + k, :], k == 0, k == 3,
                           [q_tok[4 * hd + 3], kx_ok, bank_free[b]], inc=k == 3)
                ps = PSUM[:, b, 0:T]
                s = SM[:, u % 8, :]
                V.add(lambda e, s=s, ps=ps: e.reduce_max(s[:, 0:1], ps, AX_X), [t])
                v = ts(V, s[:, 1:2], s[:, 0:1], -XSC, None, MUL)
                p = TM[:, u % 4, :]
                a = act(p, ps, ACT.Exp, [v, pt_free.get(("p", u % 4))], bias=s[:, 1:2], scale=XSC, acc=s[:, 2:3])
                bank_free[b] = [a]
                recip(s[:, 3:4], s[:, 2:3], [a])
                v = ts(V, p, p, s[:, 3:4], None, MUL)
                yield
                b = spare(1)
                for m in range(2):
                    t = tr(PSUM[:, b, 128 * m:128 * m + 128], p[:, 128 * m:128 * m + 128], ident, [v, bank_free[b]], inc=m == 1)
                pt_free[("p", u % 4)] = t
                a = act(PT[:, hd % 2, :, 128 * st:128 * st + 128], PSUM[:, b, 0:256].rearrange("p (m s) -> p m s", m=2),
                        ACT.Copy, [t, pt_free.get(hd % 2)])
                bank_free[b] = [a]
                yield
            for d in range(4):
                b = spare(2 + d % 2)
                dt = 4 * hd + d
                for m in range(2):
                    t = mm(PSUM[:, b, 0:T], VX[:, m, 128 * dt:128 * dt + 128], PT[:, hd % 2, m, :], m == 0, m == 1,
                           [a, vx_ok, bank_free[b]], inc=m == 1)
                pt_free[hd % 2] = t
                h = act(HH[:, dt, :], PSUM[:, b, 0:T], ACT.Copy, [t, out_done])
                v = tt(V, HL[:, dt, :], PSUM[:, b, 0:T], HH[:, dt, :].bitcast(F32), SUB, [h])
                bank_free[b] = [v]
                if d == 3:
                    o_ok["g"][hd] = [h, v]
                yield

        def ev_q(t, r_, ps, tok):
            assert rs_ok[0]
            q_tok[t] = tt(V, QT[:, t, :], ps, RS[:, 0, :], MUL, [tok, rs_ok[0]])
            return q_tok[t]

        side.append(xattn())
        gemm(PL["xq"], [(GH, GL)], ev_q, h_ok, every=1.4)
        q_done = TE.now()
        h_ok = {}
        ev, last = residual(XT, [(ACC[:, :], None)], SQ2, nxt=(lambda t: col("norm_ffn_g", t), GH, GL, h_ok, q_done))
        gemm(PL["xo"], [(HH, HL)], ev, o_ok)
        drain()
        xo_done = TE.now()
        factor(last)
        s5.close()

        r1 = Scope("right")
        CH = r1("chi", [P, 16, T], F32R)
        CL = r1("clo", [P, 16, T], F32R)
        s5 = Scope()
        CX = s5("cx", [P, 16, T])
        RB = s5("rb", [P, 4, T])
        TM5 = TM
        tk_cx = dma_g("d_cx", CX[:, :, :], A_["ctx"])
        hid = {}

        def mod_gain(i, g, m, c):
            return stt(GS[:, i, :], MOD[:, m:m + 16, c], 1.0, PK[:, off[g]:off[g] + 16], ADD, MUL)

        def ctx_norm():
            yield from pause(6)
            sq = yield from mean_square(CX, TM5, [tk_cx])
            mod_gain(0, "norm1_g", 16, 1)
            mod_gain(1, "norm1_g", 16, 0)
            v = tt(V, GS[:, 1, :], GS[:, 1, :], PK[:, off["final_g"]:off["final_g"] + 16], MUL)
            yield
            r = rstd_of([TM5[:, i, :] for i in range(4)], 2048, "eps6", RS[:, 1, :], [sq])
            yield
            yield from normed(CX, RS[:, 1, :], lambda j: GS[:, 0, j:j + 1], lambda j: MOD[:, j, 1:2], TM5, CH, CL,
                              [r, v], c_ok)

        c_ok = {}
        side.append(ctx_norm())
        dn_done = xo_done
        ada_open(s5, 1, RB[0:4, :, :].rearrange("p (a b) t -> p a (b t)", a=2))
        for i in range(4):
            f_ok = {"g": [[], [], [], []]}

            def ev_up(t, r_, ps, tok):
                if t % 4 == 0:
                    flush()
                assert rs_ok[0]
                q = RB[:, t % 4, :]
                v = stt(q, ps, 0.0, RS[:, 0, :], MAX, MUL, [tok, rs_ok[0], hid.get(t % 4)])

                def rest():
                    a = act(q, q, ACT.Square, [v])
                    h = act(HH[:, t, :], q, ACT.Copy, [a, dn_done])
                    hid[t % 4] = tt(V, HL[:, t, :], q, HH[:, t, :].bitcast(F32), SUB, [h])
                    f_ok["g"][t // 4] += [h, hid[t % 4]]
                tails.append((f_ok, t // 4, rest))
                return v

            gemm(PL[f"up{i}"], [(GH, GL)], ev_up, h_ok)
            acc = [(ACC[:, :], None), (AC2[:, :], lambda t: col("final_g", t))] if i == 3 else []
            ev, last = residual(XT, acc, SQ2, sq2=TM)
            gemm(PL[f"dn{i}"], [(HH, HL)], ev, f_ok)
            dn_done = TE.now()
        drain()
        flush()
        up_done = TE.now()
        def first_norm2():
            rx, xa, xb = RS[:, 0, :], SQ2[:, 0, :], SQ2[:, 1, :]
            r = rstd_of([ACC[:, :]], 2048, "eps6", rx, [last["done"]], b=2)
            t = mm(PSUM[:, 6, 0:T], ones, AC2[:, :], w=[bank_free[6]], inc=True)
            yield
            tt(V, xa, rx, rx, MUL, [r])
            v = tt(V, xa, xa, PSUM[:, 6, 0:T], MUL, [t])
            bank_free[6] = [v]
            a = act(xb, xa, ACT.Sqrt, [v], bias=col("eps6"), scale=1.0 / 2048)
            recip(xb, xb, [a])
            r = tt(V, RS[:, 1, :], xb, rx, MUL)
            yield
            yield from normed(XT, RS[:, 1, :], lambda j: GS[:, 1, j:j + 1], lambda j: MOD[:, j, 0:1], TM5, GH, GL,
                              [r, up_done], h_ok)
            for j in range(16):
                stt(XT[:, j, :], XT[:, j, :], col("final_g", j), rx, MUL, MUL)
                if j % 4 == 3:
                    yield

        h_ok = {}
        side.append(first_norm2())
        ada("ada3", NA2)
        drain()
        s5.close()
        s4.close()
        s1.close()


        s6 = Scope()
        Y2 = s6("y2", [P, 16, T])
        SM = s6("sm6", [P, 8, 4])
        FT = s6("ft", [P, 4, T])
        HY = s6("hy", [P, 12, T + 2])
        s6c = Scope()
        K2 = s6c("k2", [P, 8, 512])
        V2 = s6c("v2", [P, 4, 1024])
        hpad = fill(G, HY[:, :, 0:1], 0.0)
        hpad = fill(G, HY[:, :, T + 1:T + 2], 0.0)
        gemm(PL["k2"], [(GH, GL), (CH, CL)], ev_copy(lambda t, r_: K2[:, t, T * r_:T * r_ + T]), [h_ok, c_ok])
        k2_ok = A.now()
        gemm_tok(PL["v2"], [(GH, GL, slice(0, 128)), (GH, GL, slice(128, 256)), (CH, CL, slice(0, 128)), (CH, CL, slice(128, 256))],
                 ev_copy(lambda b, r_: V2[:, r_, 512 * b:512 * b + 512]), [h_ok, c_ok])
        v2_ok = A.now()
        r1.close()
        s7 = Scope()
        QT2 = s7("q2", [P, 8, T])
        BI = s7("bi", [P, 2, 2, T])
        MS = s7("ms", [P, 2, T])
        PP = s7("pp", [P, 2, 512])
        PT2 = s7("pt2", [P, 2, 4, T])
        tk_ms = dma_g("d_ms", MS[:, :, :].rearrange("p a t -> p (a t)"), A_["namask"])
        NSC = 128.0 ** -0.5
        q2_tok, bi_free, pp_free, pt2_free, a_tok = {}, {}, {}, {}, {}

        def na(h):
            tk = dma_g(f"d_bi{h % 2}", BI[:, h % 2, :, :], A_["bias"][h].rearrange("(a p) t -> p a t", p=P), [bi_free.get(h % 2)])
            bi = tt(G, BI[:, h % 2, :, :], BI[:, h % 2, :, :], MS[:, :, :], ADD, [tk, tk_ms])
            yield
            for qt in range(2):
                u = 2 * h + qt
                b = spare()
                t = mm(PSUM[:, b, :], QT2[:, h, 128 * qt:128 * qt + 128], K2[:, h, :], w=[q2_tok[h], k2_ok, bank_free[b]], inc=True)
                p = PP[:, u % 2, :]
                ts(V, p[:, T:512], PSUM[:, b, T:512], NSC, None, MUL, w=[t, pp_free.get(u % 2)])
                v = stt(p[:, 0:T], PSUM[:, b, 0:T], NSC, BI[:, h % 2, qt, :], MUL, ADD, [bi])
                bank_free[b] = [v]
                bi_free[h % 2] = v
                s = SM[:, u % 8, :]
                V.add(lambda e, s=s, p=p: e.reduce_max(s[:, 0:1], p, AX_X))
                v = ts(V, s[:, 1:2], s[:, 0:1], -1.0, None, MUL)
                a = act(p, p, ACT.Exp, [v], bias=s[:, 1:2], acc=s[:, 2:3])
                yield
                recip(s[:, 3:4], s[:, 2:3], [a])
                v = ts(V, p, p, s[:, 3:4], None, MUL)
                yield
                b = spare(1)
                for k in range(4):
                    t = tr(PSUM[:, b, 128 * k:128 * k + 128], p[:, 128 * k:128 * k + 128], ident, [v, bank_free[b]], inc=k == 3)
                pp_free[u % 2] = t
                a = act(PT2[:, h % 2, :, 128 * qt:128 * qt + 128], PSUM[:, b, :].rearrange("p (k s) -> p k s", k=4),
                        ACT.Copy, [t, pt2_free.get(h % 2)])
                bank_free[b] = [a]
                yield
            b = spare(2)
            for k in range(4):
                t = mm(PSUM[:, b, 0:T], V2[:, k, 128 * h:128 * h + 128], PT2[:, h % 2, k, :], k == 0, k == 3,
                       [a, v2_ok, bank_free[b]], inc=k == 3)
            pt2_free[h % 2] = t
            a_tok[h] = act(Y2[:, h, :], PSUM[:, b, 0:T], ACT.Copy, [t])
            bank_free[b] = [a_tok[h]]
            yield

        def ev_q2(t, r_, ps, tok):
            q2_tok[t] = act(QT2[:, t, :], ps, ACT.Copy, [tok])
            if t % 4 == 3:
                side.extend(na(h) for h in range(t - 3, t + 1))
            return q2_tok[t]

        gemm(PL["q2"], [(GH, GL)], ev_q2, h_ok, every=1.7)

        def ev_fh(t, r_, ps, tok):
            return act(FT[:, t, :] if t < 4 else HY[:, t - 4, 1:T + 1], ps, ACT.Copy, [tok, hpad])

        gemm(PL["fh"], [(GH, GL)], ev_fh, h_ok, every=1.7)
        fh_ok = A.now()
        fh_done = TE.now()
        drain()
        s7.close()
        s6c.close()

        s8 = Scope()
        ada_open(s8, 2)
        SPEC = s8("spec2", [P, 2, 2, 512])
        DF = s8("dft", [P, 4, 2, T])
        FC = s8("fft", [P, 1280])
        CA = s8("ca", [P, 2, T])
        RG = s8("rg2", [P, T])
        TMX = s8("tmx", [P, 4, T])
        tk_df = dma_g("d_df", DF[:, :, :, :].rearrange("p a b t -> p (a b t)"), A_["dft"])
        tk_fc = dma_g("d_fc", FC[:, :], A_["fft"])

        def load_spec(o, w):
            sp_ok[0] = dma_g("d_sp", SPEC[:, :, :, :].rearrange("p b c n -> p (b c n)"), SPD[:, 2048 * o:2048 * o + 2048], w)

        sp_ok = [None]
        load_spec(0, [spec_tok])
        s9 = Scope()
        ZK = s9("zk", [P, 2, 512])
        YF = s9("yf", [P, 2, 2, 512])
        Q1 = s9("q1", [P, 2, 512])
        Q3 = s9("q3", [P, 2, 512])
        AB = s9("ab", [P, 2, 4, T])

        def fourier():
            for g in range(4):
                b = g % 2
                for tq in range(2):
                    t = mm(PSUM[:, b, T * tq:T * tq + T], FT[:, g, 128 * tq:128 * tq + 128], FC[:, 1024:1280],
                           w=[tk_fc, fh_ok, bank_free[b]], inc=tq == 1)
                a = act(AB[:, :, g, :], PSUM[:, b, :].rearrange("p (q t) -> p q t", q=2), ACT.Copy, [t])
                bank_free[b] = [a]
                yield
            for g in range(4):
                b = g % 2
                for n in range(4):
                    k, cs = n // 2, n % 2
                    t = mm(PSUM[:, b, 0:T], AB[:, k, g, 128 * cs:128 * cs + 128], FC[:, 512 * cs + T * k:512 * cs + T * k + T],
                           n == 0, n == 3, [a, bank_free[b]], inc=n == 3)
                a2 = act(Y2[:, 8 + g, :], PSUM[:, b, 0:T], ACT.Copy, [t])
                bank_free[b] = [a2]
                yield

        hy_done = []

        def hyena():
            conv = {}
            for j in range(12):
                b = CA[:, j % 2, :]
                ts(V, b, HY[:, j, 2:T + 2], col("hy_cw", 24 + j), None, MUL, w=[fh_ok, conv.get(j % 2)])
                for i in (1, 0):
                    v = stt(b, HY[:, j, i:i + T], col("hy_cw", 12 * i + j), b, MUL, ADD)
                conv[j % 2] = src_ok = act(HY[:, j, 1:T + 1], b, ACT.Identity, [v], bias=col("hy_cb", j))
                yield
            for o in range(2):
                for tq in range(2):
                    for j in range(4):
                        t = tr(PSUM[:, 2 + tq, 128 * j:128 * j + 128], HY[:, j, 1 + 128 * tq:129 + 128 * tq], ident,
                               [src_ok, bank_free[2 + tq]], inc=j == 3)
                    a = act(ZK[:, tq, :], PSUM[:, 2 + tq, :], ACT.Copy, [t])
                    bank_free[2 + tq] = [a]
                    yield
                kr, ki = SPEC[:, 0, :, :], SPEC[:, 1, :, :]
                for ri in range(2):
                    zb = (2, 3) if ri == 0 else (5, 6)
                    for f in range(2):
                        b = zb[f]
                        for k in range(2):
                            t = mm(PSUM[:, b, :], DF[:, ri, k, 128 * f:128 * f + 128], ZK[:, k, :], k == 0, k == 1,
                                   [a, tk_df, bank_free[b]], inc=k == 1)
                    z = PSUM[:, zb[0]:zb[0] + 2, :]
                    if ri == 0:
                        tt(V, YF[:, 0, :, :], z, kr, MUL, [t, sp_ok[0]])
                        v = tt(V, YF[:, 1, :, :], z, ki, MUL)
                    else:
                        v1 = tt(V, Q1[:, :, :], z, ki, MUL, [t])
                        v = tt(V, Q3[:, :, :], z, kr, MUL)
                        g = tt(G, YF[:, 0, :, :], YF[:, 0, :, :], Q1[:, :, :], SUB, [v1])
                    bank_free[zb[0]] = bank_free[zb[1]] = [v]
                    yield
                if o == 0:
                    load_spec(1, [v])
                v = tt(V, YF[:, 1, :, :], YF[:, 1, :, :], Q3[:, :, :], ADD)
                yield
                for j in range(4):
                    b = (2, 3, 5, 6)[j]
                    for n in range(4):
                        ri, f = n // 2, n % 2
                        t = mm(PSUM[:, b, 0:T], YF[:, ri, f, 128 * j:128 * j + 128], DF[:, 2 + ri, f, :], n == 0, n == 3,
                               [g, v, bank_free[b]], inc=n == 3)
                    u_ = HY[:, j, 1:T + 1]
                    w_ = stt(u_, u_, col("hy_bias", 4 * o + j), PSUM[:, b, 0:T], MUL, ADD, [t])
                    bank_free[b] = [w_]
                    src_ok = tt(V, u_ if o == 0 else Y2[:, 12 + j, :], u_, HY[:, 4 + 4 * o + j, 1:T + 1], MUL)
                    hy_done[:] = [src_ok]
                    yield

        y_ok = {"g": [None] * 4}

        def mixed(a_, b_, n, w=()):
            for k in range(a_, b_, 4):
                a = act(TMX[:, :, :], Y2[:, k:k + 4, :], ACT.Square, list(w))
                yield
                for j in range(4):
                    t = mm(PSUM[:, 0, 0:T], ones, TMX[:, j, :], k == a_ and j == 0, k + j == b_ - 1, [a, bank_free[0]], inc=j == 3)
                bank_free[0] = []
                A.held.append(t)
            s = act(RG[:, :], PSUM[:, 0, 0:T], ACT.Sqrt, [t], bias=col("eps6"), scale=1.0 / n)
            bank_free[0] = [s]
            recip(RG[:, :], RG[:, :], [s])
            for k in range(a_, b_, 4):
                for j in range(k, k + 4):
                    v = stt(Y2[:, j, :], Y2[:, j, :], col("mix_g", j), RG[:, :], MUL, MUL)
                yield
                h = act(GH[:, k:k + 4, :], Y2[:, k:k + 4, :], ACT.Copy, [v, fh_done])
                yield
                v = tt(V, GL[:, k:k + 4, :], Y2[:, k:k + 4, :], GH[:, k:k + 4, :].bitcast(F32), SUB, [h])
                y_ok["g"][k // 4] = [h, v]
            yield

        def rest():
            yield from mixed(0, 8, 1024)
            yield from fourier()
            yield from mixed(8, 12, 512)

        sets[0] = [[4], [7]]
        turn[0] = 0
        side.append(both(rest(), hyena()))
        side.append(mixed(12, 16, 512, hy_done))
        ada("ada4", NA3)
        drain()
        sets[0] = whole
        mod_gain(2, "norm2_g", 64, 0)
        s9.close()
        s8.close()
        s6.close()

        s4 = Scope()
        TM = s4("tma", [P, 8, T])
        ACC = s4("acca", [P, T])
        SQ2 = s4("sqa", [P, 2, T])
        RS = s4("rsa", [P, 2, T])
        HH = s4("h2hi", [P, 11, T], F32R)
        HL = s4("h2lo", [P, 11, T], F32R)
        GA = s4("ga", [P, 11, T])
        ada_open(s4, 3)
        GP = s4("gp", [P, 4, T + 2])
        CV = s4("cv", [P, 2, T])
        UB = s4("ub", [P, 4, T])
        gp0 = fill(G, GP[:, :, 0:1], 0.0)
        gp0 = fill(G, GP[:, :, T + 1:T + 2], 0.0)
        ev, last = residual(XT, [(ACC[:, :], None)], SQ2, lambda t: MOD[:, 32 + t, 0:1])
        gemm(PL["out2"], [(GH, GL)], ev, y_ok)
        out_done = TE.now()
        h_ok = {}

        def second_norm():
            r = rstd_of([ACC[:, :]], 2048, "eps6", RS[:, 0, :], [last["done"]], b=2)
            yield
            yield from normed(XT, RS[:, 0, :], lambda j: GS[:, 2, j:j + 1], lambda j: MOD[:, 48 + j, 0:1], TM, GH, GL,
                              [r, out_done], h_ok)

        flush()
        side.append(second_norm())
        ada("ada5", NA4)
        drain()
        dn_done = out_done
        hid = {}
        for i in range(4):
            f_ok = {"g": [[], [], []]}

            def ev_gate(t, r_, ps, tok):
                if t % 4 == 0:
                    flush()
                gt = 11 * i + t
                src = GP[:, t % 4, :]
                e_ = act(src[:, 1:T + 1], ps, ACT.Copy, [tok, gp0, hid.get(("c", t % 4))])

                def rest():
                    b = CV[:, t % 2, :]
                    ts(V, b, src[:, 2:T + 2], col("ff_cw", 88 + gt), None, MUL, w=[e_, hid.get(("a", t % 2))])
                    stt(b, src[:, 1:T + 1], col("ff_cw", 44 + gt), b, MUL, ADD)
                    hid[("c", t % 4)] = v = stt(b, src[:, 0:T], col("ff_cw", gt), b, MUL, ADD)
                    hid[("a", t % 2)] = hid[("g", gt)] = act(GA[:, t, :], b, ACT.Gelu_apprx_tanh, [v, hid.get(("u", t))],
                                                             bias=col("ff_cb", gt))
                tails.append((None, 0, rest))
                return e_

            def ev_uu(t, r_, ps, tok):
                if t % 4 == 0:
                    flush()
                q = UB[:, t % 4, :]
                hid[("u", t)] = v = tt(V, q, ps, GA[:, t, :], MUL, [tok, hid[("g", 11 * i + t)], hid.get(("q", t % 4))])

                def rest():
                    h = act(HH[:, t, :], q, ACT.Copy, [v, dn_done])
                    hid[("q", t % 4)] = tt(V, HL[:, t, :], q, HH[:, t, :].bitcast(F32), SUB, [h])
                    f_ok["g"][t // 4] += [h, hid[("q", t % 4)]]
                tails.append((f_ok, t // 4, rest))
                return v

            gemm(PL[f"ga{i}"], [(GH, GL)], ev_gate, h_ok)
            gemm(PL[f"uu{i}"], [(GH, GL)], ev_uu, h_ok)
            ev, last = residual(XT, [(ACC[:, :], None)] if i == 3 else [], SQ2, lambda t: MOD[:, 80 + t, 0:1])
            gemm(PL[f"dd{i}"], [(HH, HL)], ev, f_ok)
            dn_done = TE.now()
        flush()
        r = rstd_of([ACC[:, :]], 2048, "eps6", RS[:, 0, :], [last["done"]])
        for j in range(16):
            v = stt(XT[:, j, :], XT[:, j, :], col("final_g2", j), RS[:, 0, :], MUL, MUL)
            if j % 4 == 3:
                dma(SP, "d_out", out[:, j - 3:j + 1, :], XT[:, j - 3:j + 1, :], [v])
        end()


def _layout(inp):
    import numpy as np
    f = np.float32
    a = {k: np.asarray(v) for k, v in inp.items()}

    def cols(v, n=None):
        v = np.asarray(v).reshape(-1)
        return np.ascontiguousarray(v.reshape(-1, 128).T)

    def padded(v):
        o = np.zeros((128, 1), f)
        v = np.asarray(v).reshape(-1)
        o[:v.size, 0] = v
        return o

    def tiles(v):
        return np.concatenate([cols(r) for r in v], axis=1)

    mu = a["rwkv_mu"][0]
    mu = np.concatenate([cols(mu[:3072]), padded(mu[3072:3168]), padded(mu[3168:3264]), cols(mu[3264:])], axis=1)
    one = np.ones((128, 1), f)
    parts = {
        "norm_mix_g": cols(a["norm_mix_g"]), "conv_w": tiles(a["ssd_conv_w"][0, :, 0]), "conv_b": cols(a["ssd_conv_b"]),
        "ssd_g": cols(a["ssd_norm_g"]), "ssd_d": cols(np.repeat(a["ssd_d"][0], 64)), "dt_bias": padded(a["ssd_dt_bias"]),
        "a_log": padded(a["ssd_a_log"]), "mu": mu, "w0": cols(a["rwkv_w0"]), "a0": cols(a["rwkv_a0"]),
        "k_k": cols(a["rwkv_k_k"]), "k_a": cols(a["rwkv_k_a"]), "r_k": cols(a["rwkv_r_k"]), "ln_w": cols(a["rwkv_ln_w"]),
        "ln_b": cols(a["rwkv_ln_b"]), "norm_x_g": cols(a["norm_x_g"]), "norm_mem_g": cols(a["norm_mem_g"]),
        "norm_ffn_g": cols(a["norm_ffn_g"]), "final_g": cols(a["final_norm_g"]), "c": cols(a["c_2"]),
        "c_ctx": cols(a["c_ctx_2"]), "ada_b": cols(a["ada_b_2"]), "norm1_g": cols(a["norm1_g_2"]),
        "norm2_g": cols(a["norm2_g_2"]), "hy_cw": tiles(a["hy_conv_w_2"][0]), "hy_cb": cols(a["hy_conv_b_2"]),
        "mix_g": cols(a["mix_norm_g_2"]), "ff_cw": tiles(a["ffn_conv_w_2"][0]), "ff_cb": cols(a["ffn_conv_b_2"]),
        "hy_bias": tiles(a["hy_bias_2"][0]), "final_g2": cols(a["final_norm_g_2"]), "hy_b1": padded(a["hy_b1_2"]),
        "hy_b2": padded(a["hy_b2_2"]), "hy_freq": padded(a["hy_freq_2"]), "one": one, "eps6": one * f(1e-6),
        "eps64": one * f(64e-5), "zero": np.zeros((128, 1), f),
    }
    d = {"pack": np.concatenate([parts[n] for n, _ in COLS], axis=1)}

    i = np.arange(128)
    r, c = i[:, None], i[None, :]
    d["mats"] = np.concatenate([np.eye(128), np.ones((128, 128)), (r // 64 == c // 64)], axis=1).astype(f)

    def level(t, u, s):
        return (t // (2 * s) == u // (2 * s)) & (t // s % 2 == 1) & (u // s % 2 == 0)

    same = r // 64 == c // 64
    m1 = [c >= r, level(r, c, 1)] + [level(c, r, s) for s in (1, 2, 4, 8, 16, 32)] + [same & (r < c), same & (r <= c)]
    t = np.arange(256)
    m1 += [np.broadcast_to(t % 128 != 0, (128, 256)), np.broadcast_to(t % 64 != 0, (128, 256))]
    d["mats1"] = np.concatenate(m1, axis=1).astype(f)
    d["comb"] = np.array([[1, 0], [0, 1], [1, 0], [0, 1]], f)
    d["sel"] = np.repeat(np.eye(16), 128, axis=1).astype(f)

    def fm(v):
        return np.ascontiguousarray(v.T.reshape(-1, 128, v.shape[0]).transpose(1, 0, 2))

    d["x"], d["mem"], d["ctx"] = fm(a["x"][0]), fm(a["mem"][0]), fm(a["ctx_2"][0])
    for n in WEIGHTS:
        d[n] = a[n][0]
    k = np.arange(256)
    th = np.pi * np.outer(t, 2 * k + 1) / 512.0

    def km(m):
        return m.reshape(2, 128, -1).transpose(1, 0, 2).reshape(128, -1)

    d["dft"] = np.ascontiguousarray(np.concatenate([km(np.cos(th)), km(-np.sin(th)), km(np.cos(th).T / 256),
                                                    km(-np.sin(th).T / 256)], axis=1).astype(f))
    w = 2 * np.pi / 256
    cl, sl = np.cos(w * (np.outer(t, t) % 256)), np.sin(w * (np.outer(t, t) % 256))
    q = np.arange(128)
    cd, sd = (fn(2 * np.pi / 128 * (np.outer(q, q) % 128)) for fn in (np.cos, np.sin))
    n = 1 / np.sqrt(256.0 * 128.0)
    d["fft"] = np.ascontiguousarray(np.concatenate([km(cl * n), km(-sl * n), cd, sd], axis=1).astype(f))
    pos = np.arange(256, dtype=f)
    tl = pos / f(255)
    bands = np.linspace(1e-4, 15, 16).astype(f)
    ang = bands[None, :] * f(2.0 * np.pi / 256) * pos[:, None]
    d["zt"] = np.ascontiguousarray(np.concatenate([tl[:, None], np.cos(ang), -np.sin(ang)], axis=1).astype(f).T)
    lo, hi = np.log(1e-2) / 1.5, np.log(1e-2) / 0.3
    deltas = np.linspace(lo, hi, 512).astype(f)
    win = np.exp(-tl[:, None] * np.abs(deltas)[None, :]).astype(f)
    winb = win.copy()
    winb[0] = 0
    d["win"] = np.ascontiguousarray(np.concatenate([km(win), km(winb)], axis=1).astype(f))
    d["hy_w1"], d["hy_w2"], d["hy_w3"] = a["hy_w1_2"][0], a["hy_w2_2"][0], a["hy_w3_2"][0]
    d["rw2"], d["ra2"], d["rg2"] = a["rwkv_w2"][0], a["rwkv_a2"][0], a["rwkv_g2"][0]
    row, cc = t // 64, t % 64
    st = np.clip(cc - 8, 0, 48)
    inside = (cc[None, :] >= st[:, None]) & (cc[None, :] < st[:, None] + 16)
    dr = row[None, :] - row[:, None] + 7
    dc = np.clip(cc[None, :] - cc[:, None] + 15, 0, 30)
    d["bias"] = np.ascontiguousarray(a["na_rpb_2"][0][:, dr, dc])
    d["namask"] = np.ascontiguousarray(km(np.where(inside, 0.0, -1e30)).astype(f))
    return {k: np.ascontiguousarray(v) for k, v in d.items()}


WEIGHTS = ["w_in", "w_out", "xattn_wq", "xattn_wk", "xattn_wv", "xattn_wo", "ffn_w1", "ffn_w2", "ada_w_2", "w_in_2",
           "w_out_2", "ffn_w_up_2", "ffn_w_down_2"]


def kernel(**inputs):
    import numpy as _np
    import concourse.bacc as _bacc
    from concourse import mybir as _mybir
    from concourse.bass_utils import run_bass_kernel_spmd as _run

    nc = _bacc.Bacc("TRN2", target_bir_lowering=False, num_devices=1)
    arrays, args = {}, {}
    for name, v in _layout(inputs).items():
        arrays["in_" + name] = v
        args[name] = nc.dram_tensor("in_" + name, v.shape, _mybir.dt.from_np(v.dtype), kind="ExternalInput").ap()
    out = nc.dram_tensor("out_0", (128, 16, 256), _mybir.dt.float32, kind="ExternalOutput").ap()
    build(nc, args, out)
    r = _run(nc, [arrays], core_ids=[0])
    y = r.results[0]["out_0"]
    return _np.ascontiguousarray(y.transpose(2, 1, 0).reshape(1, 256, 2048))
```
